# Optimizing a Trainium2 kernel written in Bass

```python
import math
import jax, jax.numpy as jnp
from jax import lax
import numpy as np

D_MODEL = 1024
BATCH = 1
SEQ = 512
DEPTH = 2

MEM_LEN = 256
HEAD_DIM = 64
DA_HEADS = 4
DA_V_DIM = 2 * HEAD_DIM
GQ_HEADS = 8
GQ_KV_HEADS = 2
GQ_REP = GQ_HEADS // GQ_KV_HEADS
MX_HEADS = 4
MX_HEAD_DIM = 128
BRANCH_W = 512
N_BRANCHES = 3
GRID_W = 64
ROPE_THETA = 10000.0
Q_BLOCK = 128
NORM_EPS = 1e-6
N_GROUPS = 4
EXPERTS_PER_GROUP = 8
N_EXPERTS = N_GROUPS * EXPERTS_PER_GROUP
TOP_K = 2
D_EXPERT = 512
MOE_BLOCK = 128
IN_WIDTHS = (DA_HEADS * 2 * HEAD_DIM,
             DA_HEADS * 2 * HEAD_DIM,
             DA_HEADS * DA_V_DIM,
             GQ_HEADS * HEAD_DIM,
             GQ_KV_HEADS * HEAD_DIM,
             GQ_KV_HEADS * HEAD_DIM,
             MX_HEADS * MX_HEAD_DIM,
             N_BRANCHES * D_MODEL)
D_IN = sum(IN_WIDTHS)

kernel_name = 'hybrid_diffattn_axialgqa_memxattn_hiermoe'

F32 = jnp.float32

def rms_norm(x, g):
    xf = x.astype(F32)
    y = xf * lax.rsqrt(jnp.mean(xf * xf, axis=-1, keepdims=True) + NORM_EPS)
    return (y * g.astype(F32)).astype(x.dtype)

def rope_angles_1d(S):
    pos = jnp.arange(S, dtype=F32)
    inv = ROPE_THETA ** (-jnp.arange(0, HEAD_DIM, 2, dtype=F32) / HEAD_DIM)
    return pos[:, None] * inv[None, :]

def rope_angles_axial(S):
    rows = S // GRID_W
    row = jnp.broadcast_to(jnp.arange(rows, dtype=F32)[:, None], (rows, GRID_W)).reshape(-1)
    col = jnp.broadcast_to(jnp.arange(GRID_W, dtype=F32)[None, :], (rows, GRID_W)).reshape(-1)
    axis_dim = HEAD_DIM // 2
    inv = ROPE_THETA ** (-jnp.arange(0, axis_dim, 2, dtype=F32) / axis_dim)
    return jnp.concatenate([row[:, None] * inv, col[:, None] * inv], axis=-1)

def apply_rope(x, ang):
    S, half = ang.shape
    shape = (S,) + (1,) * (x.ndim - 3) + (half,)
    c = jnp.cos(ang).reshape(shape)
    s = jnp.sin(ang).reshape(shape)
    xf = x.astype(F32)
    x1, x2 = xf[..., :half], xf[..., half:]
    return jnp.concatenate([x1 * c - x2 * s, x2 * c + x1 * s], axis=-1).astype(x.dtype)

def to_blocks(t):
    B, S = t.shape[:2]
    return t.reshape((B, S // Q_BLOCK, Q_BLOCK) + t.shape[2:]).swapaxes(0, 1)

def from_blocks(t):
    nb, B, qb = t.shape[:3]
    return t.swapaxes(0, 1).reshape((B, nb * qb) + t.shape[3:])

def diff_attention(q, k, v, lam):
    scale = HEAD_DIM ** -0.5

    def one_block(qb):
        s = jnp.einsum('bqhcd,bkhcd->bhcqk', qb, k).astype(F32) * scale
        p = jax.nn.softmax(s, axis=-1)
        a = p[:, :, 0] - lam * p[:, :, 1]
        return jnp.einsum('bhqk,bkhe->bqhe', a.astype(v.dtype), v)

    return from_blocks(lax.map(one_block, to_blocks(q)))

def gqa_attention(q, k, v):
    scale = HEAD_DIM ** -0.5

    def one_block(qb):
        s = jnp.einsum('bqnrd,bsnd->bnrqs', qb, k).astype(F32) * scale
        p = jax.nn.softmax(s, axis=-1)
        return jnp.einsum('bnrqs,bsnd->bqnrd', p.astype(v.dtype), v)

    return from_blocks(lax.map(one_block, to_blocks(q)))

def memory_attention(q, k, v):
    s = jnp.einsum('bqhe,bmhe->bhqm', q, k).astype(F32) * (MX_HEAD_DIM ** -0.5)
    p = jax.nn.softmax(s, axis=-1)
    return jnp.einsum('bhqm,bmhe->bqhe', p.astype(v.dtype), v)

def hier_route(t, w_rg, b_rg, w_re, b_re):
    g_prob = jax.nn.softmax((t @ w_rg + b_rg).astype(F32), axis=-1)
    g_idx = jnp.argmax(g_prob, axis=-1)
    g_p = jnp.max(g_prob, axis=-1)
    e_logits = (t @ w_re + b_re).astype(F32).reshape(-1, N_GROUPS, EXPERTS_PER_GROUP)
    in_group = jnp.take_along_axis(e_logits, g_idx[:, None, None], axis=1)[:, 0]
    e_prob = jax.nn.softmax(in_group, axis=-1)
    top_p, top_i = lax.top_k(e_prob, TOP_K)
    top_p = top_p / jnp.sum(top_p, axis=-1, keepdims=True)
    weights = g_p[:, None] * top_p
    experts = (g_idx[:, None] * EXPERTS_PER_GROUP + top_i).astype(jnp.int32)
    return experts, weights

def moe_forward(t, experts, weights, w_gate, w_up, w_down):
    T, D = t.shape
    A = T * TOP_K
    P = A + N_EXPERTS * MOE_BLOCK
    NB = P // MOE_BLOCK
    flat_e = experts.reshape(-1)
    flat_tok = jnp.arange(A, dtype=jnp.int32) // TOP_K
    flat_w = weights.reshape(-1)
    order = jnp.argsort(flat_e)
    se, stok, sw = flat_e[order], flat_tok[order], flat_w[order]
    counts = jnp.bincount(flat_e, length=N_EXPERTS)
    starts = jnp.cumsum(counts) - counts
    padded = (counts + MOE_BLOCK - 1) // MOE_BLOCK * MOE_BLOCK
    pends = jnp.cumsum(padded)
    pstarts = pends - padded
    dest = pstarts[se] + (jnp.arange(A, dtype=jnp.int32) - starts[se])
    buf = jnp.zeros((P, D), t.dtype).at[dest].set(t[stok])
    block_start = jnp.arange(NB, dtype=jnp.int32) * MOE_BLOCK
    block_e = jnp.minimum(jnp.searchsorted(pends, block_start, side='right'), N_EXPERTS - 1)

    def run(args):
        xb, e = args
        hid = jax.nn.silu(xb @ w_gate[e]) * (xb @ w_up[e])
        return hid @ w_down[e]

    ybuf = lax.map(run, (buf.reshape(NB, MOE_BLOCK, D), block_e)).reshape(P, D)
    y = ybuf[dest] * sw[:, None].astype(t.dtype)
    return jax.ops.segment_sum(y, stok, num_segments=T)

def setup_inputs(seed: int = 0) -> dict:
    key = jax.random.key(seed)
    ks = jax.random.split(key, 32)

    def nrm(k, shape, scale):
        return jax.random.normal(k, shape, F32) * scale

    def gain(k, shape):
        return 1.0 + 0.02 * jax.random.normal(k, shape, F32)

    D = D_MODEL
    return {
        'x': nrm(ks[0], (BATCH, SEQ, D), 1.0),
        'mem': nrm(ks[1], (BATCH, MEM_LEN, D), 1.0),
        'mem_norm_g': gain(ks[2], (D,)),
        'w_mem_kv': nrm(ks[3], (D, 2 * MX_HEADS * MX_HEAD_DIM), D ** -0.5),
        'norm1_g': gain(ks[4], (DEPTH, D)),
        'w_in': nrm(ks[5], (DEPTH, D, D_IN), D ** -0.5),
        'lam_q1': nrm(ks[6], (DEPTH, HEAD_DIM), 0.1),
        'lam_k1': nrm(ks[7], (DEPTH, HEAD_DIM), 0.1),
        'lam_q2': nrm(ks[8], (DEPTH, HEAD_DIM), 0.1),
        'lam_k2': nrm(ks[9], (DEPTH, HEAD_DIM), 0.1),
        'subln_g': gain(ks[10], (DEPTH, DA_V_DIM)),
        'q_norm_g': gain(ks[11], (DEPTH, HEAD_DIM)),
        'k_norm_g': gain(ks[12], (DEPTH, HEAD_DIM)),
        'w_up_a': nrm(ks[13], (DEPTH, BRANCH_W, D), BRANCH_W ** -0.5),
        'w_up_b': nrm(ks[14], (DEPTH, BRANCH_W, D), BRANCH_W ** -0.5),
        'w_up_c': nrm(ks[15], (DEPTH, BRANCH_W, D), BRANCH_W ** -0.5),
        'w_out': nrm(ks[16], (DEPTH, D, D), D ** -0.5),
        'norm2_g': gain(ks[17], (DEPTH, D)),
        'w_router_group': nrm(ks[18], (DEPTH, D, N_GROUPS), D ** -0.5),
        'b_router_group': nrm(ks[19], (DEPTH, N_GROUPS), 0.01),
        'w_router_expert': nrm(ks[20], (DEPTH, D, N_EXPERTS), D ** -0.5),
        'b_router_expert': nrm(ks[21], (DEPTH, N_EXPERTS), 0.01),
        'w_exp_gate': nrm(ks[22], (DEPTH, N_EXPERTS, D, D_EXPERT), D ** -0.5),
        'w_exp_up': nrm(ks[23], (DEPTH, N_EXPERTS, D, D_EXPERT), D ** -0.5),
        'w_exp_down': nrm(ks[24], (DEPTH, N_EXPERTS, D_EXPERT, D), D_EXPERT ** -0.5),
        'final_norm_g': gain(ks[25], (D,)),
    }

def reference(x, mem, mem_norm_g, w_mem_kv, norm1_g, w_in, lam_q1, lam_k1, lam_q2, lam_k2,
              subln_g, q_norm_g, k_norm_g, w_up_a, w_up_b, w_up_c, w_out, norm2_g,
              w_router_group, b_router_group, w_router_expert, b_router_expert,
              w_exp_gate, w_exp_up, w_exp_down, final_norm_g):
    B, S, D = x.shape
    ang_1d = rope_angles_1d(S)
    ang_2d = rope_angles_axial(S)
    split_idx = [int(i) for i in np.cumsum(IN_WIDTHS)[:-1]]

    mem_kv = rms_norm(mem, mem_norm_g) @ w_mem_kv
    mk, mv = jnp.split(mem_kv, 2, axis=-1)
    M = mem.shape[1]
    mk = mk.reshape(B, M, MX_HEADS, MX_HEAD_DIM)
    mv = mv.reshape(B, M, MX_HEADS, MX_HEAD_DIM)

    for l in range(DEPTH):
        h = rms_norm(x, norm1_g[l])
        proj = h @ w_in[l]
        aq, ak, av, bq, bk, bv, cq, gl = jnp.split(proj, split_idx, axis=-1)

        lam_init = 0.8 - 0.6 * math.exp(-0.3 * l)
        lam = (jnp.exp(jnp.sum(lam_q1[l].astype(F32) * lam_k1[l].astype(F32)))
               - jnp.exp(jnp.sum(lam_q2[l].astype(F32) * lam_k2[l].astype(F32))) + lam_init)
        aq = apply_rope(aq.reshape(B, S, DA_HEADS, 2, HEAD_DIM), ang_1d)
        ak = apply_rope(ak.reshape(B, S, DA_HEADS, 2, HEAD_DIM), ang_1d)
        av = av.reshape(B, S, DA_HEADS, DA_V_DIM)
        oa = diff_attention(aq, ak, av, lam)
        oa = rms_norm(oa, subln_g[l]) * (1.0 - lam_init)

        bq = apply_rope(rms_norm(bq.reshape(B, S, GQ_HEADS, HEAD_DIM), q_norm_g[l]), ang_2d)
        bk = apply_rope(rms_norm(bk.reshape(B, S, GQ_KV_HEADS, HEAD_DIM), k_norm_g[l]), ang_2d)
        bq = bq.reshape(B, S, GQ_KV_HEADS, GQ_REP, HEAD_DIM)
        bv = bv.reshape(B, S, GQ_KV_HEADS, HEAD_DIM)
        ob = gqa_attention(bq, bk, bv)

        oc = memory_attention(cq.reshape(B, S, MX_HEADS, MX_HEAD_DIM), mk, mv)

        ya = oa.reshape(B, S, BRANCH_W) @ w_up_a[l]
        yb = ob.reshape(B, S, BRANCH_W) @ w_up_b[l]
        yc = oc.reshape(B, S, BRANCH_W) @ w_up_c[l]
        g = jax.nn.sigmoid(gl.astype(F32)).astype(x.dtype).reshape(B, S, N_BRANCHES, D)
        merged = g[:, :, 0] * ya + g[:, :, 1] * yb + g[:, :, 2] * yc
        x = x + merged @ w_out[l]

        h2 = rms_norm(x, norm2_g[l]).reshape(B * S, D)
        experts, weights = hier_route(h2, w_router_group[l], b_router_group[l],
                                      w_router_expert[l], b_router_expert[l])
        y = moe_forward(h2, experts, weights, w_exp_gate[l], w_exp_up[l], w_exp_down[l])
        x = x + y.reshape(B, S, D)

    return rms_norm(x, final_norm_g)


_drawn_inputs = setup_inputs


def setup_inputs(seed=0):
    import zlib

    import numpy as np

    out = dict(_drawn_inputs(seed))
    spreads = {}
    factors = {'mem_norm_g': 4.774,
     'q_norm_g': 5.048,
     'k_norm_g': 5.954,
     'b_router_group': 4.12,
     'b_router_expert': 3.202,
     'final_norm_g': 7.845,
     'lam_q2': 4.334,
     'subln_g': 2.837}
    for name, (base, spread) in spreads.items():
        noise = np.random.default_rng([zlib.crc32(name.encode()), seed]).standard_normal(out[name].shape)
        drawn = base * np.exp(spread * noise) if base else spread * noise
        out[name] = __import__('jax').numpy.asarray(drawn.astype(out[name].dtype))
    for name, factor in factors.items():
        out[name] = (out[name] * factor).astype(out[name].dtype)
    return out
```

```python
import math
from contextlib import ExitStack

import numpy as np

import concourse.bass as bass
from concourse import mybir

F32 = mybir.dt.float32
F32R = mybir.dt.float32r
I32 = mybir.dt.int32
ALU = mybir.AluOpType
ACT = mybir.ActivationFunctionType
AX = mybir.AxisListType

P = 128
D = 1024
SEQ = 512
DEPTH = 2
MEM = 256
HD = 64
GRID_W = 64
EPS = 1e-6
NG, EPG = 4, 8
NE = NG * EPG
TOPK = 2
FE = 512
KT = D // P
TT = SEQ // P
SLOTS = SEQ * TOPK
CAP = 96
MAXOV = SLOTS // CAP
NSMALL = 13 * DEPTH + 11
HALF = SLOTS // 2

AQ, AK, AV, BQ, BK, BV, CQ, GL = 0, 512, 1024, 1536, 2048, 2176, 2304, 2816

RING = 6
DENSE_PANELS = (
    ("in", AQ, 512), ("in", AK, 512), ("in", AV, 512),
    ("in", GL, 512), ("up", 0, 0), ("in", GL + 512, 512),
    ("in", BQ, 512), ("in", BK, 128), ("in", BV, 128),
    ("in", GL + 1024, 512), ("up", 1, 0), ("in", GL + 1536, 512),
    ("in", CQ, 512),
    ("in", GL + 2048, 512), ("up", 2, 0), ("in", GL + 2560, 512),
    ("out", 0, 512), ("out", 512, 512),
)
FIRST_PANELS = 2
PER_DV, PER_DA, FIRST_DA = 48, 36, 6
DENSE_USED = (("dv", 4), ("dv", 8), ("da", 4), ("da", 8), ("dv", 16), ("da", 12),
              ("dv", 20), ("dv", 24), ("da", 16), ("da", 20), ("dv", 32), ("da", 24),
              ("da", 28), ("da", 32), ("dv", 40), ("da", 36), ("dv", 44), ("dv", 48))
ND = len(DENSE_PANELS)
PER_LAYER = ND + 3 * NE
assert PER_LAYER % RING == 0 and (3 * 2) % RING == 0

ITEMS = [(br, j, t) for br in range(3) for j in (range(4) if br < 2 else range(2)) for t in range(TT)]
BRANCH_ITEMS = [[n for n, it in enumerate(ITEMS) if it[0] == br] for br in range(3)]
NI = len(ITEMS)


def build(nc, a, out):
    with ExitStack() as ctx:
        return _build(nc, ctx, a, out)


def _build(nc, ctx, a, out):
    def sem(name):
        return ctx.enter_context(nc.semaphore(name))

    def sb(name, shape, dt=F32):
        return ctx.enter_context(nc.sbuf_tensor(name, shape, dt))

    KB = 1024
    arena_kb = 78
    base = -(-nc.sbuf_base // 64) * 64
    sb("arena", [P, (arena_kb * KB + base - nc.sbuf_base) // 4 + 16])
    ring = [sb(f"ring{i}", [P, 4096]) for i in range(RING)]
    xres = sb("xres", [P, TT, D])
    ident = sb("ident", [P, P])
    ones = sb("ones", [P, P])
    upper = sb("upper", [P, P])
    cosA = sb("cosA", [P, TT, 32])
    sinA = sb("sinA", [P, TT, 2, 32])
    cosB = sb("cosB", [P, TT, 32])
    sinB = sb("sinB", [P, TT, 2, 32])
    memkT = sb("memkT", [P, 4, MEM])
    memv = sb("memv", [P, 2, 512])
    router_w = sb("router_w", [P, DEPTH, KT, NG + NE])
    router_b = sb("router_b", [P, DEPTH, NG + NE])
    gcols = sb("gcols", [P, 2 * DEPTH + 1, KT])
    subg = sb("subg", [P, DEPTH])
    qg = sb("qg", [P, DEPTH, 2, HD])
    laminit = sb("laminit", [P, DEPTH, 2])
    lamd = sb("lamd", [P, 2 * DEPTH])
    lam = sb("lam", [P, DEPTH])
    eps = sb("eps", [P, 1])
    ss = sb("ss", [P, TT])
    std = sb("std", [P, TT])
    rstd = sb("rstd", [P, TT])
    mx = sb("mx", [P, 4])
    nbias = sb("nbias", [P, 4])
    rowsum = sb("rowsum", [P, 4])
    rsum = sb("rsum", [P, 4])
    hss = sb("hss", [P, 8])
    hstd = sb("hstd", [P, 8])
    hr = sb("hr", [P, 8])
    sidx = sb("sidx", [1, NE], I32)
    ovn = sb("ovn", [1, 1], I32)
    ove = sb("ove", [1, MAXOV], I32)
    ovs = sb("ovs", [1, MAXOV], I32)
    destf = sb("destf", [P, 2, TT])
    desth = sb("desth", [P, 2, TT])
    desti = sb("desti", [P, 2, TT], I32)
    wts = sb("wts", [P, 2, TT])

    def at(name, shape, kb, dt=F32):
        size = 4 * int(np.prod(shape[1:]))
        assert kb * KB + size <= arena_kb * KB, name
        return nc.alloc_sbuf_tensor_at(name, shape, dt, offset=base + int(kb * KB))

    lamv = at("lamv", [P, 4 * DEPTH, HD], 52)
    hT = at("hT", [P, KT, SEQ], 0)
    memx = at("memx", [P, 2, D], 16)
    qT = at("qT", [P, 4, SEQ], 16)
    kT = at("kT", [P, 4, SEQ], 24)
    bv = at("bv", [P, TT, P], 32)
    av = at("av", [P, TT, 512], 32)
    oT = at("oT", [P, 4, SEQ], 40)
    mergedT = at("mergedT", [P, KT, SEQ], 48)
    prob = at("prob", [P, 4, 512], 64)
    xn = at("xn", [P, 2, D], 64)
    roped = at("roped", [P, 2, 512], 64)
    raw = at("raw", [P, 512], 68)
    tmp = at("tmp", [P, 512], 70)
    pT = at("pT", [P, 2, 4, P], 72)
    junk = at("junk", [P, D], 72)
    foldc = at("foldc", [P, 2, TT, 2, 32], 72)
    folds = at("folds", [P, 2, TT, 2, 32], 74)
    iota = at("iota", [P, HALF], 76)
    hsT = at("hsT", [P, KT, SLOTS + CAP], 16)
    xnH = at("xnH", [P, TT, D], 52, F32R)
    xnL = at("xnL", [P, TT, D], 0, F32R)
    pick = at("pick", [P, TT, HALF], 68, F32R)
    gate_s = at("gate_s", [P, 2, 4, CAP], 52)
    hid = at("hid", [P, 2, 4, CAP], 55)
    ysb = at("ysb", [P, 2, D], 58)
    gath = at("gath", [P, 2 * TT, D], 16)
    lg = at("lg", [P, TT, NG + NE], 16)
    em = at("em", [P, TT, NE], 17)
    cand = at("cand", [P, TT, NE], 17.5)
    sel1 = at("sel1", [P, TT, NE], 18)
    sel2 = at("sel2", [P, TT, NE], 18.5)
    gt = at("gt", [P, TT, NG], 19)
    gsel = at("gsel", [P, TT, NG], 19.25)
    first = sb("first", [P, NE])
    slotno = sb("slotno", [1, MAXOV])
    m1 = sb("m1", [P, TT])
    m2 = sb("m2", [P, TT])
    gp = sb("gp", [P, TT])
    ex = sb("ex", [P, TT])
    cnt = sb("cnt", [P, NE])
    incl = sb("incl", [P, NE])
    start = sb("start", [P, NE])
    ovc = at("ovc", [1, 4, NE], 68)
    ovr = at("ovr", [1, 6, MAXOV], 69)
    ovt = at("ovt", [1, 3, MAXOV, NE], 70)

    bank = [ctx.enter_context(nc.psum_tensor(f"bank{i}", [P, 512], F32)) for i in range(8)]
    ybuf = nc.dram_tensor("ybuf", [SLOTS + CAP, D], F32, kind="Internal").ap()

    consts_in = sem("consts_in")
    x_in = sem("x_in")
    mem_in = sem("mem_in")
    const_made = sem("const_made")
    loaded = [sem(f"loaded{i}") for i in range(RING)]
    ss_done = sem("ss_done")
    std_done = sem("std_done")
    xn_ready = sem("xn_ready")
    nt_done = sem("nt_done")
    nt_out = sem("nt_out")
    dv_done = sem("dv_done")
    dv_free = sem("dv_free")
    da_done = sem("da_done")
    da_free = sem("da_free")
    rope_ready = sem("rope_ready")
    tr_done = sem("tr_done")
    tr_out = sem("tr_out")
    hss_done = sem("hss_done")
    hstd_done = sem("hstd_done")
    s_done = sem("s_done")
    bias_ready = sem("bias_ready")
    exp_done = sem("exp_done")
    p_ready = sem("p_ready")
    pt_done = sem("pt_done")
    pt_out = sem("pt_out")
    pv_done = sem("pv_done")
    o_out = sem("o_out")
    sq_done = sem("sq_done")
    sq_sum = sem("sq_sum")
    sq_root = sem("sq_root")
    sub_out = sem("sub_out")
    merged = sem("merged")
    lg_done = sem("lg_done")
    gd_ready = sem("gd_ready")
    gexp_done = sem("gexp_done")
    sel_ready = sem("sel_ready")
    rank_done = sem("rank_done")
    tab_ready = sem("tab_ready")
    starts_ready = sem("starts_ready")
    split_ready = sem("split_ready")
    pick_ready = sem("pick_ready")
    perm_done = sem("perm_done")
    perm_out = sem("perm_out")
    pad_done = sem("pad_done")
    gate_done = sem("gate_done")
    silu_done = sem("silu_done")
    up_done = sem("up_done")
    hid_done = sem("hid_done")
    down_done = sem("down_done")
    y_out = sem("y_out")
    y_stored = sem("y_stored")
    ov = [{n: sem(f"ov_{n}{l}") for n in ("l0", "l1", "l2", "gate", "silu", "up", "hid", "down", "yout", "store", "over")}
          for l in range(DEPTH)]
    y_all = sem("y_all")
    gathered = [sem(f"gathered{i}") for i in range(2 * TT)]
    combined = sem("combined")
    fin = sem("fin")
    out_sem = sem("out_sem")
    vs = sem("vs")
    asm = sem("asm")
    lam_d = sem("lam_d")
    lam_e = sem("lam_e")
    fing_in = sem("fing_in")

    fing = at("fing", [P, D], 48)
    yfin = at("yfin", [P, 2, D], 52)

    block = ctx.enter_context(nc.Block())

    def wait(eng, s, n):
        if not isinstance(n, int) or n > 0:
            eng.wait_ge(s, n)

    def dense_used(l, kind, count):
        return (dv_done, PER_DV * l + count) if kind == "dv" else (da_done, FIRST_DA + PER_DA * l + count)

    def slot_of(l, j):
        n = FIRST_PANELS + j
        return n % RING, 16 * (l * (PER_LAYER // RING) + n // RING + 1)

    def wait_panel(eng, l, j):
        s, v = slot_of(l, j)
        eng.wait_ge(loaded[s], v)
        return ring[s]

    def wide(t, c):
        return t[:, 0:KT * c].rearrange("p (k c) -> p k c", k=KT)

    @block.sync
    def _(sp):
        sp.dma_start(memx[:], a["mem"].rearrange("b (t p) d -> p (b t) d", p=P)).then_inc(mem_in, 16)
        for n in range(2):
            sp.dma_start(wide(ring[n], 512), a["w_mem_kv"][:, n * 512:(n + 1) * 512].rearrange(
                "(k p) c -> p k c", p=P)).then_inc(loaded[n], 16)
        sp.dma_start(xres[:], a["x"].rearrange("b (t p) d -> p (b t) d", p=P)).then_inc(x_in, 16)

        for l in range(DEPTH):
            if l:
                sp.wait_ge(ov[l - 1]["over"], 1)
            for j, (kind, c0, width) in enumerate(DENSE_PANELS):
                s, _ = slot_of(l, j)
                if j >= RING:
                    kind_used, count = DENSE_USED[j - RING]
                    sp.wait_ge(*dense_used(l, kind_used, count))
                elif l == 0 and j + FIRST_PANELS >= RING:
                    sp.wait_ge(da_done, (4, 6)[j + FIRST_PANELS - RING])
                if kind == "in":
                    dst, src = wide(ring[s], width), a["w_in"][l, :, c0:c0 + width].rearrange("(k p) c -> p k c", p=P)
                elif kind == "out":
                    dst, src = wide(ring[s], width), a["w_out"][l, :, c0:c0 + width].rearrange("(k p) c -> p k c", p=P)
                else:
                    w = (a["w_up_a"], a["w_up_b"], a["w_up_c"])[c0]
                    dst, src = ring[s][:].rearrange("p (k c) -> p k c", k=4), w[l].rearrange("(k p) c -> p k c", p=P)
                sp.dma_start(dst, src).then_inc(loaded[s], 16)

            def expert_loads(i):
                for b in range(2):
                    e = 2 * i + b
                    ei = slice(e, e + 1) if isinstance(e, int) else bass.ds(e, 1)
                    for k, w in enumerate((a["w_exp_gate"], a["w_exp_up"], a["w_exp_down"])):
                        j = ND + 3 * b + k
                        s, _ = slot_of(l, j)
                        if isinstance(i, int):
                            sp.wait_ge(*dense_used(l, *DENSE_USED[j - RING]))
                        else:
                            E = NE * l + e - 2
                            sp.wait_ge(*((gate_done, E + 1), (up_done, 2 * E + 2), (down_done, 2 * E + 2))[k])
                        sp.dma_start(ring[s][:].rearrange("p (k c) -> p k c", c=w.shape[3]),
                                     w[l, ei].rearrange("e (k p) c -> p (e k) c", p=P)).then_inc(loaded[s], 16)
            expert_loads(0)
            with sp.Fori(1, NE // 2) as i:
                expert_loads(i)
            sp.wait_ge(down_done, 2 * (NE * (l + 1) - 1))
            sp.wait_ge(tab_ready, l + 1)
            nov = sp.value_load(ovn[0:1, 0:1], min_val=0, max_val=MAXOV)
            with sp.If(nov > 0):
                with sp.Fori(0, nov) as i:
                    e = sp.value_load(ove[0:1, bass.ds(i, 1)], min_val=0, max_val=NE - 1)
                    for k, w in enumerate((a["w_exp_gate"], a["w_exp_up"], a["w_exp_down"])):
                        s, _ = slot_of(l, ND + k)
                        o = ov[l]
                        sp.wait_ge(*((o["gate"], i + 1), (o["up"], 2 * i + 2), (o["down"], 2 * i + 2))[k])
                        sp.dma_start(ring[s][:].rearrange("p (k c) -> p k c", c=w.shape[3]),
                                     w[l, bass.ds(e, 1)].rearrange("e (k p) c -> p (e k) c", p=P)
                                     ).then_inc(ov[l][f"l{k}"], 16)
            sp.nop()
        for t in range(TT):
            sp.wait_ge(fin, t + 1)
            sp.dma_start(out[0, t * P:(t + 1) * P, :], yfin[:, t % 2, :]).then_inc(out_sem, 16)
            sp.wait_ge(out_sem, 16 * (t + 1))

    @block.gpsimd
    def _(pool):
        small = []

        def load(dst, src):
            small.append(pool.dma_start(dst, src, allow_slow_non_contiguous=True).then_inc(consts_in, 16))

        def col(v, n):
            return v.rearrange("(k p) -> p k", p=P)

        for l in range(DEPTH):
            load(gcols[:, 2 * l, :], col(a["norm1_g"][l], KT))
            load(gcols[:, 2 * l + 1, :], col(a["norm2_g"][l], KT))
            load(router_w[:, l, :, 0:NG], a["w_router_group"][l].rearrange("(k p) c -> p k c", p=P))
            load(router_w[:, l, :, NG:], a["w_router_expert"][l].rearrange("(k p) c -> p k c", p=P))
            load(router_b[:, l, 0:NG], a["b_router_group"][l:l + 1].broadcast_to([P, NG]))
            load(router_b[:, l, NG:], a["b_router_expert"][l:l + 1].broadcast_to([P, NE]))
            load(subg[:, l:l + 1], a["subln_g"][l:l + 1].rearrange("o p -> p o"))
            load(qg[:, l, 0], a["q_norm_g"][l:l + 1].broadcast_to([P, HD]))
            load(qg[:, l, 1], a["k_norm_g"][l:l + 1].broadcast_to([P, HD]))
            for n, name in enumerate(("lam_q1", "lam_k1", "lam_q2", "lam_k2")):
                load(lamv[:, 4 * l + n], a[name][l:l + 1].broadcast_to([P, HD]))
        load(gcols[:, 2 * DEPTH, :], col(a["mem_norm_g"], KT))
        load(cosA[:], a["cos_a"].rearrange("(t p) c -> p t c", p=P))
        load(sinA[:].rearrange("p t a c -> p t (a c)"), a["sin_a"].rearrange("(t p) c -> p t c", p=P))
        load(cosB[:], a["cos_b"].rearrange("(t p) c -> p t c", p=P))
        load(sinB[:].rearrange("p t a c -> p t (a c)"), a["sin_b"].rearrange("(t p) c -> p t c", p=P))
        load(laminit[:].rearrange("p l a -> p (l a)"), a["lam_init"].broadcast_to([P, 2 * DEPTH]))
        load(ident[:], a["ident"])
        load(upper[:], a["upper"])
        load(iota[:], a["iota"].broadcast_to([P, HALF]))
        load(first[:], a["first"].broadcast_to([P, NE]))
        load(slotno[:], a["iota"][:, 0:MAXOV])
        assert len(small) == NSMALL
        for l in range(DEPTH):
            pool.wait_ge(y_all, l + 1)
            for t in range(TT):
                for j in range(2):
                    pool.indirect_dma_start(
                        out=gath[:, 2 * t + j, :], out_offset=None, in_=ybuf[0:SLOTS, :],
                        in_offset=bass.IndirectOffsetOnAxis(ap=desti[:, j, t:t + 1], axis=0),
                    ).then_inc(gathered[2 * t + j], 16)
        pool.wait_ge(combined, DEPTH * TT)
        pool.dma_start(fing[:], a["final_norm_g"].rearrange("(o d) -> o d", o=1).broadcast_to([P, D])).then_inc(fing_in, 16)

    all_consts = 16 * NSMALL
    norm_tiles = {"mem": 0}
    for l in range(DEPTH):
        norm_tiles["n1", l] = 2 + 8 * l
        norm_tiles["n2", l] = 2 + 8 * l + 4
    norm_tiles["fin"] = 2 + 8 * DEPTH
    norm_no = {"mem": 1, "fin": 2 * DEPTH + 2} | {("n1", l): 2 + 2 * l for l in range(DEPTH)} | {("n2", l): 3 + 2 * l for l in range(DEPTH)}

    @block.tensor
    def _(pe):
        cnt_ = {"dv": 0, "da": 0, "tr": 0, "it": 0, "perm": 0}

        def dense(kind, lhs, rhs, n, cols):
            c = cnt_[kind]
            cnt_[kind] += 1
            done, free, b = (dv_done, dv_free, 0) if kind == "dv" else (da_done, da_free, 2)
            wait(pe, free, c - 1)
            for k in range(n):
                mm = pe.matmul(bank[b + c % 2][:, 0:cols], lhs(k), rhs(k), start=(k == 0), stop=(k == n - 1))
            return mm.then_inc(done, 1)

        def norm_transposes(key, nt):
            g0 = norm_tiles[key]
            for t in range(nt):
                g = g0 + t
                pe.wait_ge(xn_ready, g + 1)
                wait(pe, nt_out, g - 1)
                for k in range(KT):
                    tr = pe.transpose(bank[4 + 2 * (g % 2) + k // 4][:, (k % 4) * P:(k % 4 + 1) * P],
                                      xn[:, g % 2, k * P:(k + 1) * P], ident[:])
                tr.then_inc(nt_done, 1)

        def head_transposes(nb):
            r = cnt_["tr"]
            cnt_["tr"] += 1
            pe.wait_ge(rope_ready, r + 1)
            wait(pe, tr_out, r - 1)
            for k in range(nb):
                tr = pe.transpose(bank[4 + r % 2][:, k * P:(k + 1) * P], roped[:, r % 2, k * P:(k + 1) * P], ident[:])
            tr.then_inc(tr_done, 1)

        def by_tokens(kind, l, j, c, follow):
            w = wide(wait_panel(pe, l, j), c)
            for t in range(TT):
                mm = dense(kind, lambda k: hT[:, k, t * P:(t + 1) * P], lambda k: w[:, k, :], KT, c)
                if t < len(follow) and follow[t]:
                    head_transposes(follow[t])

        def attention(l, br):
            items = [l * NI + n for n in BRANCH_ITEMS[br]]
            wait(pe, dv_free, cnt_["dv"])
            pe.wait_ge(da_free, cnt_["da"])

            def scores(n):
                _, j, t = ITEMS[n % NI]
                tok = slice(t * P, (t + 1) * P)
                for m in range(2):
                    wait(pe, exp_done, 2 * n + m - 3)
                    b = bank[2 * (n % 2) + m]
                    if br < 2:
                        r = slice(m * HD, (m + 1) * HD)
                        kb = j if br == 0 else j // 2
                        mm = pe.matmul(b[:], qT[r, j, tok], kT[r, kb, :], start=True, stop=True)
                    else:
                        mm = pe.matmul(b[:, 0:MEM], av[:, 2 * j + m, tok], memkT[:, 2 * j + m, :], start=True, stop=True)
                    mm.then_inc(s_done, 1)

            def turn(n):
                pe.wait_ge(p_ready, n + 1)
                wait(pe, pt_out, n)
                maps = 1 if br == 0 else 2
                nk = 4 if br < 2 else 2
                for m in range(maps):
                    for k in range(nk):
                        tr = pe.transpose(bank[4 + m][:, k * P:(k + 1) * P], prob[:, 2 * (n % 2) + m, k * P:(k + 1) * P], ident[:])
                tr.then_inc(pt_done, 1)

            def values(n):
                _, j, t = ITEMS[n % NI]
                pe.wait_ge(pt_out, n + 1)
                wait(pe, o_out, n - 1)
                b = bank[6 + n % 2]
                if br == 0:
                    for k in range(4):
                        mm = pe.matmul(b[:, 0:P], av[:, k, j * P:(j + 1) * P], pT[:, 0, k, :], start=(k == 0), stop=(k == 3))
                elif br == 1:
                    for m in range(2):
                        for k in range(4):
                            mm = pe.matmul(b[m * HD:(m + 1) * HD, 0:P], bv[:, k, (j // 2) * HD:(j // 2 + 1) * HD],
                                           pT[:, m, k, :], start=(k == 0), stop=(k == 3))
                else:
                    for m in range(2):
                        for k in range(2):
                            mm = pe.matmul(b[:, m * P:(m + 1) * P], memv[:, k, (2 * j + m) * P:(2 * j + m + 1) * P],
                                           pT[:, m, k, :], start=(k == 0), stop=(k == 1))
                mm.then_inc(pv_done, 1)

            scores(items[0])
            for q, n in enumerate(items):
                if q + 1 < len(items):
                    scores(n + 1)
                if q:
                    values(n - 1)
                turn(n)
            values(items[-1])

        def gates(l, br, j0):
            up = None
            for f in range(KT):
                w = wide(wait_panel(pe, l, j0 + 2 * (f // 4)), 512) if f % 4 == 0 else w
                mm = dense("da", lambda k: w[:, k, (f % 4) * P:(f % 4 + 1) * P], lambda k: hT[:, k, :], KT, 512)
                if f == 0:
                    up = wait_panel(pe, l, j0 + 1)[:].rearrange("p (k c) -> p k c", k=4)
                    if br == 0:
                        pe.wait_ge(sub_out, 4 * (l + 1))
                    else:
                        pe.wait_ge(o_out, l * NI + BRANCH_ITEMS[br][-1] + 1)
                mm = dense("dv", lambda k: up[:, k, f * P:(f + 1) * P], lambda k: oT[:, k, :], 4, 512)

        pe.wait_ge(consts_in, all_consts)
        for l in range(DEPTH):
            pe.sem_inc(ov[l]["gate"], 1)
            pe.sem_inc(ov[l]["up"], 2)
            pe.sem_inc(ov[l]["down"], 2)
        norm_transposes("mem", 2)
        pe.wait_ge(nt_out, 2)
        pe.wait_ge(loaded[0], 16)
        w = wide(ring[0], 512)
        for h in range(4):
            mm = dense("da", lambda k: w[:, k, h * P:(h + 1) * P], lambda k: hT[:, k, 0:MEM], KT, MEM)
        pe.wait_ge(loaded[1], 16)
        w = wide(ring[1], 512)
        for t in range(2):
            mm = dense("da", lambda k: hT[:, k, t * P:(t + 1) * P], lambda k: w[:, k, :], KT, 512)

        for l in range(DEPTH):
            norm_transposes(("n1", l), TT)
            pe.wait_ge(nt_out, norm_tiles["n1", l] + TT)
            by_tokens("dv", l, 0, 512, [0, 4, 4, 4])
            by_tokens("dv", l, 1, 512, [4, 4, 4, 4])
            by_tokens("da", l, 2, 512, [4])
            pe.wait_ge(tr_out, cnt_["tr"])
            pe.wait_ge(da_free, cnt_["da"])
            attention(l, 0)
            for h in range(4):
                pe.wait_ge(sq_done, 4 * l + h + 1)
                wait(pe, sq_root, 4 * l + h - 1)
                pe.matmul(bank[4 + h % 2][:], ones[:], prob[:, h % 2, :], start=True, stop=True).then_inc(sq_sum, 1)
            gates(l, 0, 3)
            by_tokens("dv", l, 6, 512, [0, 4, 4, 4])
            by_tokens("dv", l, 7, 128, [4, 2, 2, 2])
            by_tokens("da", l, 8, 128, [2])
            pe.wait_ge(tr_out, cnt_["tr"])
            pe.wait_ge(da_free, cnt_["da"])
            attention(l, 1)
            gates(l, 1, 9)
            w = wide(wait_panel(pe, l, 12), 512)
            for h in range(4):
                mm = dense("da", lambda k: w[:, k, h * P:(h + 1) * P], lambda k: hT[:, k, :], KT, 512)
            pe.wait_ge(da_free, cnt_["da"])
            attention(l, 2)
            gates(l, 2, 13)
            pe.wait_ge(merged, 16 * (l + 1))
            pe.wait_ge(dv_free, cnt_["dv"])
            for n in range(2):
                w = wide(wait_panel(pe, l, 16 + n), 512)
                for t in range(TT):
                    mm = dense("dv", lambda k: mergedT[:, k, t * P:(t + 1) * P], lambda k: w[:, k, :], KT, 512)
            norm_transposes(("n2", l), TT)
            pe.wait_ge(nt_out, norm_tiles["n2", l] + TT)
            for t in range(TT):
                for k in range(KT):
                    mm = pe.matmul(bank[0][:, t * 36:(t + 1) * 36], hT[:, k, t * P:(t + 1) * P],
                                   router_w[:, l, k, :], start=(k == 0), stop=(k == KT - 1))
            mm.then_inc(lg_done, 1)
            pe.wait_ge(sel_ready, l + 1)
            for t in range(TT):
                for u in range(t + 1):
                    mm = pe.matmul(bank[1][:, t * NE:(t + 1) * NE], upper[:] if u == t else ones[:], cand[:, u, :],
                                   start=(u == 0), stop=(u == t))
            for u in range(TT):
                mm = pe.matmul(bank[1][:, TT * NE:(TT + 1) * NE], ones[:], cand[:, u, :], start=(u == 0), stop=(u == TT - 1))
            mm.then_inc(rank_done, 1)
            pe.wait_ge(split_ready, l + 1)
            for hf in range(2):
                pe.wait_ge(pick_ready, 2 * l + hf + 1)
                for k in range(KT):
                    g = cnt_["perm"]
                    cnt_["perm"] += 1
                    wait(pe, perm_out, g - 3)
                    for t in range(TT):
                        for part in (xnH, xnL):
                            mm = pe.matmul(bank[4 + g % 4][:], part[:, t, k * P:(k + 1) * P], pick[:, t, :],
                                           start=(t == 0 and part is xnH), stop=(t == TT - 1 and part is xnL))
                    mm.then_inc(perm_done, 1)
            pe.wait_ge(perm_out, cnt_["perm"])
            pe.wait_ge(pad_done, l + 1)
            pe.wait_ge(starts_ready, l + 1)

            def expert(i, b):
                E = NE * l + b + 2 * i
                panels = [slot_of(l, ND + 3 * b + k) for k in range(3)]
                s0 = pe.value_load(sidx[0:1, bass.ds(2 * i + b, 1)] if not isinstance(i, int) else sidx[0:1, b:b + 1],
                                   min_val=0, max_val=SLOTS)
                wg, wu, wd = (ring[s] for s, _ in panels)
                one_expert(s0, wg, wu, wd, b, [(loaded[s], v + 16 * i) for s, v in panels],
                           silu_free=(silu_done, E - 1), hid_free=(hid_done, 2 * (E - 1)), hid_at=(hid_done, 2 * E),
                           y_free=(y_out, 2 * (E - 1)), done=(gate_done, up_done, down_done))

            def one_expert(s0, wg, wu, wd, b, arrive, silu_free, hid_free, hid_at, y_free, done):
                wgv, wuv, wdv = wide(wg, 512), wide(wu, 512), wd[:].rearrange("p (k c) -> p k c", k=4)
                pe.wait_ge(*arrive[0])
                wait(pe, *silu_free)
                for f in range(4):
                    for k in range(KT):
                        mm = pe.matmul(bank[b][:, f * CAP:(f + 1) * CAP], wgv[:, k, f * P:(f + 1) * P],
                                       hsT[:, k, bass.ds(s0, CAP)], start=(k == 0), stop=(k == KT - 1))
                mm.then_inc(done[0], 1)
                pe.wait_ge(*arrive[1])
                wait(pe, *hid_free)
                for f in range(4):
                    for k in range(KT):
                        mm = pe.matmul(bank[2 + 4 * b + f // 2][:, f % 2 * CAP:(f % 2 + 1) * CAP], wuv[:, k, f * P:(f + 1) * P],
                                       hsT[:, k, bass.ds(s0, CAP)], start=(k == 0), stop=(k == KT - 1))
                    if f % 2:
                        mm.then_inc(done[1], 1)
                pe.wait_ge(*arrive[2])
                for h in range(2):
                    wait(pe, y_free[0], y_free[1] + h + 1)
                    for f in range(4):
                        if h == 0 and f % 2 == 0:
                            pe.wait_ge(hid_at[0], hid_at[1] + f // 2 + 1)
                        mm = pe.matmul(bank[4 + h][0:CAP, :], hid[:, b, f, :], wdv[:, f, h * 512:(h + 1) * 512],
                                       start=(f == 0), stop=(f == 3))
                    mm.then_inc(done[2], 1)

            for b in range(2):
                expert(0, b)
            with pe.Fori(1, NE // 2) as i:
                for b in range(2):
                    expert(i, b)
            o = ov[l]
            pe.wait_ge(tab_ready, l + 1)
            nov = pe.value_load(ovn[0:1, 0:1], min_val=0, max_val=MAXOV)
            with pe.If(nov > 0):
                with pe.Fori(0, nov) as i:
                    s0 = pe.value_load(ovs[0:1, bass.ds(i, 1)], min_val=0, max_val=SLOTS)
                    w = [ring[slot_of(l, ND + k)[0]] for k in range(3)]
                    one_expert(s0, *w, 0, [(o[f"l{k}"], 16 * i + 16) for k in range(3)],
                               silu_free=(silu_done, NE * (l + 1)), hid_free=(o["hid"], 2 * i + 2), hid_at=(o["hid"], 2 * i + 2),
                               y_free=(o["yout"], 2 * i), done=(o["gate"], o["up"], o["down"]))
                    pe.wait_ge(o["down"], 2 * i + 4)
            pe.wait_ge(down_done, 2 * NE * (l + 1))
            pe.sem_inc(o["over"], 1)

    @block.scalar
    def _(act):
        c = {"da": 0, "tr": 0}
        made = {}

        def own(s):
            made[s.name] = made.get(s.name, 0) + 1
            act.wait_ge(s, made[s.name])

        def squares(key, nt, src, ready):
            g0 = norm_tiles[key]
            for t in range(nt):
                ready(t)
                act.activation(junk[:], src(t), ACT.Square, accum_out=ss[:, t:t + 1]).then_inc(ss_done, 1)
                own(ss_done)
                act.wait_ge(ss_done, g0 + t + 1)
            act.activation(std[:, 0:nt], ss[:, 0:nt], ACT.Sqrt, scale=1.0 / D, bias=eps[:, 0:1]).then_inc(std_done, 1)
            own(std_done)

        def dense_out(dst, cols):
            n = c["da"]
            c["da"] += 1
            act.wait_ge(da_done, n + 1)
            act.activation(dst, bank[2 + n % 2][:, 0:cols], ACT.Copy).then_inc(da_free, 1)
            own(da_free)

        def heads_out(dst, tok, nb):
            n = c["tr"]
            c["tr"] += 1
            act.wait_ge(tr_done, n + 1)
            act.activation(dst[:, 0:nb, tok], bank[4 + n % 2][:, 0:nb * P].rearrange("p (b t) -> p b t", b=nb),
                           ACT.Copy).then_inc(tr_out, 1)
            own(tr_out)

        act.wait_ge(const_made, 2)
        act.wait_ge(mem_in, 16)
        squares("mem", 2, lambda t: memx[:, t, :], lambda t: None)
        act.wait_ge(lam_d, DEPTH)
        act.activation(lamd[:], lamd[:], ACT.Exp).then_inc(lam_e, 1)
        own(lam_e)
        for h in range(4):
            dense_out(memkT[:, h, :], MEM)
        for t in range(2):
            dense_out(memv[:, t, :], 512)

        def attention(l, br):
            maps_t = 1 if br == 0 else 2
            nk = 4 if br < 2 else 2
            cols = 512 if br < 2 else MEM
            scale = HD ** -0.5 if br < 2 else P ** -0.5
            items = [l * NI + n for n in BRANCH_ITEMS[br]]

            def exps(n):
                for m in range(2):
                    act.wait_ge(bias_ready, 2 * n + m + 1)
                    wait(act, pt_done, n - 1)
                    act.activation(prob[:, 2 * (n % 2) + m, 0:cols], bank[2 * (n % 2) + m][:, 0:cols], ACT.Exp,
                                   bias=nbias[:, 2 * (n % 2) + m:2 * (n % 2) + m + 1], scale=scale,
                                   accum_out=rowsum[:, 2 * (n % 2) + m:2 * (n % 2) + m + 1]).then_inc(exp_done, 1)
                    own(exp_done)

            def turned(n):
                act.wait_ge(pt_done, n + 1)
                wait(act, pv_done, n)
                for m in range(maps_t):
                    ins = act.activation(pT[:, m, 0:nk, :], bank[4 + m][:, 0:nk * P].rearrange("p (k t) -> p k t", k=nk), ACT.Copy)
                ins.then_inc(pt_out, 1)
                own(pt_out)

            def outputs(n):
                _, j, t = ITEMS[n % NI]
                tok = slice(t * P, (t + 1) * P)
                act.wait_ge(pv_done, n + 1)
                b = bank[6 + n % 2]
                if br < 2:
                    ins = act.activation(oT[:, j, tok], b[:, 0:P], ACT.Copy)
                else:
                    ins = act.activation(oT[:, 2 * j:2 * j + 2, tok], b[:, 0:2 * P].rearrange("p (m t) -> p m t", m=2), ACT.Copy)
                ins.then_inc(o_out, 1)
                own(o_out)

            exps(items[0])
            for q, n in enumerate(items):
                if q + 1 < len(items):
                    exps(n + 1)
                if q:
                    outputs(n - 1)
                turned(n)
            outputs(items[-1])

        def gates(l, br):
            for f in range(KT):
                n = c["da"]
                c["da"] += 1
                g = 24 * l + 8 * br + f
                act.wait_ge(da_done, n + 1)
                if f >= 2:
                    act.wait_ge(dv_free, 48 * l + (8, 24, 32)[br] + f - 1)
                act.activation(prob[:, g % 2, :], bank[2 + n % 2][:], ACT.Sigmoid).then_inc(da_free, 1)
                own(da_free)

        for l in range(DEPTH):
            squares(("n1", l), TT, lambda t: xres[:, t, :],
                    (lambda t: act.wait_ge(x_in, 16)) if l == 0 else (lambda t: act.wait_ge(combined, (l - 1) * TT + t + 1)))
            def turned_tile(i, nbk):
                heads_out(kT if i >= TT else qT, slice(i % TT * P, (i % TT + 1) * P), nbk if i >= TT else 4)

            for i in range(2 * TT - 1):
                turned_tile(i, 4)
            for t in range(TT):
                dense_out(av[:, t, :], 512)
                if t == 0:
                    turned_tile(2 * TT - 1, 4)
            attention(l, 0)
            for h in range(4):
                act.wait_ge(o_out, l * NI + 16)
                wait(act, sq_sum, 4 * l + h - 1)
                act.activation(prob[:, h % 2, :], oT[:, h, :], ACT.Square).then_inc(sq_done, 1)
                own(sq_done)
            for h in range(4):
                act.wait_ge(sq_sum, 4 * l + h + 1)
                wait(act, sub_out, 4 * l + h - 1)
                act.activation(prob[:, 2 + h % 2, :], bank[4 + h % 2][:], ACT.Sqrt, scale=1.0 / P,
                               bias=eps[:, 0:1]).then_inc(sq_root, 1)
                own(sq_root)
            act.wait_ge(sub_out, 4 * (l + 1))
            gates(l, 0)
            for t in range(2 * TT):
                act.wait_ge(hss_done, 8 * l + t + 1)
                nh = 8 if t < TT else 2
                act.activation(hstd[:, 0:nh], hss[:, 0:nh], ACT.Sqrt, scale=1.0 / HD, bias=eps[:, 0:1]).then_inc(hstd_done, 1)
                own(hstd_done)
                if t:
                    turned_tile(t - 1, 2)
            for t in range(TT):
                dense_out(bv[:, t, :], P)
                if t == 0:
                    turned_tile(2 * TT - 1, 2)
            attention(l, 1)
            gates(l, 1)
            for h in range(4):
                dense_out(av[:, h, :], 512)
            attention(l, 2)
            gates(l, 2)
            squares(("n2", l), TT, lambda t: xres[:, t, :], lambda t: act.wait_ge(dv_free, 48 * l + 44 + t + 1))
            act.wait_ge(gd_ready, 2 * l + 1)
            act.activation(gt[:], gt[:], ACT.Exp).then_inc(gexp_done, 1)
            own(gexp_done)
            act.wait_ge(gd_ready, 2 * l + 2)
            act.activation(ex[:], m2[:], ACT.Exp).then_inc(gexp_done, 1)
            own(gexp_done)
            for hf in range(2):
                for k in range(KT):
                    g = 16 * l + 8 * hf + k
                    act.wait_ge(perm_done, g + 1)
                    act.activation(hsT[:, k, hf * HALF:(hf + 1) * HALF], bank[4 + g % 4][:], ACT.Copy,
                                   scale=gcols[:, 2 * l + 1, k:k + 1]).then_inc(perm_out, 1)
                    own(perm_out)
            act.wait_ge(starts_ready, l + 1)

            def window(b, s0, gate_at, hid_at, up_unused, down_at, silu, y, store, store_before):
                act.wait_ge(*gate_at)
                wait(act, *hid_at)
                act.activation(gate_s[:, b], bank[b][:, 0:4 * CAP].rearrange("p (f c) -> p f c", f=4), ACT.Silu).then_inc(silu, 1)
                for h in range(2):
                    act.wait_ge(down_at[0], down_at[1] + h + 1)
                    if h == 0:
                        wait(act, store[0], store_before)
                    act.activation(ysb[0:CAP, b, h * 512:(h + 1) * 512], bank[4 + h][0:CAP, :], ACT.Copy).then_inc(y[0], 1)
                act.wait_ge(y[0], y[1] + 2)
                act.dma_start(ybuf[bass.ds(s0, CAP), :], ysb[0:CAP, b, :]).then_inc(store[0], 16)

            def expert(i, b):
                E = NE * l + 2 * i + b
                s0 = act.value_load(sidx[0:1, bass.ds(2 * i + b, 1)] if not isinstance(i, int) else sidx[0:1, b:b + 1],
                                    min_val=0, max_val=SLOTS)
                window(b, s0, (gate_done, E + 1), (hid_done, 2 * (E - 1)), None, (down_done, 2 * E), silu_done,
                       (y_out, 2 * E), (y_stored,), 16 * E)

            for b in range(2):
                expert(0, b)
            with act.Fori(1, NE // 2) as i:
                for b in range(2):
                    expert(i, b)
            act.wait_ge(y_stored, 16 * NE * (l + 1))
            act.wait_ge(tab_ready, l + 1)
            o = ov[l]
            act.sem_inc(o["yout"], 2)
            nov = act.value_load(ovn[0:1, 0:1], min_val=0, max_val=MAXOV)
            with act.If(nov > 0):
                with act.Fori(0, nov) as i:
                    s0 = act.value_load(ovs[0:1, bass.ds(i, 1)], min_val=0, max_val=SLOTS)
                    window(0, s0, (o["gate"], i + 2), (o["hid"], 2 * i + 2), None, (o["down"], 2 * i + 2), o["silu"],
                           (o["yout"], 2 * i + 2), (o["store"],), 0)
                    act.wait_ge(o["store"], 16 * i + 16)
            act.sem_inc(y_all, 1)
        squares("fin", TT, lambda t: xres[:, t, :], lambda t: act.wait_ge(combined, (DEPTH - 1) * TT + t + 1))

    @block.vector
    def _(dve):
        c = {"dv": 0, "vs": 0, "rope": 0}
        made = {}

        def own(s):
            made[s.name] = made.get(s.name, 0) + 1
            dve.wait_ge(s, made[s.name])

        def v(ins):
            c["vs"] += 1
            ins.then_inc(vs, 1)
            dve.wait_ge(vs, c["vs"])

        def norm(key, nt, src, gcol, dst, xn_of=None):
            g0 = norm_tiles[key]
            dve.wait_ge(std_done, norm_no[key])
            v(dve.reciprocal(rstd[:, 0:nt], std[:, 0:nt]))

            def normalise(t):
                g = g0 + t
                wait(dve, nt_done, g - 1)
                dve.tensor_scalar(xn[:, g % 2, :], src(t), rstd[:, t:t + 1], None, ALU.mult).then_inc(xn_ready, 1)
                own(xn_ready)

            def columns(t):
                g = g0 + t
                dve.wait_ge(nt_done, g + 1)
                for h in range(2):
                    ins = dve.tensor_tensor(dst[:, 4 * h:4 * h + 4, t * P:(t + 1) * P],
                                            bank[4 + 2 * (g % 2) + h][:].rearrange("p (k t) -> p k t", k=4),
                                            gcol[:, 4 * h:4 * h + 4].unsqueeze(2).broadcast_to([P, 4, P]), ALU.mult)
                ins.then_inc(nt_out, 1)
                own(nt_out)
            normalise(0)
            for t in range(nt):
                if t + 1 < nt:
                    normalise(t + 1)
                columns(t)

        def take_dense():
            n = c["dv"]
            c["dv"] += 1
            dve.wait_ge(dv_done, n + 1)
            return bank[n % 2]

        def rotate(x, cos, sin, nh, dst, free):
            xv = x.rearrange("p (h a c) -> p h a c", a=2, c=32)
            dv = dst.rearrange("p (h a c) -> p h a c", a=2, c=32)
            tv = tmp[:, 0:nh * HD].rearrange("p (h a c) -> p h a c", a=2, c=32)
            dve.tensor_tensor(dv, xv, cos, ALU.mult)
            dve.tensor_tensor(tv[:, :, 0], xv[:, :, 1], sin[:, 0].unsqueeze(1).broadcast_to([P, nh, 32]), ALU.mult)
            ins = dve.tensor_tensor(tv[:, :, 1], xv[:, :, 0], sin[:, 1].unsqueeze(1).broadcast_to([P, nh, 32]), ALU.mult)
            if free:
                ins.then_inc(dv_free, 1)
                own(dv_free)
            else:
                v(ins)
            return dve.tensor_tensor(dst, dst, tmp[:, 0:nh * HD], ALU.add)

        dve.memset(ones[:], 1.0).then_inc(const_made, 1)
        own(const_made)
        dve.memset(eps[:], EPS).then_inc(const_made, 1)
        own(const_made)
        dve.wait_ge(consts_in, all_consts)
        dve.wait_ge(const_made, 2)
        dve.wait_ge(mem_in, 16)
        for l in range(DEPTH):
            lv = lamv[:, 4 * l:4 * l + 4, :].rearrange("p (a b) c -> p a b c", b=2)
            v(dve.tensor_tensor(lv[:, :, 0], lv[:, :, 0], lv[:, :, 1], ALU.mult))
            dve.tensor_reduce(lamd[:, 2 * l:2 * l + 2], lv[:, :, 0], AX.X, ALU.add).then_inc(lam_d, 1)
            own(lam_d)
        dve.wait_ge(lam_e, 1)
        for l in range(DEPTH):
            v(dve.tensor_tensor(lam[:, l:l + 1], lamd[:, 2 * l:2 * l + 1], lamd[:, 2 * l + 1:2 * l + 2], ALU.subtract))
            v(dve.tensor_tensor(lam[:, l:l + 1], lam[:, l:l + 1], laminit[:, l, 0:1], ALU.add))
            v(dve.tensor_tensor(subg[:, l:l + 1], subg[:, l:l + 1], laminit[:, l, 1:2], ALU.mult))
        norm("mem", 2, lambda t: memx[:, t, :], gcols[:, 2 * DEPTH, :], hT)

        def attention(l, br):
            cols = 512 if br < 2 else MEM
            scale = HD ** -0.5 if br < 2 else P ** -0.5
            items = [l * NI + n for n in BRANCH_ITEMS[br]]

            def maxima(n):
                for m in range(2):
                    q = 2 * (n % 2) + m
                    dve.wait_ge(s_done, 2 * n + m + 1)
                    wait(dve, exp_done, 2 * n + m - 3)
                    v(dve.tensor_reduce(mx[:, q:q + 1], bank[q][:, 0:cols], AX.X, ALU.max))
                    dve.tensor_scalar(nbias[:, q:q + 1], mx[:, q:q + 1], -scale, None, ALU.mult).then_inc(bias_ready, 1)
                    own(bias_ready)

            def normalise(n):
                q = 2 * (n % 2)
                dve.wait_ge(exp_done, 2 * n + 2)
                v(dve.reciprocal(rsum[:, q:q + 2], rowsum[:, q:q + 2]))
                p0, p1 = prob[:, q, 0:cols], prob[:, q + 1, 0:cols]
                if br == 0:
                    v(dve.tensor_scalar(p1, p1, rsum[:, q + 1:q + 2], lam[:, l:l + 1], ALU.mult, ALU.mult))
                    ins = dve.scalar_tensor_tensor(out=p0, in0=p0, scalar=rsum[:, q:q + 1], in1=p1, op0=ALU.mult, op1=ALU.subtract)
                else:
                    dve.tensor_scalar(p0, p0, rsum[:, q:q + 1], None, ALU.mult)
                    ins = dve.tensor_scalar(p1, p1, rsum[:, q + 1:q + 2], None, ALU.mult)
                ins.then_inc(p_ready, 1)
                own(p_ready)

            maxima(items[0])
            for q, n in enumerate(items):
                if q + 1 < len(items):
                    maxima(n + 1)
                normalise(n)

        def gates(l, br):
            for f in range(KT):
                g = 24 * l + 8 * br + f
                b = take_dense()
                nact = 6 + 36 * l + (4, 16, 28)[br] + f + 1
                dve.wait_ge(da_free, nact)
                if br == 0:
                    ins = dve.tensor_tensor(mergedT[:, f, :], prob[:, g % 2, :], b[:], ALU.mult)
                    ins.then_inc(dv_free, 1)
                    own(dv_free)
                else:
                    dve.tensor_tensor(tmp[:], prob[:, g % 2, :], b[:], ALU.mult).then_inc(dv_free, 1)
                    own(dv_free)
                    dve.tensor_tensor(mergedT[:, f, :], mergedT[:, f, :], tmp[:], ALU.add).then_inc(merged, 1)
                    own(merged)

        for l in range(DEPTH):
            norm(("n1", l), TT, lambda t: xres[:, t, :], gcols[:, 2 * l, :], hT)
            for i in range(2 * TT):
                t = i % TT
                b = take_dense()
                r = c["rope"]
                c["rope"] += 1
                wait(dve, tr_done, r - 1)
                rotate(b[:], cosA[:, t].unsqueeze(1).unsqueeze(1).broadcast_to([P, 8, 2, 32]), sinA[:, t], 8,
                       roped[:, r % 2, :], True).then_inc(rope_ready, 1)
                own(rope_ready)
            attention(l, 0)
            for h in range(4):
                dve.wait_ge(sq_root, 4 * l + h + 1)
                v(dve.reciprocal(prob[:, 2 + h % 2, :], prob[:, 2 + h % 2, :]))
                dve.scalar_tensor_tensor(out=oT[:, h, :], in0=oT[:, h, :], scalar=subg[:, l:l + 1], in1=prob[:, 2 + h % 2, :],
                                         op0=ALU.mult, op1=ALU.mult).then_inc(sub_out, 1)
                own(sub_out)
            gates(l, 0)
            for m in range(2):
                for t in range(TT):
                    g2 = qg[:, l, m].rearrange("p (a c) -> p a c", a=2)
                    dve.tensor_tensor(foldc[:, m, t], g2, cosB[:, t].unsqueeze(1).broadcast_to([P, 2, 32]), ALU.mult)
                    dve.tensor_tensor(folds[:, m, t, 0], g2[:, 1], sinB[:, t, 0], ALU.mult)
                    last = dve.tensor_tensor(folds[:, m, t, 1], g2[:, 0], sinB[:, t, 1], ALU.mult)
            v(last)
            for i in range(2 * TT):
                t, m = i % TT, i // TT
                nh = 8 if m == 0 else 2
                w = nh * HD
                b = take_dense()
                r = c["rope"]
                c["rope"] += 1
                dve.tensor_copy(raw[:, 0:w], b[:, 0:w]).then_inc(dv_free, 1)
                own(dv_free)
                v(dve.tensor_tensor(tmp[:, 0:w], raw[:, 0:w], raw[:, 0:w], ALU.mult))
                dve.tensor_reduce(hss[:, 0:nh], tmp[:, 0:w].rearrange("p (h c) -> p h c", c=HD), AX.X, ALU.add).then_inc(hss_done, 1)
                own(hss_done)
                dve.wait_ge(hstd_done, 8 * l + i + 1)
                v(dve.reciprocal(hr[:, 0:nh], hstd[:, 0:nh]))
                rv = raw[:, 0:w].rearrange("p (h c) -> p h c", c=HD)
                v(dve.tensor_tensor(rv, rv, hr[:, 0:nh].unsqueeze(2).broadcast_to([P, nh, HD]), ALU.mult))
                wait(dve, tr_done, r - 1)
                fc = foldc[:, m, t].unsqueeze(1).broadcast_to([P, nh, 2, 32])
                if m == 0:
                    rotate(raw[:, 0:w], fc, folds[:, m, t], nh, roped[:, r % 2, :], False).then_inc(rope_ready, 1)
                    own(rope_ready)
                else:
                    v(rotate(raw[:, 0:w], fc, folds[:, m, t], nh, roped[:, r % 2, 256:256 + w], False))
                    dve.tensor_copy(roped[:, r % 2, 0:256].rearrange("p (h a c) -> p h a c", a=2, c=HD),
                                    roped[:, r % 2, 256:384].rearrange("p (h c) -> p h c", c=HD).unsqueeze(2).broadcast_to(
                                        [P, 2, 2, HD])).then_inc(rope_ready, 1)
                    own(rope_ready)
            attention(l, 1)
            gates(l, 1)
            attention(l, 2)
            gates(l, 2)
            for n in range(2):
                for t in range(TT):
                    b = take_dense()
                    xs = xres[:, t, n * 512:(n + 1) * 512]
                    dve.tensor_tensor(xs, xs, b[:], ALU.add).then_inc(dv_free, 1)
                    own(dv_free)
            norm(("n2", l), TT, lambda t: xres[:, t, :], gcols[:, 2 * l + 1, :], hT)
            dve.memset(hsT[:, :, SLOTS:], 0.0).then_inc(pad_done, 1)
            own(pad_done)

            dve.wait_ge(lg_done, l + 1)
            v(dve.tensor_tensor(lg[:], bank[0][:, 0:TT * 36].rearrange("p (t c) -> p t c", t=TT),
                                router_b[:, l, :].unsqueeze(1).broadcast_to([P, TT, 36]), ALU.add))

            def argmax(vals, width, m, sel, cnd):
                v(dve.tensor_reduce(m, vals, AX.X, ALU.max))
                v(dve.tensor_tensor(cnd, vals, m.unsqueeze(2).broadcast_to([P, TT, width]), ALU.is_equal))
                v(dve.tensor_tensor(cnd, cnd, first[:, 0:width].unsqueeze(1).broadcast_to([P, TT, width]), ALU.mult))
                v(dve.tensor_reduce(ex[:], cnd, AX.X, ALU.max))
                v(dve.tensor_tensor(sel, cnd, ex[:].unsqueeze(2).broadcast_to([P, TT, width]), ALU.is_equal))

            lgg = lg[:, :, 0:NG]
            argmax(lgg, NG, m1[:], gsel[:], gt[:])
            dve.tensor_tensor(gt[:], lgg, m1[:].unsqueeze(2).broadcast_to([P, TT, NG]), ALU.subtract).then_inc(gd_ready, 1)
            own(gd_ready)
            v(dve.tensor_scalar(gsel[:], gsel[:], 1.0, 1e30, ALU.subtract, ALU.mult))
            v(dve.tensor_tensor(em[:].rearrange("p t (g e) -> p t g e", g=NG),
                                lg[:, :, NG:].rearrange("p t (g e) -> p t g e", g=NG),
                                gsel[:].unsqueeze(3).broadcast_to([P, TT, NG, EPG]), ALU.add))
            argmax(em[:], NE, m1[:], sel1[:], cand[:])
            v(dve.tensor_scalar(cand[:], sel1[:], -3e38, None, ALU.mult))
            v(dve.tensor_tensor(em[:], em[:], cand[:], ALU.add))
            argmax(em[:], NE, m2[:], sel2[:], cand[:])
            dve.tensor_tensor(cand[:], sel1[:], sel2[:], ALU.add).then_inc(sel_ready, 1)
            own(sel_ready)
            dve.wait_ge(gexp_done, 2 * l + 1)
            dve.tensor_tensor(m2[:], m2[:], m1[:], ALU.subtract).then_inc(gd_ready, 1)
            own(gd_ready)
            v(dve.tensor_reduce(gp[:], gt[:], AX.X, ALU.add))
            v(dve.reciprocal(gp[:], gp[:]))
            dve.wait_ge(gexp_done, 2 * l + 2)
            v(dve.tensor_scalar(m1[:], ex[:], 1.0, None, ALU.add))
            v(dve.reciprocal(m1[:], m1[:]))
            v(dve.tensor_tensor(wts[:, 0], gp[:], m1[:], ALU.mult))
            v(dve.tensor_tensor(wts[:, 1], wts[:, 0], ex[:], ALU.mult))
            for t in range(TT):
                v(dve.tensor_scalar(xnH[:, t, :], xres[:, t, :], rstd[:, t:t + 1], None, ALU.mult))
                ins = dve.scalar_tensor_tensor(out=xnL[:, t, :], in0=xres[:, t, :], scalar=rstd[:, t:t + 1],
                                               in1=xnH[:, t, :].bitcast(F32), op0=ALU.mult, op1=ALU.subtract)
            ins.then_inc(split_ready, 1)
            own(split_ready)
            dve.wait_ge(rank_done, l + 1)
            v(dve.tensor_copy(cnt[:], bank[1][:, TT * NE:(TT + 1) * NE]))
            v(dve.tensor_tensor_scan(incl[:], ones[:, 0:NE], cnt[:], 0.0, ALU.mult, ALU.add))
            v(dve.tensor_tensor(start[:], incl[:], cnt[:], ALU.subtract))
            v(dve.tensor_tensor(em[:], bank[1][:, 0:TT * NE].rearrange("p (t e) -> p t e", t=TT),
                                start[:].unsqueeze(1).broadcast_to([P, TT, NE]), ALU.add))
            for j, s in enumerate((sel1, sel2)):
                v(dve.tensor_tensor(s[:], s[:], em[:], ALU.mult))
                v(dve.tensor_reduce(destf[:, j], s[:], AX.X, ALU.add))
            dve.tensor_copy(desti[:], destf[:])
            v(dve.tensor_copy(sidx[:], start[0:1]))
            dve.sem_inc(starts_ready, 1)
            for hf in range(2):
                v(dve.tensor_scalar(desth[:], destf[:], float(-hf * HALF), None, ALU.add))
                if hf:
                    dve.wait_ge(perm_done, 16 * l + 8)
                for t in range(TT):
                    v(dve.tensor_scalar(pick[:, t, :], iota[:], desth[:, 0, t:t + 1], None, ALU.is_equal))
                    ins = dve.scalar_tensor_tensor(out=pick[:, t, :], in0=iota[:], scalar=desth[:, 1, t:t + 1],
                                                   in1=pick[:, t, :].bitcast(F32),
                                                   op0=ALU.is_equal, op1=ALU.add)
                    if t == TT - 1:
                        ins.then_inc(pick_ready, 1)
                        own(pick_ready)
                    else:
                        v(ins)
            dve.wait_ge(perm_done, 16 * (l + 1))
            c0, s0, e0 = cnt[0:1], start[0:1], incl[0:1]
            n_ov, cum, exc, t_ = (ovc[:, q] for q in range(4))
            v(dve.tensor_scalar(n_ov, c0, float(CAP), None, ALU.is_gt))
            for q in range(2, SEQ // CAP + 1):
                v(dve.tensor_scalar(t_, c0, float(CAP * q), None, ALU.is_gt))
                v(dve.tensor_tensor(n_ov, n_ov, t_, ALU.add))
            v(dve.tensor_tensor_scan(cum, ones[0:1, 0:NE], n_ov, 0.0, ALU.mult, ALU.add))
            v(dve.tensor_tensor(exc, cum, n_ov, ALU.subtract))
            full = [1, MAXOV, NE]
            T0, T1, T2 = (ovt[:, q] for q in range(3))
            sl = slotno[:].unsqueeze(2).broadcast_to(full)

            def per_e(x):
                return x.unsqueeze(1).broadcast_to(full)
            v(dve.tensor_tensor(T0, per_e(cum), sl, ALU.is_le))
            v(dve.tensor_reduce(ovr[:, 0], T0, AX.X, ALU.add))
            v(dve.tensor_tensor(T1, per_e(exc), sl, ALU.is_le))
            v(dve.tensor_tensor(T1, T1, T0, ALU.subtract))
            for q, x in ((1, s0), (2, e0), (3, exc)):
                v(dve.tensor_tensor(T2, T1, per_e(x), ALU.mult))
                v(dve.tensor_reduce(ovr[:, q], T2, AX.X, ALU.add))
            v(dve.tensor_tensor(ovr[:, 4], slotno[:], ovr[:, 3], ALU.subtract))
            v(dve.tensor_scalar(ovr[:, 4], ovr[:, 4], 1.0, float(CAP), ALU.add, ALU.mult))
            v(dve.tensor_tensor(ovr[:, 4], ovr[:, 4], ovr[:, 1], ALU.add))
            v(dve.tensor_scalar(ovr[:, 2], ovr[:, 2], float(-CAP), None, ALU.add))
            v(dve.tensor_tensor(ovr[:, 4], ovr[:, 4], ovr[:, 2], ALU.min))
            v(dve.tensor_scalar(ovr[:, 4], ovr[:, 4], 0.0, None, ALU.max))
            v(dve.tensor_scalar(ovr[:, 0], ovr[:, 0], float(NE - 1), None, ALU.min))
            dve.tensor_copy(ovs[:], ovr[:, 4])
            dve.tensor_copy(ove[:], ovr[:, 0])
            v(dve.tensor_copy(ovn[:], cum[:, NE - 1:NE]))
            dve.sem_inc(tab_ready, 1)

            def window(b, silu_at, up_at, hid_sem):
                dve.wait_ge(*silu_at)
                for h in range(2):
                    dve.wait_ge(up_at[0], up_at[1] + h + 1)
                    dve.tensor_tensor(hid[:, b, 2 * h:2 * h + 2, :], gate_s[:, b, 2 * h:2 * h + 2, :],
                                      bank[2 + 4 * b + h][:, 0:2 * CAP].rearrange("p (f c) -> p f c", f=2),
                                      ALU.mult).then_inc(hid_sem, 1)
            for b in range(2):
                window(b, (silu_done, NE * l + b + 1), (up_done, 2 * (NE * l + b)), hid_done)
            with dve.Fori(1, NE // 2) as i:
                for b in range(2):
                    E = NE * l + 2 * i + b
                    window(b, (silu_done, E + 1), (up_done, 2 * E), hid_done)
            o = ov[l]
            dve.sem_inc(o["hid"], 2)
            nov = dve.value_load(ovn[0:1, 0:1], min_val=0, max_val=MAXOV)
            with dve.If(nov > 0):
                with dve.Fori(0, nov) as i:
                    window(0, (o["silu"], i + 1), (o["up"], 2 * i + 2), o["hid"])
            dve.nop()
            for t in range(TT):
                for j in range(2):
                    dve.wait_ge(gathered[2 * t + j], 16 * (l + 1))
                    ins = dve.scalar_tensor_tensor(out=xres[:, t, :], in0=gath[:, 2 * t + j, :], scalar=wts[:, j, t:t + 1],
                                                   in1=xres[:, t, :], op0=ALU.mult, op1=ALU.add)
                    if j == 0:
                        v(ins)
                ins.then_inc(combined, 1)
                own(combined)
        dve.wait_ge(fing_in, 16)
        dve.wait_ge(std_done, norm_no["fin"])
        v(dve.reciprocal(rstd[:], std[:]))
        for t in range(TT):
            wait(dve, out_sem, 16 * (t - 1))
            dve.scalar_tensor_tensor(out=yfin[:, t % 2, :], in0=xres[:, t, :], scalar=rstd[:, t:t + 1], in1=fing[:],
                                     op0=ALU.mult, op1=ALU.mult).then_inc(fin, 1)
            own(fin)


_INS = ("x", "mem", "mem_norm_g", "w_mem_kv", "norm1_g", "w_in", "lam_q1", "lam_k1", "lam_q2", "lam_k2",
        "subln_g", "q_norm_g", "k_norm_g", "w_up_a", "w_up_b", "w_up_c", "w_out", "norm2_g",
        "w_router_group", "b_router_group", "w_router_expert", "b_router_expert",
        "w_exp_gate", "w_exp_up", "w_exp_down", "final_norm_g")


def _constants():
    pos = np.arange(SEQ, dtype=np.float32)
    inv = (10000.0 ** (-np.arange(0, HD, 2, dtype=np.float32) / HD)).astype(np.float32)
    ang_a = pos[:, None] * inv
    inv = (10000.0 ** (-np.arange(0, HD // 2, 2, dtype=np.float32) / (HD // 2))).astype(np.float32)
    ang_b = np.concatenate([(pos // GRID_W)[:, None] * inv, (pos % GRID_W)[:, None] * inv], 1)
    made = {}
    for n, ang in (("a", ang_a), ("b", ang_b)):
        ang = ang.astype(np.float32).astype(np.float64)
        made["cos_" + n] = np.cos(ang)
        made["sin_" + n] = np.concatenate([-np.sin(ang), np.sin(ang)], 1)
    li = [0.8 - 0.6 * math.exp(-0.3 * l) for l in range(DEPTH)]
    made["lam_init"] = np.array([[x for l in li for x in (l, 1.0 - l)]])
    made["ident"] = np.eye(P)
    made["upper"] = np.triu(np.ones((P, P)), 1)
    made["iota"] = np.arange(HALF)[None]
    made["first"] = (NE - np.arange(NE))[None]
    return {k: np.ascontiguousarray(v, np.float32) for k, v in made.items()}


def kernel(**inputs):
    import concourse.bacc as bacc
    from concourse.bass_utils import run_bass_kernel_spmd

    nc = bacc.Bacc("TRN2", target_bir_lowering=False, num_devices=1)
    given = {n: np.ascontiguousarray(inputs[n]) for n in _INS} | _constants()
    arrays, aps = {}, {}
    for name, arr in given.items():
        arrays[f"in_{name}"] = arr
        aps[name] = nc.dram_tensor(f"in_{name}", arr.shape, mybir.dt.from_np(arr.dtype), kind="ExternalInput").ap()
    result = nc.dram_tensor("result", (1, SEQ, D), F32, kind="ExternalOutput").ap()
    build(nc, aps, result)
    r = run_bass_kernel_spmd(nc, [arrays], core_ids=[0])
    return r.results[0]["result"]
```

```python
import math
from contextlib import ExitStack

import numpy as np

import concourse.bass as bass
from concourse import mybir

F32 = mybir.dt.float32
F32R = mybir.dt.float32r
I32 = mybir.dt.int32
ALU = mybir.AluOpType
ACT = mybir.ActivationFunctionType
AX = mybir.AxisListType

P = 128
D = 1024
SEQ = 512
DEPTH = 2
MEM = 256
HD = 64
GRID_W = 64
EPS = 1e-6
NG, EPG = 4, 8
NE = NG * EPG
TOPK = 2
FE = 512
KT = D // P
TT = SEQ // P
SLOTS = SEQ * TOPK
CAP = 96
MAXOV = SLOTS // CAP
NSMALL = 13 * DEPTH + 11
HALF = SLOTS // 2

AQ, AK, AV, BQ, BK, BV, CQ, GL = 0, 512, 1024, 1536, 2048, 2176, 2304, 2816

RING = 6
MEM_SLOTS = (5, 4)
DENSE_PANELS = (
    ("in", AQ, 512, "dv", 8), ("in", AK, 512, "dv", 8), ("in", AV, 512, "da", 8),
    ("in", GL, 512, "da", 4), ("in", GL + 512, 512, "da", 4), ("up", 0, 0, "dv", 8),
    ("in", BQ, 512, "dv", 8), ("in", BK, 256, "dv", 4),
    ("in", GL + 1024, 512, "da", 4), ("in", GL + 1536, 512, "da", 4), ("up", 1, 0, "dv", 8),
    ("in", CQ, 512, "da", 4),
    ("in", GL + 2048, 512, "da", 4), ("in", GL + 2560, 512, "da", 4), ("up", 2, 0, "dv", 8),
    ("out", 0, 512, "dv", 8), ("out", 512, 512, "dv", 8),
)
ND = len(DENSE_PANELS)
PANEL_AT = {n: j for j, n in enumerate(("aq", "ak", "av", "gate0", "", "up0", "bq", "bkv", "gate1", "", "up1",
                                        "cq", "gate2", "", "up2", "out0", "out1")) if n}
PER_DV = sum(n for *_, kind, n in DENSE_PANELS if kind == "dv")
PER_DA = sum(n for *_, kind, n in DENSE_PANELS if kind == "da")
FIRST_DA = 6
UPS_DV = [sum(p[4] for p in DENSE_PANELS[:PANEL_AT[f"up{br}"] + 1] if p[3] == "dv") for br in range(3)]
CW = 256
CHUNKS = [(j, c) for j, p in enumerate(DENSE_PANELS) for c in range(p[2] // CW)]
NC = len(CHUNKS)


def used_after(l, j, c=None):
    kind, n = DENSE_PANELS[j][3:]
    before = sum(p[4] for p in DENSE_PANELS[:j] if p[3] == kind)
    parts = max(DENSE_PANELS[j][2] // CW, 1)
    return kind, (PER_DV * l if kind == "dv" else FIRST_DA + PER_DA * l) + before + n * (parts if c is None else c + 1) // parts


DRING = 2
PARTS_SLOT, LOW_SLOT, GATE_SLOT = 2, 4, 5
EXPERT_SLOTS = ((5, 1, 0), (3, 2, 4))
OVER_SLOTS = (5, 3, 2)


def dense_slot(l, j):
    slot = j % DRING
    return slot, l * len(range(slot, ND, DRING)) + j // DRING + 1


ITEMS = [(br, j, t) for br in range(3) for j in (range(4) if br < 2 else range(2)) for t in range(TT)]
BRANCH_ITEMS = [[n for n, it in enumerate(ITEMS) if it[0] == br] for br in range(3)]
NI = len(ITEMS)


def build(nc, a, out):
    with ExitStack() as ctx:
        return _build(nc, ctx, a, out)


def _build(nc, ctx, a, out):
    def sem(name):
        return ctx.enter_context(nc.semaphore(name))

    def sb(name, shape, dt=F32):
        return ctx.enter_context(nc.sbuf_tensor(name, shape, dt))

    KB = 1024
    arena_kb = 78
    base = -(-nc.sbuf_base // 64) * 64
    sb("arena", [P, (arena_kb * KB + base - nc.sbuf_base) // 4])
    ring_base = -(-nc.sbuf_base // 64) * 64
    sb("ring_space", [P, RING * 4096 + (ring_base - nc.sbuf_base) // 4])
    ring = [nc.alloc_sbuf_tensor_at(f"ring{i}", [P, 4096], F32, offset=ring_base + i * 16 * KB) for i in range(RING)]
    xres = sb("xres", [P, TT, D])
    ident = sb("ident", [P, P])
    ones = sb("ones", [P, P])
    upper = sb("upper", [P, P])
    cosA = sb("cosA", [P, TT, 32])
    sinA = sb("sinA", [P, TT, 2, 32])
    cosB = sb("cosB", [P, TT, 32])
    sinB = sb("sinB", [P, TT, 2, 32])
    memkT = sb("memkT", [P, 4, MEM])
    memv = sb("memv", [P, 2, 512])
    router_w = sb("router_w", [P, DEPTH, KT, NG + NE])
    router_b = sb("router_b", [P, DEPTH, NG + NE])
    gcols = sb("gcols", [P, 2 * DEPTH + 1, KT])
    subg = sb("subg", [P, DEPTH])
    qg = sb("qg", [P, DEPTH, 2, HD])
    laminit = sb("laminit", [P, DEPTH, 2])
    lamd = sb("lamd", [P, 2 * DEPTH])
    lam = sb("lam", [P, DEPTH])
    eps = sb("eps", [P, 1])
    ss = sb("ss", [P, TT])
    std = sb("std", [P, TT])
    rstd = sb("rstd", [P, TT])
    mx = sb("mx", [P, 4])
    nbias = sb("nbias", [P, 4])
    rowsum = sb("rowsum", [P, 4])
    rsum = sb("rsum", [P, 4])
    hsq = sb("hsq", [P, 4 * TT])
    hss = sb("hss", [P, 8])
    hstd = sb("hstd", [P, 8])
    hr = sb("hr", [P, 8])
    sidx = sb("sidx", [1, NE], I32)
    ovn = sb("ovn", [1, 1], I32)
    ove = sb("ove", [1, MAXOV], I32)
    ovs = sb("ovs", [1, MAXOV], I32)
    destf = sb("destf", [P, 2, TT])
    desth = sb("desth", [P, 2, TT])
    desti = sb("desti", [P, 2, TT], I32)
    wts = sb("wts", [P, 2, TT])

    def at(name, shape, kb, dt=F32):
        size = 4 * int(np.prod(shape[1:]))
        assert kb * KB + size <= arena_kb * KB, name
        return nc.alloc_sbuf_tensor_at(name, shape, dt, offset=base + int(kb * KB))

    gates_s = nc.alloc_sbuf_tensor_at("gates_s", [P, KT, SEQ], F32, offset=ring_base + GATE_SLOT * 16 * KB)
    lamv = at("lamv", [P, 4 * DEPTH, HD], 52)
    hT = at("hT", [P, KT, SEQ], 0)
    memx = at("memx", [P, 2, D], 16)
    qT = at("qT", [P, 4, SEQ], 16)
    kT = at("kT", [P, 4, SEQ], 24)
    bv = at("bv", [P, TT, P], 32)
    av = at("av", [P, TT, 512], 32)
    oT = at("oT", [P, 4, SEQ], 40)
    hH = at("hH", [P, KT, SEQ], 0, F32R)
    hL = nc.alloc_sbuf_tensor_at("hL", [P, KT, SEQ], F32R, offset=ring_base + LOW_SLOT * 16 * KB)
    wH = [nc.alloc_sbuf_tensor_at(f"wH{i}", [P, KT, CW], F32R, offset=ring_base + (PARTS_SLOT + i) * 16 * KB) for i in range(2)]
    wL = [nc.alloc_sbuf_tensor_at(f"wL{i}", [P, KT, CW], F32R, offset=ring_base + ((PARTS_SLOT + i) * 16 + 8) * KB) for i in range(2)]
    mergedT = at("mergedT", [P, KT, SEQ], 48)
    o_tok = at("o_tok", [P, 4 * TT, P], 48)
    junk_a = at("junk_a", [P, P], 56)
    prob = at("prob", [P, 4, 512], 64)
    xn = at("xn", [P, 2, D], 48)
    scaledT = at("scaledT", [P, 2, KT, P], 56)
    roped = at("roped", [P, 2, CW], 64)
    raw = at("raw", [P, 512], 68)
    tmp = at("tmp", [P, 512], 70)
    pT = at("pT", [P, 2, 4, P], 72)
    junk = at("junk", [P, D], 72)
    foldc = at("foldc", [P, 2, TT, 2, 32], 72)
    folds = at("folds", [P, 2, TT, 2, 32], 74)
    iota = at("iota", [P, HALF], 76)
    hsT = at("hsT", [P, KT, SLOTS + CAP], 16)
    xnH = at("xnH", [P, TT, D], 52, F32R)
    xnL = at("xnL", [P, TT, D], 0, F32R)
    pick = at("pick", [P, TT, HALF], 68, F32R)
    gate_s = at("gate_s", [P, 2, 4, CAP], 52)
    hidH = at("hidH", [P, 2, 4, CAP], 55, F32R)
    hidL = at("hidL", [P, 2, 4, CAP], 58, F32R)
    ysb = at("ysb", [P, D], 61)
    dH = [at(f"dH{i}", [P, D], kb, F32R) for i, kb in enumerate((0, 4, 8))]
    dL = [at(f"dL{i}", [P, D], kb, F32R) for i, kb in enumerate((12, 66, 70))]
    gath = at("gath", [P, 2 * TT, D], 16)
    lg = at("lg", [P, TT, NG + NE], 16)
    em = at("em", [P, TT, NE], 17)
    cand = at("cand", [P, TT, NE], 17.5)
    sel1 = at("sel1", [P, TT, NE], 18)
    sel2 = at("sel2", [P, TT, NE], 18.5)
    gt = at("gt", [P, TT, NG], 19)
    gsel = at("gsel", [P, TT, NG], 19.25)
    first = sb("first", [P, NE])
    slotno = sb("slotno", [1, MAXOV])
    m1 = sb("m1", [P, TT])
    m2 = sb("m2", [P, TT])
    gp = sb("gp", [P, TT])
    ex = sb("ex", [P, TT])
    cnt = at("cnt", [P, NE], 51)
    incl = at("incl", [P, NE], 51.25)
    start = at("start", [P, NE], 51.5)
    ovc = at("ovc", [1, 4, NE], 68)
    ovr = at("ovr", [1, 6, MAXOV], 69)
    ovt = at("ovt", [1, 3, MAXOV, NE], 70)

    bank = [ctx.enter_context(nc.psum_tensor(f"bank{i}", [P, 512], F32)) for i in range(8)]
    ybuf = nc.dram_tensor("ybuf", [SLOTS + CAP, D], F32, kind="Internal").ap()

    consts_in = sem("consts_in")
    x_in = sem("x_in")
    mem_in = sem("mem_in")
    const_made = sem("const_made")
    mem_w_in = [sem(f"mem_w_in{i}") for i in range(2)]
    loaded = [sem(f"loaded{i}") for i in range(DRING)]
    high_done = sem("high_done")
    split_done = sem("split_done")
    exp_loaded = [sem(f"exp_loaded{i}") for i in range(RING)]
    ss_done = sem("ss_done")
    std_done = sem("std_done")
    xn_ready = sem("xn_ready")
    nt_done = sem("nt_done")
    nt_out = sem("nt_out")
    dv_done = sem("dv_done")
    dv_free = sem("dv_free")
    da_done = sem("da_done")
    da_free = sem("da_free")
    rope_ready = sem("rope_ready")
    tr_done = sem("tr_done")
    tr_out = sem("tr_out")
    hss_done = sem("hss_done")
    hstd_done = sem("hstd_done")
    s_done = sem("s_done")
    bias_ready = sem("bias_ready")
    exp_done = sem("exp_done")
    p_ready = sem("p_ready")
    pt_done = sem("pt_done")
    pt_out = sem("pt_out")
    pv_done = sem("pv_done")
    o_out = sem("o_out")
    sub_scaled = sem("sub_scaled")
    sub_turned = sem("sub_turned")
    sq_root = sem("sq_root")
    sub_out = sem("sub_out")
    gate_ready = sem("gate_ready")
    merged = sem("merged")
    lg_done = sem("lg_done")
    gd_ready = sem("gd_ready")
    gexp_done = sem("gexp_done")
    sel_ready = sem("sel_ready")
    rank_done = sem("rank_done")
    tab_ready = sem("tab_ready")
    starts_ready = sem("starts_ready")
    split_ready = sem("split_ready")
    pick_ready = sem("pick_ready")
    perm_done = sem("perm_done")
    perm_out = sem("perm_out")
    pad_done = sem("pad_done")
    gate_done = sem("gate_done")
    silu_done = sem("silu_done")
    up_done = sem("up_done")
    hid_done = sem("hid_done")
    hid_steps = sem("hid_steps")
    down_done = sem("down_done")
    down_high = sem("down_high")
    down_split = sem("down_split")
    y_out = sem("y_out")
    y_stored = sem("y_stored")
    ov = [{n: sem(f"ov_{n}{l}") for n in ("l0", "l1", "l2", "gate", "silu", "up", "hid", "steps", "high", "split", "down", "yout", "store", "over")}
          for l in range(DEPTH)]
    y_all = sem("y_all")
    gathered = [sem(f"gathered{i}") for i in range(2 * TT)]
    combined = sem("combined")
    fin = sem("fin")
    out_sem = sem("out_sem")
    vs = sem("vs")
    asm = sem("asm")
    lam_d = sem("lam_d")
    lam_e = sem("lam_e")
    fing_in = sem("fing_in")

    fing = at("fing", [P, D], 48)
    yfin = at("yfin", [P, 2, D], 52)

    block = ctx.enter_context(nc.Block())

    def wait(eng, s, n):
        if not isinstance(n, int) or n > 0:
            eng.wait_ge(s, n)

    def used(l, j, c=None):
        kind, n = used_after(l, j, c)
        return (dv_done if kind == "dv" else da_done), n

    def panel_free(l, j):
        if DENSE_PANELS[j][0] == "up":
            return used(l, j)
        return split_done, NC * l + sum(q <= j for q, _ in CHUNKS)

    def slot_free(l, s):
        if s == GATE_SLOT:
            return dv_free, PER_DV * l + UPS_DV[2]
        if s == LOW_SLOT:
            return used(l, ND - 1)
        if s >= PARTS_SLOT:
            return used(l, *CHUNKS[max(n for n in range(NC) if n % 2 == s - PARTS_SLOT)])
        return panel_free(l, max(j for j in range(ND) if j % DRING == s))

    def wide(t, c):
        return t[:, 0:KT * c].rearrange("p (k c) -> p k c", k=KT)

    @block.sync
    def _(sp):
        sp.dma_start(memx[:], a["mem"].rearrange("b (t p) d -> p (b t) d", p=P)).then_inc(mem_in, 16)
        for n in range(2):
            sp.dma_start(wide(ring[MEM_SLOTS[n]], 512), a["w_mem_kv"][:, n * 512:(n + 1) * 512].rearrange(
                "(k p) c -> p k c", p=P)).then_inc(mem_w_in[n], 16)
        sp.dma_start(xres[:], a["x"].rearrange("b (t p) d -> p (b t) d", p=P)).then_inc(x_in, 16)

        def dense_loads(l, js):
            for j in js:
                kind, c0, width = DENSE_PANELS[j][:3]
                s, _ = dense_slot(l, j)
                if j >= DRING:
                    sp.wait_ge(*panel_free(l, j - DRING))
                elif l:
                    sp.wait_ge(down_split, 4 * (NE * l - 1))
                if kind == "in":
                    dst, src = wide(ring[s], width), a["w_in"][l, :, c0:c0 + width].rearrange("(k p) c -> p k c", p=P)
                elif kind == "out":
                    dst, src = wide(ring[s], width), a["w_out"][l, :, c0:c0 + width].rearrange("(k p) c -> p k c", p=P)
                else:
                    w = (a["w_up_a"], a["w_up_b"], a["w_up_c"])[c0]
                    dst, src = ring[s][:].rearrange("p (k c) -> p k c", k=4), w[l].rearrange("(k p) c -> p k c", p=P)
                sp.dma_start(dst, src).then_inc(loaded[s], 16)

        dense_loads(0, range(DRING))
        for l in range(DEPTH):
            dense_loads(l, range(DRING, ND))

            def expert_loads(i):
                for b in range(2):
                    e = 2 * i + b
                    ei = slice(e, e + 1) if isinstance(e, int) else bass.ds(e, 1)
                    for k, w in enumerate((a["w_exp_gate"], a["w_exp_up"], a["w_exp_down"])):
                        s = EXPERT_SLOTS[b][k]
                        if isinstance(i, int):
                            sp.wait_ge(*slot_free(l, s))
                        else:
                            E = NE * l + e - 2
                            sp.wait_ge(*((gate_done, E + 1), (up_done, 2 * E + 2), (down_split, 4 * E + 4))[k])
                        sp.dma_start(ring[s][:].rearrange("p (k c) -> p k c", c=w.shape[3]),
                                     w[l, ei].rearrange("e (k p) c -> p (e k) c", p=P)).then_inc(exp_loaded[s], 16)
            expert_loads(0)
            with sp.Fori(1, NE // 2) as i:
                expert_loads(i)
            if l + 1 < DEPTH:
                dense_loads(l + 1, range(DRING))
            sp.wait_ge(up_done, 2 * NE * (l + 1))
            sp.wait_ge(tab_ready, l + 1)
            nov = sp.value_load(ovn[0:1, 0:1], min_val=0, max_val=MAXOV)
            with sp.If(nov > 0):
                with sp.Fori(0, nov) as i:
                    e = sp.value_load(ove[0:1, bass.ds(i, 1)], min_val=0, max_val=NE - 1)
                    for k, w in enumerate((a["w_exp_gate"], a["w_exp_up"], a["w_exp_down"])):
                        s = OVER_SLOTS[k]
                        o = ov[l]
                        sp.wait_ge(*((o["gate"], i + 1), (o["up"], 2 * i + 2), (o["down"], 4 * i + 4))[k])
                        sp.dma_start(ring[s][:].rearrange("p (k c) -> p k c", c=w.shape[3]),
                                     w[l, bass.ds(e, 1)].rearrange("e (k p) c -> p (e k) c", p=P)
                                     ).then_inc(ov[l][f"l{k}"], 16)
            sp.nop()
        for t in range(TT):
            sp.wait_ge(fin, t + 1)
            sp.dma_start(out[0, t * P:(t + 1) * P, :], yfin[:, t % 2, :]).then_inc(out_sem, 16)
            sp.wait_ge(out_sem, 16 * (t + 1))

    @block.gpsimd
    def _(pool):
        small = []

        def load(dst, src):
            small.append(pool.dma_start(dst, src, allow_slow_non_contiguous=True).then_inc(consts_in, 16))

        def col(v, n):
            return v.rearrange("(k p) -> p k", p=P)

        for l in range(DEPTH):
            load(gcols[:, 2 * l, :], col(a["norm1_g"][l], KT))
            load(gcols[:, 2 * l + 1, :], col(a["norm2_g"][l], KT))
            load(router_w[:, l, :, 0:NG], a["w_router_group"][l].rearrange("(k p) c -> p k c", p=P))
            load(router_w[:, l, :, NG:], a["w_router_expert"][l].rearrange("(k p) c -> p k c", p=P))
            load(router_b[:, l, 0:NG], a["b_router_group"][l:l + 1].broadcast_to([P, NG]))
            load(router_b[:, l, NG:], a["b_router_expert"][l:l + 1].broadcast_to([P, NE]))
            load(subg[:, l:l + 1], a["subln_g"][l:l + 1].rearrange("o p -> p o"))
            load(qg[:, l, 0], a["q_norm_g"][l:l + 1].broadcast_to([P, HD]))
            load(qg[:, l, 1], a["k_norm_g"][l:l + 1].broadcast_to([P, HD]))
            for n, name in enumerate(("lam_q1", "lam_k1", "lam_q2", "lam_k2")):
                load(lamv[:, 4 * l + n], a[name][l:l + 1].broadcast_to([P, HD]))
        load(gcols[:, 2 * DEPTH, :], col(a["mem_norm_g"], KT))
        load(cosA[:], a["cos_a"].rearrange("(t p) c -> p t c", p=P))
        load(sinA[:].rearrange("p t a c -> p t (a c)"), a["sin_a"].rearrange("(t p) c -> p t c", p=P))
        load(cosB[:], a["cos_b"].rearrange("(t p) c -> p t c", p=P))
        load(sinB[:].rearrange("p t a c -> p t (a c)"), a["sin_b"].rearrange("(t p) c -> p t c", p=P))
        load(laminit[:].rearrange("p l a -> p (l a)"), a["lam_init"].broadcast_to([P, 2 * DEPTH]))
        load(ident[:], a["ident"])
        load(upper[:], a["upper"])
        load(iota[:], a["iota"].broadcast_to([P, HALF]))
        load(first[:], a["first"].broadcast_to([P, NE]))
        load(slotno[:], a["iota"][:, 0:MAXOV])
        assert len(small) == NSMALL
        for l in range(DEPTH):
            if l:
                pool.wait_ge(ov[l - 1]["over"], 1)
            for n, (j, ch) in enumerate(CHUNKS):
                if n >= 2:
                    pool.wait_ge(*used(l, *CHUNKS[n - 2]))
                s, count = dense_slot(l, j)
                pool.wait_ge(loaded[s], 16 * count)
                w = wide(ring[s], DENSE_PANELS[j][2])[:, :, ch * CW:(ch + 1) * CW]
                pool.tensor_copy(wH[n % 2][:], w).then_inc(high_done, 1)
                pool.wait_ge(high_done, NC * l + n + 1)
                pool.tensor_tensor(wL[n % 2][:], w, wH[n % 2][:].bitcast(F32), ALU.subtract).then_inc(split_done, 1)
            pool.wait_ge(y_all, l + 1)
            for t in range(TT):
                for j in range(2):
                    pool.indirect_dma_start(
                        out=gath[:, 2 * t + j, :], out_offset=None, in_=ybuf[0:SLOTS, :],
                        in_offset=bass.IndirectOffsetOnAxis(ap=desti[:, j, t:t + 1], axis=0),
                    ).then_inc(gathered[2 * t + j], 16)
        pool.wait_ge(combined, DEPTH * TT)
        pool.dma_start(fing[:], a["final_norm_g"].rearrange("(o d) -> o d", o=1).broadcast_to([P, D])).then_inc(fing_in, 16)

    all_consts = 16 * NSMALL
    norm_tiles = {"mem": 0}
    for l in range(DEPTH):
        norm_tiles["n1", l] = 2 + 8 * l
        norm_tiles["n2", l] = 2 + 8 * l + 4
    norm_tiles["fin"] = 2 + 8 * DEPTH
    norm_no = {"mem": 1, "fin": 2 * DEPTH + 2} | {("n1", l): 2 + 2 * l for l in range(DEPTH)} | {("n2", l): 3 + 2 * l for l in range(DEPTH)}

    @block.tensor
    def _(pe):
        cnt_ = {"dv": 0, "da": 0, "tr": 0, "perm": 0, "chunk": 0}

        def chunk():
            n = cnt_["chunk"]
            cnt_["chunk"] += 1
            pe.wait_ge(split_done, n + 1)
            return wH[n % NC % 2], wL[n % NC % 2]

        def product(dst, lhs, rhs, k):
            (lH, lL), (rH, rL) = lhs, rhs
            pe.matmul(dst, lH, rH, start=(k == 0), stop=False)
            pe.matmul(dst, lH, rL, start=False, stop=False)
            return pe.matmul(dst, lL, rH, start=False, stop=(k == KT - 1))

        def dense(kind, lhs, rhs, n, cols):
            c = cnt_[kind]
            cnt_[kind] += 1
            done, free, b = (dv_done, dv_free, 0) if kind == "dv" else (da_done, da_free, 2)
            wait(pe, free, c - 1)
            for k in range(n):
                mm = pe.matmul(bank[b + c % 2][:, 0:cols], lhs(k), rhs(k), start=(k == 0), stop=(k == n - 1))
            return mm.then_inc(done, 1)

        def split_dense(kind, lhs, rhs, cols):
            c = cnt_[kind]
            cnt_[kind] += 1
            done, free, b = (dv_done, dv_free, 0) if kind == "dv" else (da_done, da_free, 2)
            wait(pe, free, c - 1)
            for k in range(KT):
                mm = product(bank[b + c % 2][:, 0:cols], lhs(k), rhs(k), k)
            mm.then_inc(done, 1)

        def norm_transposes(key, tiles):
            g0 = norm_tiles[key]
            for t in tiles:
                g = g0 + t
                pe.wait_ge(xn_ready, g + 1)
                wait(pe, nt_out, g - 1)
                for k in range(KT):
                    tr = pe.transpose(bank[4 + 2 * (g % 2) + k // 4][:, (k % 4) * P:(k % 4 + 1) * P],
                                      xn[:, g % 2, k * P:(k + 1) * P], ident[:])
                tr.then_inc(nt_done, 1)

        def head_transposes():
            r = cnt_["tr"]
            cnt_["tr"] += 1
            pe.wait_ge(rope_ready, r + 1)
            wait(pe, tr_out, r - 1)
            for k in range(2):
                tr = pe.transpose(bank[4 + r % 2][:, k * P:(k + 1) * P], roped[:, r % 2, k * P:(k + 1) * P], ident[:])
            tr.then_inc(tr_done, 1)

        def by_tokens(kind, chunks, between):
            for ch in range(chunks):
                H, L = chunk()
                for t in range(TT):
                    tok = slice(t * P, (t + 1) * P)
                    split_dense(kind, lambda k: (hH[:, k, tok], hL[:, k, tok]), lambda k: (H[:, k, :], L[:, k, :]), CW)
                    between(TT * ch + t)

        def by_features(groups):
            for f in range(groups):
                if f % 2 == 0:
                    H, L = chunk()
                cols = slice(f % 2 * P, (f % 2 + 1) * P)
                split_dense("da", lambda k: (H[:, k, cols], L[:, k, cols]), lambda k: (hH[:, k, :], hL[:, k, :]), 512)

        def attention(l, br):
            items = [l * NI + n for n in BRANCH_ITEMS[br]]
            wait(pe, dv_free, cnt_["dv"])
            pe.wait_ge(da_free, cnt_["da"])

            def scores(n):
                _, j, t = ITEMS[n % NI]
                tok = slice(t * P, (t + 1) * P)
                for m in range(2):
                    wait(pe, exp_done, 2 * n + m - 1)
                    b = bank[m]
                    if br < 2:
                        r = slice(m * HD, (m + 1) * HD)
                        kb = j if br == 0 else j // 2
                        mm = pe.matmul(b[:], qT[r, j, tok], kT[r, kb, :], start=True, stop=True)
                    else:
                        mm = pe.matmul(b[:, 0:MEM], av[:, 2 * j + m, tok], memkT[:, 2 * j + m, :], start=True, stop=True)
                    mm.then_inc(s_done, 1)

            def gate_part(q):
                for x in range(64 // len(items) * q, 64 // len(items) * (q + 1)):
                    f, k = x // KT, x % KT
                    if x % (2 * KT) == 0:
                        gate_w[0] = chunk()
                    if k == 0:
                        wait(pe, da_free, cnt_["da"] - 1)
                    H, L = (w[:, k, f % 2 * P:(f % 2 + 1) * P] for w in gate_w[0])
                    mm = product(bank[2 + cnt_["da"] % 2][:], (H, L), (hH[:, k, :], hL[:, k, :]), k)
                    if k == KT - 1:
                        mm.then_inc(da_done, 1)
                        cnt_["da"] += 1

            def turn(n):
                pe.wait_ge(p_ready, n + 1)
                wait(pe, pt_out, n)
                maps = 1 if br == 0 else 2
                nk = 4 if br < 2 else 2
                for m in range(maps):
                    for k in range(nk):
                        tr = pe.transpose(bank[4 + m][:, k * P:(k + 1) * P], prob[:, 2 * (n % 2) + m, k * P:(k + 1) * P], ident[:])
                tr.then_inc(pt_done, 1)

            def values(n):
                _, j, t = ITEMS[n % NI]
                pe.wait_ge(pt_out, n + 1)
                wait(pe, o_out, n - 1)
                b = bank[6 + n % 2]
                if br == 0:
                    for k in range(4):
                        mm = pe.matmul(b[:, 0:P], pT[:, 0, k, :], av[:, k, j * P:(j + 1) * P], start=(k == 0), stop=(k == 3))
                elif br == 1:
                    for m in range(2):
                        for k in range(4):
                            mm = pe.matmul(b[m * HD:(m + 1) * HD, 0:P], bv[:, k, (j // 2) * HD:(j // 2 + 1) * HD],
                                           pT[:, m, k, :], start=(k == 0), stop=(k == 3))
                else:
                    for m in range(2):
                        for k in range(2):
                            mm = pe.matmul(b[:, m * P:(m + 1) * P], memv[:, k, (2 * j + m) * P:(2 * j + m + 1) * P],
                                           pT[:, m, k, :], start=(k == 0), stop=(k == 1))
                mm.then_inc(pv_done, 1)

            gate_w = [None]
            for q, n in enumerate(items):
                scores(n)
                if q:
                    values(n - 1)
                gate_part(q)
                turn(n)
            values(items[-1])

        def ups(l, br):
            s, count = dense_slot(l, PANEL_AT[f"up{br}"])
            pe.wait_ge(loaded[s], 16 * count)
            up = ring[s][:].rearrange("p (k c) -> p k c", k=4)
            if br == 0:
                pe.wait_ge(sub_out, 4 * (l + 1))
            else:
                pe.wait_ge(o_out, l * NI + BRANCH_ITEMS[br][-1] + 1)
            for f in range(KT):
                dense("dv", lambda k: up[:, k, f * P:(f + 1) * P], lambda k: oT[:, k, :], 4, 512)

        pe.wait_ge(consts_in, all_consts)
        for l in range(DEPTH):
            pe.sem_inc(ov[l]["gate"], 1)
            pe.sem_inc(ov[l]["up"], 2)
            pe.sem_inc(ov[l]["down"], 4)
        norm_transposes("mem", range(2))
        pe.wait_ge(nt_out, 2)
        pe.wait_ge(mem_w_in[0], 16)
        w = wide(ring[MEM_SLOTS[0]], 512)
        for h in range(4):
            dense("da", lambda k: w[:, k, h * P:(h + 1) * P], lambda k: hT[:, k, 0:MEM], KT, MEM)
        pe.wait_ge(mem_w_in[1], 16)
        w = wide(ring[MEM_SLOTS[1]], 512)
        for t in range(2):
            dense("da", lambda k: hT[:, k, t * P:(t + 1) * P], lambda k: w[:, k, :], KT, 512)

        for l in range(DEPTH):
            n1 = norm_tiles["n1", l]
            norm_transposes(("n1", l), range(2))
            pe.wait_ge(nt_out, n1 + 1)

            def after_query(i):
                if i < 2:
                    norm_transposes(("n1", l), [i + 2])
                if i < 3:
                    pe.wait_ge(nt_out, n1 + i + 2)
                for _ in range((0, 0, 1, 2)[i] if i < 4 else 1):
                    head_transposes()
            by_tokens("dv", 2, after_query)
            by_tokens("dv", 2, lambda i: head_transposes())
            by_tokens("da", 2, lambda i: i or head_transposes())
            pe.wait_ge(tr_out, cnt_["tr"])
            attention(l, 0)
            for h in range(4):
                pe.wait_ge(sub_scaled, 4 * l + h + 1)
                for t in range(TT):
                    tr = pe.transpose(bank[4 + h][:, t * P:(t + 1) * P], o_tok[:, TT * h + t, :], ident[:])
                tr.then_inc(sub_turned, 1)
            ups(l, 0)
            by_tokens("dv", 2, lambda i: i and head_transposes())
            by_tokens("dv", 1, lambda i: head_transposes())
            head_transposes()
            pe.wait_ge(tr_out, cnt_["tr"])
            attention(l, 1)
            ups(l, 1)
            by_features(4)
            attention(l, 2)
            ups(l, 2)
            pe.wait_ge(merged, KT * (l + 1))
            by_tokens("dv", 4, lambda i: None)
            norm_transposes(("n2", l), range(TT))
            pe.wait_ge(nt_out, norm_tiles["n2", l] + TT)
            for t in range(TT):
                for k in range(KT):
                    mm = pe.matmul(bank[0][:, t * 36:(t + 1) * 36], hT[:, k, t * P:(t + 1) * P],
                                   router_w[:, l, k, :], start=(k == 0), stop=(k == KT - 1))
            mm.then_inc(lg_done, 1)
            pe.wait_ge(sel_ready, l + 1)
            for t in range(TT):
                for u in range(t + 1):
                    mm = pe.matmul(bank[1][:, t * NE:(t + 1) * NE], upper[:] if u == t else ones[:], cand[:, u, :],
                                   start=(u == 0), stop=(u == t))
            for u in range(TT):
                mm = pe.matmul(bank[1][:, TT * NE:(TT + 1) * NE], ones[:], cand[:, u, :], start=(u == 0), stop=(u == TT - 1))
            mm.then_inc(rank_done, 1)
            pe.wait_ge(split_ready, l + 1)
            for hf in range(2):
                pe.wait_ge(pick_ready, 2 * l + hf + 1)
                for k in range(KT):
                    g = cnt_["perm"]
                    cnt_["perm"] += 1
                    wait(pe, perm_out, g - 3)
                    for t in range(TT):
                        for part in (xnH, xnL):
                            mm = pe.matmul(bank[4 + g % 4][:], part[:, t, k * P:(k + 1) * P], pick[:, t, :],
                                           start=(t == 0 and part is xnH), stop=(t == TT - 1 and part is xnL))
                    mm.then_inc(perm_done, 1)
            pe.wait_ge(perm_out, cnt_["perm"])
            pe.wait_ge(pad_done, l + 1)
            pe.wait_ge(starts_ready, l + 1)

            def expert(i, b):
                E = NE * l + b + 2 * i
                panels = EXPERT_SLOTS[b]
                s0 = pe.value_load(sidx[0:1, bass.ds(2 * i + b, 1)] if not isinstance(i, int) else sidx[0:1, b:b + 1],
                                   min_val=0, max_val=SLOTS)
                wg, wu = (ring[s] for s in panels[:2])
                one_expert(s0, wg, wu, b, [(exp_loaded[s], 16 * (NE // 2 * l + i + 1)) for s in panels[:2]],
                           silu_free=(silu_done, E - 1), hid_free=(hid_done, 2 * (E - 1)), hid_at=(hid_done, 2 * E),
                           y_free=(y_out, 2 * E), split_at=(down_split, 4 * E), done=(gate_done, up_done, down_done))

            def one_expert(s0, wg, wu, b, arrive, silu_free, hid_free, hid_at, y_free, split_at, done):
                wgv, wuv = wide(wg, 512), wide(wu, 512)
                pe.wait_ge(*arrive[0])
                wait(pe, *silu_free)
                for f in range(4):
                    for k in range(KT):
                        mm = pe.matmul(bank[b][:, f * CAP:(f + 1) * CAP], wgv[:, k, f * P:(f + 1) * P],
                                       hsT[:, k, bass.ds(s0, CAP)], start=(k == 0), stop=(k == KT - 1))
                mm.then_inc(done[0], 1)
                pe.wait_ge(*arrive[1])
                wait(pe, *hid_free)
                for f in range(4):
                    for k in range(KT):
                        mm = pe.matmul(bank[2 + 4 * b + f // 2][:, f % 2 * CAP:(f % 2 + 1) * CAP], wuv[:, k, f * P:(f + 1) * P],
                                       hsT[:, k, bass.ds(s0, CAP)], start=(k == 0), stop=(k == KT - 1))
                    if f % 2:
                        mm.then_inc(done[1], 1)
                wait(pe, *y_free)
                for f in range(4):
                    if f % 2 == 0:
                        pe.wait_ge(hid_at[0], hid_at[1] + f // 2 + 1)
                    pe.wait_ge(split_at[0], split_at[1] + f + 1)
                    H, L = dH[f % 3], dL[f % 3]
                    for h in range(2):
                        y, cols = bank[4 + h][0:CAP, :], slice(h * 512, (h + 1) * 512)
                        pe.matmul(y, hidH[:, b, f, :], H[:, cols], start=(f == 0), stop=False)
                        pe.matmul(y, hidH[:, b, f, :], L[:, cols], start=False, stop=False)
                        mm = pe.matmul(y, hidL[:, b, f, :], H[:, cols], start=False, stop=(f == 3))
                    mm.then_inc(done[2], 1)

            for b in range(2):
                expert(0, b)
            with pe.Fori(1, NE // 2) as i:
                for b in range(2):
                    expert(i, b)
            o = ov[l]
            pe.wait_ge(tab_ready, l + 1)
            nov = pe.value_load(ovn[0:1, 0:1], min_val=0, max_val=MAXOV)
            with pe.If(nov > 0):
                with pe.Fori(0, nov) as i:
                    s0 = pe.value_load(ovs[0:1, bass.ds(i, 1)], min_val=0, max_val=SLOTS)
                    one_expert(s0, *(ring[slot] for slot in OVER_SLOTS[:2]), 0, [(o[f"l{k}"], 16 * i + 16) for k in range(2)],
                               silu_free=(silu_done, NE * (l + 1)), hid_free=(o["hid"], 2 * i + 2), hid_at=(o["hid"], 2 * i + 2),
                               y_free=(o["yout"], 2 * i + 2), split_at=(o["split"], 4 * i), done=(o["gate"], o["up"], o["down"]))
                    pe.wait_ge(o["down"], 4 * i + 8)
            pe.wait_ge(down_done, 4 * NE * (l + 1))
            pe.sem_inc(o["over"], 1)

    @block.scalar
    def _(act):
        c = {"da": 0, "tr": 0}
        made = {}

        def own(s):
            made[s.name] = made.get(s.name, 0) + 1
            act.wait_ge(s, made[s.name])

        def squares(key, nt, src, ready):
            g0 = norm_tiles[key]
            for t in range(nt):
                ready(t)
                act.activation(junk[:], src(t), ACT.Square, accum_out=ss[:, t:t + 1]).then_inc(ss_done, 1)
                own(ss_done)
                act.wait_ge(ss_done, g0 + t + 1)
            act.activation(std[:, 0:nt], ss[:, 0:nt], ACT.Sqrt, scale=1.0 / D, bias=eps[:, 0:1]).then_inc(std_done, 1)
            own(std_done)

        def dense_out(dst, cols):
            n = c["da"]
            c["da"] += 1
            act.wait_ge(da_done, n + 1)
            act.activation(dst, bank[2 + n % 2][:, 0:cols], ACT.Copy).then_inc(da_free, 1)
            own(da_free)

        def heads_out(dst, tok):
            n = c["tr"]
            c["tr"] += 1
            act.wait_ge(tr_done, n + 1)
            act.activation(dst[:, :, tok], bank[4 + n % 2][:, 0:2 * P].rearrange("p (b t) -> p b t", b=2),
                           ACT.Copy).then_inc(tr_out, 1)
            own(tr_out)

        act.wait_ge(const_made, 2)
        act.wait_ge(mem_in, 16)
        squares("mem", 2, lambda t: memx[:, t, :], lambda t: None)
        act.wait_ge(lam_d, DEPTH)
        act.activation(lamd[:], lamd[:], ACT.Exp).then_inc(lam_e, 1)
        own(lam_e)
        for h in range(4):
            dense_out(memkT[:, h, :], MEM)
        for t in range(2):
            dense_out(memv[:, t, :], 512)

        def attention(l, br):
            maps_t = 1 if br == 0 else 2
            nk = 4 if br < 2 else 2
            cols = 512 if br < 2 else MEM
            scale = HD ** -0.5 if br < 2 else P ** -0.5
            items = [l * NI + n for n in BRANCH_ITEMS[br]]

            def exps(n):
                for m in range(2):
                    act.wait_ge(bias_ready, 2 * n + m + 1)
                    wait(act, pt_done, n - 1)
                    act.activation(prob[:, 2 * (n % 2) + m, 0:cols], bank[m][:, 0:cols], ACT.Exp,
                                   bias=nbias[:, 2 * (n % 2) + m:2 * (n % 2) + m + 1], scale=scale,
                                   accum_out=rowsum[:, 2 * (n % 2) + m:2 * (n % 2) + m + 1]).then_inc(exp_done, 1)
                    own(exp_done)

            def turned(n):
                act.wait_ge(pt_done, n + 1)
                wait(act, pv_done, n)
                for m in range(maps_t):
                    ins = act.activation(pT[:, m, 0:nk, :], bank[4 + m][:, 0:nk * P].rearrange("p (k t) -> p k t", k=nk), ACT.Copy)
                ins.then_inc(pt_out, 1)
                own(pt_out)

            def outputs(n):
                _, j, t = ITEMS[n % NI]
                tok = slice(t * P, (t + 1) * P)
                act.wait_ge(pv_done, n + 1)
                b = bank[6 + n % 2]
                if br == 0:
                    i = n % NI
                    act.activation(junk_a[:], b[:, 0:P], ACT.Square, accum_out=hsq[:, i:i + 1])
                    ins = act.activation(o_tok[:, i, :], b[:, 0:P], ACT.Copy)
                elif br == 1:
                    ins = act.activation(oT[:, j, tok], b[:, 0:P], ACT.Copy)
                else:
                    ins = act.activation(oT[:, 2 * j:2 * j + 2, tok], b[:, 0:2 * P].rearrange("p (m t) -> p m t", m=2), ACT.Copy)
                ins.then_inc(o_out, 1)
                own(o_out)

            def gate_out(f):
                g = c["da"]
                c["da"] += 1
                act.wait_ge(da_done, g + 1)
                if f == 0:
                    wait(act, dv_free, PER_DV * l + UPS_DV[br - 1] if br else 0)
                act.activation(gates_s[:, f, :], bank[2 + g % 2][:], ACT.Copy).then_inc(da_free, 1)
                own(da_free)

            per = len(items) // KT
            for q, n in enumerate(items):
                exps(n)
                if q:
                    outputs(n - 1)
                turned(n)
                if q % per == per - 1:
                    gate_out(q // per)
            outputs(items[-1])

        def sigmoids():
            for f in range(KT):
                act.activation(gates_s[:, f, :], gates_s[:, f, :], ACT.Sigmoid).then_inc(gate_ready, 1)
                own(gate_ready)

        for l in range(DEPTH):
            squares(("n1", l), TT, lambda t: xres[:, t, :],
                    (lambda t: act.wait_ge(x_in, 16)) if l == 0 else (lambda t: act.wait_ge(combined, (l - 1) * TT + t + 1)))
            def turned_tile(i):
                h = i // TT % 2 * 2
                heads_out((qT if i < 2 * TT else kT)[:, h:h + 2], slice(i % TT * P, (i % TT + 1) * P))

            for i in range(4 * TT - 1):
                turned_tile(i)
            for i in range(2 * TT):
                dense_out(av[:, i % TT, i // TT * CW:(i // TT + 1) * CW], CW)
                if i == 0:
                    turned_tile(4 * TT - 1)
            attention(l, 0)
            act.activation(hsq[:], hsq[:], ACT.Sqrt, scale=1.0 / P, bias=eps[:, 0:1]).then_inc(sq_root, 1)
            own(sq_root)
            for h in range(4):
                act.wait_ge(sub_turned, 4 * l + h + 1)
                act.activation(oT[:, h, :], bank[4 + h][:], ACT.Copy, scale=subg[:, l:l + 1]).then_inc(sub_out, 1)
                own(sub_out)
            sigmoids()
            for i in range(3 * TT):
                act.wait_ge(hss_done, 3 * TT * l + i + 1)
                nh = 4 if i < 2 * TT else 2
                act.activation(hstd[:, 0:nh], hss[:, 0:nh], ACT.Sqrt, scale=1.0 / HD, bias=eps[:, 0:1]).then_inc(hstd_done, 1)
                own(hstd_done)
                if i:
                    turned_tile(i - 1)
            turned_tile(3 * TT - 1)
            attention(l, 1)
            sigmoids()
            for h in range(4):
                dense_out(av[:, h, :], 512)
            attention(l, 2)
            sigmoids()
            squares(("n2", l), TT, lambda t: xres[:, t, :], lambda t: act.wait_ge(dv_free, PER_DV * (l + 1) - TT + t + 1))
            act.wait_ge(gd_ready, 2 * l + 1)
            act.activation(gt[:], gt[:], ACT.Exp).then_inc(gexp_done, 1)
            own(gexp_done)
            act.wait_ge(gd_ready, 2 * l + 2)
            act.activation(ex[:], m2[:], ACT.Exp).then_inc(gexp_done, 1)
            own(gexp_done)
            for hf in range(2):
                for k in range(KT):
                    g = 16 * l + 8 * hf + k
                    act.wait_ge(perm_done, g + 1)
                    act.activation(hsT[:, k, hf * HALF:(hf + 1) * HALF], bank[4 + g % 4][:], ACT.Copy,
                                   scale=gcols[:, 2 * l + 1, k:k + 1]).then_inc(perm_out, 1)
                    own(perm_out)
            act.wait_ge(starts_ready, l + 1)

            def window(b, s0, down_w, arrive, gate_at, hid_at, down_at, high, silu, y, store):
                wd = down_w[:].rearrange("p (k c) -> p k c", k=4)

                def high_part(f):
                    wait(act, down_at[0], down_at[1] + (0, -2, -1, 1)[f])
                    act.activation(dH[f % 3][:], wd[:, f, :], ACT.Copy).then_inc(high, 1)

                act.wait_ge(*arrive)
                for f in range(3):
                    high_part(f)
                act.wait_ge(*gate_at)
                wait(act, *hid_at)
                act.activation(gate_s[:, b], bank[b][:, 0:4 * CAP].rearrange("p (f c) -> p f c", f=4), ACT.Silu).then_inc(silu, 1)
                high_part(3)
                act.wait_ge(down_at[0], down_at[1] + 4)
                wait(act, *store)
                for h in range(2):
                    act.activation(ysb[0:CAP, h * 512:(h + 1) * 512], bank[4 + h][0:CAP, :], ACT.Copy).then_inc(y[0], 1)
                act.wait_ge(y[0], y[1] + 2)
                act.dma_start(ybuf[bass.ds(s0, CAP), :], ysb[0:CAP, :]).then_inc(store[0], 16)

            def expert(i, b):
                E = NE * l + 2 * i + b
                s0 = act.value_load(sidx[0:1, bass.ds(2 * i + b, 1)] if not isinstance(i, int) else sidx[0:1, b:b + 1],
                                    min_val=0, max_val=SLOTS)
                slot = EXPERT_SLOTS[b][2]
                window(b, s0, ring[slot], (exp_loaded[slot], 16 * (NE // 2 * l + i + 1)), (gate_done, E + 1),
                       (hid_done, 2 * (E - 1)), (down_done, 4 * E), down_high, silu_done, (y_out, 2 * E), (y_stored, 16 * E))

            for b in range(2):
                expert(0, b)
            with act.Fori(1, NE // 2) as i:
                for b in range(2):
                    expert(i, b)
            act.wait_ge(y_stored, 16 * NE * (l + 1))
            act.wait_ge(tab_ready, l + 1)
            o = ov[l]
            act.sem_inc(o["yout"], 2)
            nov = act.value_load(ovn[0:1, 0:1], min_val=0, max_val=MAXOV)
            with act.If(nov > 0):
                with act.Fori(0, nov) as i:
                    s0 = act.value_load(ovs[0:1, bass.ds(i, 1)], min_val=0, max_val=SLOTS)
                    window(0, s0, ring[OVER_SLOTS[2]], (o["l2"], 16 * i + 16), (o["gate"], i + 2), (o["hid"], 2 * i + 2),
                           (o["down"], 4 * i + 4), o["high"], o["silu"], (o["yout"], 2 * i + 2), (o["store"], 0))
                    act.wait_ge(o["store"], 16 * i + 16)
            act.sem_inc(y_all, 1)
        squares("fin", TT, lambda t: xres[:, t, :], lambda t: act.wait_ge(combined, (DEPTH - 1) * TT + t + 1))

    @block.vector
    def _(dve):
        c = {"dv": 0, "vs": 0, "rope": 0}
        made = {}

        def own(s):
            made[s.name] = made.get(s.name, 0) + 1
            dve.wait_ge(s, made[s.name])

        def v(ins):
            c["vs"] += 1
            ins.then_inc(vs, 1)
            dve.wait_ge(vs, c["vs"])

        def norm(key, nt, src, gcol, dst, between=lambda t: None):
            g0 = norm_tiles[key]
            dve.wait_ge(std_done, norm_no[key])
            v(dve.reciprocal(rstd[:, 0:nt], std[:, 0:nt]))

            def normalise(t):
                g = g0 + t
                wait(dve, nt_done, g - 1)
                dve.tensor_scalar(xn[:, g % 2, :], src(t), rstd[:, t:t + 1], None, ALU.mult).then_inc(xn_ready, 1)
                own(xn_ready)

            def columns(t):
                g = g0 + t
                dve.wait_ge(nt_done, g + 1)
                for h in range(2):
                    ins = dve.tensor_tensor(dst[:, 4 * h:4 * h + 4, t * P:(t + 1) * P],
                                            bank[4 + 2 * (g % 2) + h][:].rearrange("p (k t) -> p k t", k=4),
                                            gcol[:, 4 * h:4 * h + 4].unsqueeze(2).broadcast_to([P, 4, P]), ALU.mult)
                ins.then_inc(nt_out, 1)
                own(nt_out)

            def split_columns(t):
                g = g0 + t
                tok = slice(t * P, (t + 1) * P)
                dve.wait_ge(nt_done, g + 1)
                for h in range(2):
                    ins = dve.tensor_tensor(scaledT[:, g % 2, 4 * h:4 * h + 4, :],
                                            bank[4 + 2 * (g % 2) + h][:].rearrange("p (k t) -> p k t", k=4),
                                            gcol[:, 4 * h:4 * h + 4].unsqueeze(2).broadcast_to([P, 4, P]), ALU.mult)
                v(ins)
                v(dve.tensor_copy(hH[:, :, tok], scaledT[:, g % 2]))
                dve.tensor_tensor(hL[:, :, tok], scaledT[:, g % 2], hH[:, :, tok].bitcast(F32),
                                  ALU.subtract).then_inc(nt_out, 1)
                own(nt_out)
            normalise(0)
            for t in range(nt):
                if t + 1 < nt:
                    normalise(t + 1)
                if dst is None:
                    split_columns(t)
                else:
                    columns(t)
                if t >= 2:
                    between(t - 2)

        def take_dense():
            n = c["dv"]
            c["dv"] += 1
            dve.wait_ge(dv_done, n + 1)
            return bank[n % 2]

        def rotate(x, cos, sin, nh, dst, free):
            xv = x.rearrange("p (h a c) -> p h a c", a=2, c=32)
            dv = dst.rearrange("p (h a c) -> p h a c", a=2, c=32)
            tv = tmp[:, 0:nh * HD].rearrange("p (h a c) -> p h a c", a=2, c=32)
            dve.tensor_tensor(dv, xv, cos, ALU.mult)
            dve.tensor_tensor(tv[:, :, 0], xv[:, :, 1], sin[:, 0].unsqueeze(1).broadcast_to([P, nh, 32]), ALU.mult)
            ins = dve.tensor_tensor(tv[:, :, 1], xv[:, :, 0], sin[:, 1].unsqueeze(1).broadcast_to([P, nh, 32]), ALU.mult)
            if free:
                ins.then_inc(dv_free, 1)
                own(dv_free)
            else:
                v(ins)
            return dve.tensor_tensor(dst, dst, tmp[:, 0:nh * HD], ALU.add)

        dve.memset(ones[:], 1.0).then_inc(const_made, 1)
        own(const_made)
        dve.memset(eps[:], EPS).then_inc(const_made, 1)
        own(const_made)
        dve.wait_ge(consts_in, all_consts)
        dve.wait_ge(const_made, 2)
        dve.wait_ge(mem_in, 16)
        for l in range(DEPTH):
            lv = lamv[:, 4 * l:4 * l + 4, :].rearrange("p (a b) c -> p a b c", b=2)
            v(dve.tensor_tensor(lv[:, :, 0], lv[:, :, 0], lv[:, :, 1], ALU.mult))
            dve.tensor_reduce(lamd[:, 2 * l:2 * l + 2], lv[:, :, 0], AX.X, ALU.add).then_inc(lam_d, 1)
            own(lam_d)
        dve.wait_ge(lam_e, 1)
        for l in range(DEPTH):
            v(dve.tensor_tensor(lam[:, l:l + 1], lamd[:, 2 * l:2 * l + 1], lamd[:, 2 * l + 1:2 * l + 2], ALU.subtract))
            v(dve.tensor_tensor(lam[:, l:l + 1], lam[:, l:l + 1], laminit[:, l, 0:1], ALU.add))
            v(dve.tensor_tensor(subg[:, l:l + 1], subg[:, l:l + 1], laminit[:, l, 1:2], ALU.mult))
        norm("mem", 2, lambda t: memx[:, t, :], gcols[:, 2 * DEPTH, :], hT)

        def attention(l, br):
            cols = 512 if br < 2 else MEM
            scale = HD ** -0.5 if br < 2 else P ** -0.5
            items = [l * NI + n for n in BRANCH_ITEMS[br]]

            def maxima(n):
                for m in range(2):
                    q = 2 * (n % 2) + m
                    dve.wait_ge(s_done, 2 * n + m + 1)
                    wait(dve, exp_done, 2 * n + m - 3)
                    v(dve.tensor_reduce(mx[:, q:q + 1], bank[m][:, 0:cols], AX.X, ALU.max))
                    dve.tensor_scalar(nbias[:, q:q + 1], mx[:, q:q + 1], -scale, None, ALU.mult).then_inc(bias_ready, 1)
                    own(bias_ready)

            def normalise(n):
                q = 2 * (n % 2)
                dve.wait_ge(exp_done, 2 * n + 2)
                v(dve.reciprocal(rsum[:, q:q + 2], rowsum[:, q:q + 2]))
                p0, p1 = prob[:, q, 0:cols], prob[:, q + 1, 0:cols]
                if br == 0:
                    v(dve.tensor_scalar(p1, p1, rsum[:, q + 1:q + 2], lam[:, l:l + 1], ALU.mult, ALU.mult))
                    ins = dve.scalar_tensor_tensor(out=p0, in0=p0, scalar=rsum[:, q:q + 1], in1=p1, op0=ALU.mult, op1=ALU.subtract)
                else:
                    dve.tensor_scalar(p0, p0, rsum[:, q:q + 1], None, ALU.mult)
                    ins = dve.tensor_scalar(p1, p1, rsum[:, q + 1:q + 2], None, ALU.mult)
                ins.then_inc(p_ready, 1)
                own(p_ready)

            for n in items:
                maxima(n)
                normalise(n)

        def gates(l, br):
            for f in range(KT):
                b = take_dense()
                dve.wait_ge(gate_ready, 24 * l + 8 * br + f + 1)
                to = mergedT[:, f, :] if br == 0 else tmp[:]
                mf = mergedT[:, f, :]
                dve.tensor_tensor(to, gates_s[:, f, :], b[:], ALU.mult).then_inc(dv_free, 1)
                own(dv_free)
                if br:
                    v(dve.tensor_tensor(mf, mf, tmp[:], ALU.add))
                if br == 2:
                    v(dve.tensor_copy(hH[:, f, :], mf))
                    dve.tensor_tensor(hL[:, f, :], mf, hH[:, f, :].bitcast(F32), ALU.subtract).then_inc(merged, 1)
                    own(merged)

        for l in range(DEPTH):
            def rope_a(i):
                t = i % TT
                b = take_dense()
                r = c["rope"]
                c["rope"] += 1
                wait(dve, tr_done, r - 1)
                rotate(b[:, 0:CW], cosA[:, t].unsqueeze(1).unsqueeze(1).broadcast_to([P, 4, 2, 32]), sinA[:, t], 4,
                       roped[:, r % 2, :], True).then_inc(rope_ready, 1)
                own(rope_ready)
            norm(("n1", l), TT, lambda t: xres[:, t, :], gcols[:, 2 * l, :], None, rope_a)
            for i in range(2, 4 * TT):
                rope_a(i)
            attention(l, 0)
            dve.wait_ge(sq_root, l + 1)
            v(dve.reciprocal(hsq[:], hsq[:]))
            for h in range(4):
                oh = o_tok[:, TT * h:TT * h + TT, :]
                dve.tensor_tensor(oh, oh, hsq[:, TT * h:TT * h + TT].unsqueeze(2).broadcast_to([P, TT, P]),
                                  ALU.mult).then_inc(sub_scaled, 1)
                own(sub_scaled)
            gates(l, 0)
            for m in range(2):
                for t in range(TT):
                    g2 = qg[:, l, m].rearrange("p (a c) -> p a c", a=2)
                    dve.tensor_tensor(foldc[:, m, t], g2, cosB[:, t].unsqueeze(1).broadcast_to([P, 2, 32]), ALU.mult)
                    dve.tensor_tensor(folds[:, m, t, 0], g2[:, 1], sinB[:, t, 0], ALU.mult)
                    last = dve.tensor_tensor(folds[:, m, t, 1], g2[:, 0], sinB[:, t, 1], ALU.mult)
            v(last)
            for i in range(3 * TT):
                t, m = i % TT, i // (2 * TT)
                nh = 4 if m == 0 else 2
                w = nh * HD
                b = take_dense()
                r = c["rope"]
                c["rope"] += 1
                if m:
                    dve.tensor_copy(bv[:, t, :], b[:, w:2 * w])
                dve.tensor_copy(raw[:, 0:w], b[:, 0:w]).then_inc(dv_free, 1)
                own(dv_free)
                v(dve.tensor_tensor(tmp[:, 0:w], raw[:, 0:w], raw[:, 0:w], ALU.mult))
                dve.tensor_reduce(hss[:, 0:nh], tmp[:, 0:w].rearrange("p (h c) -> p h c", c=HD), AX.X, ALU.add).then_inc(hss_done, 1)
                own(hss_done)
                dve.wait_ge(hstd_done, 3 * TT * l + i + 1)
                v(dve.reciprocal(hr[:, 0:nh], hstd[:, 0:nh]))
                rv = raw[:, 0:w].rearrange("p (h c) -> p h c", c=HD)
                v(dve.tensor_tensor(rv, rv, hr[:, 0:nh].unsqueeze(2).broadcast_to([P, nh, HD]), ALU.mult))
                wait(dve, tr_done, r - 1)
                fc = foldc[:, m, t].unsqueeze(1).broadcast_to([P, nh, 2, 32])
                if m == 0:
                    rotate(raw[:, 0:w], fc, folds[:, m, t], nh, roped[:, r % 2, :], False).then_inc(rope_ready, 1)
                    own(rope_ready)
                else:
                    v(rotate(raw[:, 0:w], fc, folds[:, m, t], nh, raw[:, 256:256 + w], False))
                    dve.tensor_copy(roped[:, r % 2, :].rearrange("p (h a c) -> p h a c", a=2, c=HD),
                                    raw[:, 256:384].rearrange("p (h c) -> p h c", c=HD).unsqueeze(2).broadcast_to(
                                        [P, 2, 2, HD])).then_inc(rope_ready, 1)
                    own(rope_ready)
            attention(l, 1)
            gates(l, 1)
            attention(l, 2)
            gates(l, 2)
            for i in range(4 * TT):
                n, t = i // TT, i % TT
                b = take_dense()
                xs = xres[:, t, n * CW:(n + 1) * CW]
                dve.tensor_tensor(xs, xs, b[:, 0:CW], ALU.add).then_inc(dv_free, 1)
                own(dv_free)
            norm(("n2", l), TT, lambda t: xres[:, t, :], gcols[:, 2 * l + 1, :], hT)
            dve.memset(hsT[:, :, SLOTS:], 0.0).then_inc(pad_done, 1)
            own(pad_done)

            dve.wait_ge(lg_done, l + 1)
            v(dve.tensor_tensor(lg[:], bank[0][:, 0:TT * 36].rearrange("p (t c) -> p t c", t=TT),
                                router_b[:, l, :].unsqueeze(1).broadcast_to([P, TT, 36]), ALU.add))

            def argmax(vals, width, m, sel, cnd):
                v(dve.tensor_reduce(m, vals, AX.X, ALU.max))
                v(dve.tensor_tensor(cnd, vals, m.unsqueeze(2).broadcast_to([P, TT, width]), ALU.is_equal))
                v(dve.tensor_tensor(cnd, cnd, first[:, 0:width].unsqueeze(1).broadcast_to([P, TT, width]), ALU.mult))
                v(dve.tensor_reduce(ex[:], cnd, AX.X, ALU.max))
                v(dve.tensor_tensor(sel, cnd, ex[:].unsqueeze(2).broadcast_to([P, TT, width]), ALU.is_equal))

            lgg = lg[:, :, 0:NG]
            argmax(lgg, NG, m1[:], gsel[:], gt[:])
            dve.tensor_tensor(gt[:], lgg, m1[:].unsqueeze(2).broadcast_to([P, TT, NG]), ALU.subtract).then_inc(gd_ready, 1)
            own(gd_ready)
            v(dve.tensor_scalar(gsel[:], gsel[:], 1.0, 1e30, ALU.subtract, ALU.mult))
            v(dve.tensor_tensor(em[:].rearrange("p t (g e) -> p t g e", g=NG),
                                lg[:, :, NG:].rearrange("p t (g e) -> p t g e", g=NG),
                                gsel[:].unsqueeze(3).broadcast_to([P, TT, NG, EPG]), ALU.add))
            argmax(em[:], NE, m1[:], sel1[:], cand[:])
            v(dve.tensor_scalar(cand[:], sel1[:], -3e38, None, ALU.mult))
            v(dve.tensor_tensor(em[:], em[:], cand[:], ALU.add))
            argmax(em[:], NE, m2[:], sel2[:], cand[:])
            dve.tensor_tensor(cand[:], sel1[:], sel2[:], ALU.add).then_inc(sel_ready, 1)
            own(sel_ready)
            dve.wait_ge(gexp_done, 2 * l + 1)
            dve.tensor_tensor(m2[:], m2[:], m1[:], ALU.subtract).then_inc(gd_ready, 1)
            own(gd_ready)
            v(dve.tensor_reduce(gp[:], gt[:], AX.X, ALU.add))
            v(dve.reciprocal(gp[:], gp[:]))
            dve.wait_ge(gexp_done, 2 * l + 2)
            v(dve.tensor_scalar(m1[:], ex[:], 1.0, None, ALU.add))
            v(dve.reciprocal(m1[:], m1[:]))
            v(dve.tensor_tensor(wts[:, 0], gp[:], m1[:], ALU.mult))
            v(dve.tensor_tensor(wts[:, 1], wts[:, 0], ex[:], ALU.mult))
            for t in range(TT):
                v(dve.tensor_scalar(xnH[:, t, :], xres[:, t, :], rstd[:, t:t + 1], None, ALU.mult))
                ins = dve.scalar_tensor_tensor(out=xnL[:, t, :], in0=xres[:, t, :], scalar=rstd[:, t:t + 1],
                                               in1=xnH[:, t, :].bitcast(F32), op0=ALU.mult, op1=ALU.subtract)
            ins.then_inc(split_ready, 1)
            own(split_ready)
            dve.wait_ge(rank_done, l + 1)
            v(dve.tensor_copy(cnt[:], bank[1][:, TT * NE:(TT + 1) * NE]))
            v(dve.tensor_tensor_scan(incl[:], ones[:, 0:NE], cnt[:], 0.0, ALU.mult, ALU.add))
            v(dve.tensor_tensor(start[:], incl[:], cnt[:], ALU.subtract))
            v(dve.tensor_tensor(em[:], bank[1][:, 0:TT * NE].rearrange("p (t e) -> p t e", t=TT),
                                start[:].unsqueeze(1).broadcast_to([P, TT, NE]), ALU.add))
            for j, s in enumerate((sel1, sel2)):
                v(dve.tensor_tensor(s[:], s[:], em[:], ALU.mult))
                v(dve.tensor_reduce(destf[:, j], s[:], AX.X, ALU.add))
            dve.tensor_copy(desti[:], destf[:])
            v(dve.tensor_copy(sidx[:], start[0:1]))
            dve.sem_inc(starts_ready, 1)
            for hf in range(2):
                v(dve.tensor_scalar(desth[:], destf[:], float(-hf * HALF), None, ALU.add))
                if hf:
                    dve.wait_ge(perm_done, 16 * l + 8)
                for t in range(TT):
                    v(dve.tensor_scalar(pick[:, t, :], iota[:], desth[:, 0, t:t + 1], None, ALU.is_equal))
                    ins = dve.scalar_tensor_tensor(out=pick[:, t, :], in0=iota[:], scalar=desth[:, 1, t:t + 1],
                                                   in1=pick[:, t, :].bitcast(F32),
                                                   op0=ALU.is_equal, op1=ALU.add)
                    if t == TT - 1:
                        ins.then_inc(pick_ready, 1)
                        own(pick_ready)
                    else:
                        v(ins)
            dve.wait_ge(perm_done, 16 * (l + 1))
            c0, s0, e0 = cnt[0:1], start[0:1], incl[0:1]
            n_ov, cum, exc, t_ = (ovc[:, q] for q in range(4))
            v(dve.tensor_scalar(n_ov, c0, float(CAP), None, ALU.is_gt))
            for q in range(2, SEQ // CAP + 1):
                v(dve.tensor_scalar(t_, c0, float(CAP * q), None, ALU.is_gt))
                v(dve.tensor_tensor(n_ov, n_ov, t_, ALU.add))
            v(dve.tensor_tensor_scan(cum, ones[0:1, 0:NE], n_ov, 0.0, ALU.mult, ALU.add))
            v(dve.tensor_tensor(exc, cum, n_ov, ALU.subtract))
            full = [1, MAXOV, NE]
            T0, T1, T2 = (ovt[:, q] for q in range(3))
            sl = slotno[:].unsqueeze(2).broadcast_to(full)

            def per_e(x):
                return x.unsqueeze(1).broadcast_to(full)
            v(dve.tensor_tensor(T0, per_e(cum), sl, ALU.is_le))
            v(dve.tensor_reduce(ovr[:, 0], T0, AX.X, ALU.add))
            v(dve.tensor_tensor(T1, per_e(exc), sl, ALU.is_le))
            v(dve.tensor_tensor(T1, T1, T0, ALU.subtract))
            for q, x in ((1, s0), (2, e0), (3, exc)):
                v(dve.tensor_tensor(T2, T1, per_e(x), ALU.mult))
                v(dve.tensor_reduce(ovr[:, q], T2, AX.X, ALU.add))
            v(dve.tensor_tensor(ovr[:, 4], slotno[:], ovr[:, 3], ALU.subtract))
            v(dve.tensor_scalar(ovr[:, 4], ovr[:, 4], 1.0, float(CAP), ALU.add, ALU.mult))
            v(dve.tensor_tensor(ovr[:, 4], ovr[:, 4], ovr[:, 1], ALU.add))
            v(dve.tensor_scalar(ovr[:, 2], ovr[:, 2], float(-CAP), None, ALU.add))
            v(dve.tensor_tensor(ovr[:, 4], ovr[:, 4], ovr[:, 2], ALU.min))
            v(dve.tensor_scalar(ovr[:, 4], ovr[:, 4], 0.0, None, ALU.max))
            v(dve.tensor_scalar(ovr[:, 0], ovr[:, 0], float(NE - 1), None, ALU.min))
            dve.tensor_copy(ovs[:], ovr[:, 4])
            dve.tensor_copy(ove[:], ovr[:, 0])
            v(dve.tensor_copy(ovn[:], cum[:, NE - 1:NE]))
            dve.sem_inc(tab_ready, 1)

            def window(b, down_w, high_at, split, down_at, silu_at, up_at, hid_sem, made_at):
                wd = down_w[:].rearrange("p (k c) -> p k c", k=4)

                def low_part(f):
                    dve.wait_ge(high_at[0], high_at[1] + f + 1)
                    wait(dve, down_at[0], down_at[1] + (0, -2, -1, 1)[f])
                    dve.tensor_tensor(dL[f % 3][:], wd[:, f, :], dH[f % 3][:].bitcast(F32), ALU.subtract).then_inc(split, 1)

                for f in range(3):
                    low_part(f)
                dve.wait_ge(*silu_at)
                for h in range(2):
                    fs = slice(2 * h, 2 * h + 2)
                    dve.wait_ge(up_at[0], up_at[1] + h + 1)
                    dve.tensor_tensor(gate_s[:, b, fs, :], gate_s[:, b, fs, :],
                                      bank[2 + 4 * b + h][:, 0:2 * CAP].rearrange("p (f c) -> p f c", f=2),
                                      ALU.mult).then_inc(hid_whole, 1)
                    dve.wait_ge(hid_whole, made_at + 2 * h + 1)
                    dve.tensor_copy(hidH[:, b, fs, :], gate_s[:, b, fs, :]).then_inc(hid_whole, 1)
                    dve.wait_ge(hid_whole, made_at + 2 * h + 2)
                    dve.tensor_tensor(hidL[:, b, fs, :], gate_s[:, b, fs, :], hidH[:, b, fs, :].bitcast(F32),
                                      ALU.subtract).then_inc(hid_sem, 1)
                low_part(3)

            def expert(i, b):
                E = NE * l + 2 * i + b
                window(b, ring[EXPERT_SLOTS[b][2]], (down_high, 4 * E), down_split, (down_done, 4 * E),
                       (silu_done, E + 1), (up_done, 2 * E), hid_done, 4 * E)
            hid_whole = hid_steps
            for b in range(2):
                expert(0, b)
            with dve.Fori(1, NE // 2) as i:
                for b in range(2):
                    expert(i, b)
            o = ov[l]
            hid_whole = o["steps"]
            dve.sem_inc(o["hid"], 2)
            nov = dve.value_load(ovn[0:1, 0:1], min_val=0, max_val=MAXOV)
            with dve.If(nov > 0):
                with dve.Fori(0, nov) as i:
                    window(0, ring[OVER_SLOTS[2]], (o["high"], 4 * i), o["split"], (o["down"], 4 * i + 4),
                           (o["silu"], i + 1), (o["up"], 2 * i + 2), o["hid"], 4 * i)
            dve.nop()
            for t in range(TT):
                for j in range(2):
                    dve.wait_ge(gathered[2 * t + j], 16 * (l + 1))
                    ins = dve.scalar_tensor_tensor(out=xres[:, t, :], in0=gath[:, 2 * t + j, :], scalar=wts[:, j, t:t + 1],
                                                   in1=xres[:, t, :], op0=ALU.mult, op1=ALU.add)
                    if j == 0:
                        v(ins)
                ins.then_inc(combined, 1)
                own(combined)
        dve.wait_ge(fing_in, 16)
        dve.wait_ge(std_done, norm_no["fin"])
        v(dve.reciprocal(rstd[:], std[:]))
        for t in range(TT):
            wait(dve, out_sem, 16 * (t - 1))
            dve.scalar_tensor_tensor(out=yfin[:, t % 2, :], in0=xres[:, t, :], scalar=rstd[:, t:t + 1], in1=fing[:],
                                     op0=ALU.mult, op1=ALU.mult).then_inc(fin, 1)
            own(fin)


_INS = ("x", "mem", "mem_norm_g", "w_mem_kv", "norm1_g", "w_in", "lam_q1", "lam_k1", "lam_q2", "lam_k2",
        "subln_g", "q_norm_g", "k_norm_g", "w_up_a", "w_up_b", "w_up_c", "w_out", "norm2_g",
        "w_router_group", "b_router_group", "w_router_expert", "b_router_expert",
        "w_exp_gate", "w_exp_up", "w_exp_down", "final_norm_g")


def _constants():
    pos = np.arange(SEQ, dtype=np.float32)
    inv = (10000.0 ** (-np.arange(0, HD, 2, dtype=np.float32) / HD)).astype(np.float32)
    ang_a = pos[:, None] * inv
    inv = (10000.0 ** (-np.arange(0, HD // 2, 2, dtype=np.float32) / (HD // 2))).astype(np.float32)
    ang_b = np.concatenate([(pos // GRID_W)[:, None] * inv, (pos % GRID_W)[:, None] * inv], 1)
    made = {}
    for n, ang in (("a", ang_a), ("b", ang_b)):
        ang = ang.astype(np.float32).astype(np.float64)
        made["cos_" + n] = np.cos(ang)
        made["sin_" + n] = np.concatenate([-np.sin(ang), np.sin(ang)], 1)
    li = [0.8 - 0.6 * math.exp(-0.3 * l) for l in range(DEPTH)]
    made["lam_init"] = np.array([[x for l in li for x in (l, 1.0 - l)]])
    made["ident"] = np.eye(P)
    made["upper"] = np.triu(np.ones((P, P)), 1)
    made["iota"] = np.arange(HALF)[None]
    made["first"] = (NE - np.arange(NE))[None]
    return {k: np.ascontiguousarray(v, np.float32) for k, v in made.items()}


def kernel(**inputs):
    import concourse.bacc as bacc
    from concourse.bass_utils import run_bass_kernel_spmd

    nc = bacc.Bacc("TRN2", target_bir_lowering=False, num_devices=1)
    given = {n: np.ascontiguousarray(inputs[n]) for n in _INS} | _constants()
    arrays, aps = {}, {}
    for name, arr in given.items():
        arrays[f"in_{name}"] = arr
        aps[name] = nc.dram_tensor(f"in_{name}", arr.shape, mybir.dt.from_np(arr.dtype), kind="ExternalInput").ap()
    result = nc.dram_tensor("result", (1, SEQ, D), F32, kind="ExternalOutput").ap()
    build(nc, aps, result)
    r = run_bass_kernel_spmd(nc, [arrays], core_ids=[0])
    return r.results[0]["result"]
```

```python
import math
from contextlib import ExitStack

import numpy as np

import concourse.bass as bass
from concourse import mybir

F32 = mybir.dt.float32
F32R = mybir.dt.float32r
I32 = mybir.dt.int32
ALU = mybir.AluOpType
ACT = mybir.ActivationFunctionType
AX = mybir.AxisListType

P = 128
D = 1024
SEQ = 512
DEPTH = 2
MEM = 256
HD = 64
GRID_W = 64
EPS = 1e-6
NG, EPG = 4, 8
NE = NG * EPG
TOPK = 2
FE = 512
KT = D // P
TT = SEQ // P
SLOTS = SEQ * TOPK
CAP = 84
MAXOV = SLOTS // CAP
NSMALL = 13 * DEPTH + 9
QW = 256
NQ = SLOTS // QW

AQ, AK, AV, BQ, BK, BV, CQ, GL = 0, 512, 1024, 1536, 2048, 2176, 2304, 2816

RING = 6
MEM_SLOTS = (5, 4)
DENSE_PANELS = (
    ("in", AQ, 512, "dv", 8), ("in", AK, 512, "dv", 8), ("in", AV, 512, "da", 8),
    ("in", GL, 512, "da", 4), ("in", GL + 512, 512, "da", 4), ("up", 0, 0, "dv", 8),
    ("in", BQ, 512, "da", 8), ("in", BK, 256, "da", 4),
    ("in", GL + 1024, 512, "da", 4), ("in", GL + 1536, 512, "da", 4), ("up", 1, 0, "dv", 8),
    ("in", CQ, 512, "da", 4),
    ("in", GL + 2048, 512, "da", 4), ("in", GL + 2560, 512, "da", 4), ("up", 2, 0, "dv", 8),
    ("out", 0, 512, "dv", 8), ("out", 512, 512, "dv", 8),
)
ND = len(DENSE_PANELS)
PANEL_AT = {n: j for j, n in enumerate(("aq", "ak", "av", "gate0", "", "up0", "bq", "bkv", "gate1", "", "up1",
                                        "cq", "gate2", "", "up2", "out0", "out1")) if n}
PER_DV = sum(n for *_, kind, n in DENSE_PANELS if kind == "dv")
PER_DA = sum(n for *_, kind, n in DENSE_PANELS if kind == "da")
FIRST_DA = 6
UPS_DV = [sum(p[4] for p in DENSE_PANELS[:PANEL_AT[f"up{br}"] + 1] if p[3] == "dv") for br in range(3)]
CW = 256
CHUNKS = [(j, c) for j, p in enumerate(DENSE_PANELS) for c in range(p[2] // CW if p[0] != "up" else 2)]
NC = len(CHUNKS)


def chunks_of(name):
    return [n for n, (j, _) in enumerate(CHUNKS) if j == PANEL_AT[name]]


ACT_HIGH = [n for name in ("ak", "av", "bq", "cq", "out0", "out1") for n in chunks_of(name)]


def used_after(l, j, c=None):
    kind, n = DENSE_PANELS[j][3:]
    before = sum(p[4] for p in DENSE_PANELS[:j] if p[3] == kind)
    parts = sum(q == j for q, _ in CHUNKS)
    return kind, (PER_DV * l if kind == "dv" else FIRST_DA + PER_DA * l) + before + n * (parts if c is None else c + 1) // parts


DRING = 2
PARTS_SLOT, LOW_SLOT, GATE_SLOT = 2, 4, 5
EXPERT_SLOTS = ((5, 1, 0), (3, 2, 4))
OVER_SLOTS = (5, 3, 2)


def dense_slot(l, j):
    slot = j % DRING
    return slot, l * len(range(slot, ND, DRING)) + j // DRING + 1


ITEMS = [(br, j, t) for br in range(3) for j in (range(4) if br < 2 else range(2)) for t in range(TT)]
BRANCH_ITEMS = [[n for n, it in enumerate(ITEMS) if it[0] == br] for br in range(3)]
NI = len(ITEMS)


def build(nc, a, out):
    with ExitStack() as ctx:
        return _build(nc, ctx, a, out)


def _build(nc, ctx, a, out):
    def sem(name):
        return ctx.enter_context(nc.semaphore(name))

    def sb(name, shape, dt=F32):
        return ctx.enter_context(nc.sbuf_tensor(name, shape, dt))

    KB = 1024
    arena_kb = 78
    base = -(-nc.sbuf_base // 64) * 64
    sb("arena", [P, (arena_kb * KB + base - nc.sbuf_base) // 4])
    ring_base = -(-nc.sbuf_base // 64) * 64
    sb("ring_space", [P, RING * 4096 + (ring_base - nc.sbuf_base) // 4])
    ring = [nc.alloc_sbuf_tensor_at(f"ring{i}", [P, 4096], F32, offset=ring_base + i * 16 * KB) for i in range(RING)]
    xres = sb("xres", [P, TT, D])
    ident = sb("ident", [P, P])
    ones = sb("ones", [P, P])
    upper = sb("upper", [P, P])
    cosA = sb("cosA", [P, TT, 32])
    sinA = sb("sinA", [P, TT, 2, 32])
    cosB = sb("cosB", [P, TT, 32])
    sinB = sb("sinB", [P, TT, 2, 32])
    memkT = sb("memkT", [P, 4, MEM])
    memv = sb("memv", [P, 2, 512])
    router_w = sb("router_w", [P, DEPTH, KT, NG + NE])
    router_b = sb("router_b", [P, DEPTH, NG + NE])
    gcols = sb("gcols", [P, 2 * DEPTH + 1, KT])
    subg = sb("subg", [P, DEPTH])
    qg = sb("qg", [P, DEPTH, 2, HD])
    laminit = sb("laminit", [P, DEPTH, 2])
    lamd = sb("lamd", [P, 2 * DEPTH])
    lam = sb("lam", [P, DEPTH])
    eps = sb("eps", [P, 1])
    ss = sb("ss", [P, TT])
    std = sb("std", [P, TT])
    rstd = sb("rstd", [P, TT])
    mx = sb("mx", [P, 4])
    nbias = sb("nbias", [P, 4])
    rowsum = sb("rowsum", [P, 4])
    rsum = sb("rsum", [P, 4])
    hsq = sb("hsq", [P, 4 * TT])
    hss = sb("hss", [P, 2, 4])
    hstd = sb("hstd", [P, 2, 4])
    hr = sb("hr", [P, 4])
    sidx = sb("sidx", [1, NE], I32)
    ovn = sb("ovn", [1, 1], I32)
    ove = sb("ove", [1, MAXOV], I32)
    ovs = sb("ovs", [1, MAXOV], I32)
    destf = sb("destf", [P, 2, TT])
    desth = sb("desth", [P, 2, TT])
    desti = sb("desti", [P, 2, TT], I32)
    wts = sb("wts", [P, 2, TT])

    def at(name, shape, kb, dt=F32):
        size = 4 * int(np.prod(shape[1:]))
        assert kb * KB + size <= arena_kb * KB, name
        return nc.alloc_sbuf_tensor_at(name, shape, dt, offset=base + int(kb * KB))

    gates_s = nc.alloc_sbuf_tensor_at("gates_s", [P, KT, SEQ], F32, offset=ring_base + GATE_SLOT * 16 * KB)
    lamv = at("lamv", [P, 4 * DEPTH, HD], 40)
    hT = at("hT", [P, KT, SEQ], 0)
    memx = at("memx", [P, 2, D], 16)
    qT = at("qT", [P, 4, SEQ], 16)
    kT = at("kT", [P, 4, SEQ], 24)
    bv = at("bv", [P, TT, P], 32)
    av = at("av", [P, TT, 512], 32)
    oT = at("oT", [P, 4, SEQ], 40)
    hH = at("hH", [P, KT, SEQ], 0, F32R)
    hL = nc.alloc_sbuf_tensor_at("hL", [P, KT, SEQ], F32R, offset=ring_base + LOW_SLOT * 16 * KB)
    wH = [nc.alloc_sbuf_tensor_at(f"wH{i}", [P, KT, CW], F32R, offset=ring_base + (PARTS_SLOT + i) * 16 * KB) for i in range(2)]
    wL = [nc.alloc_sbuf_tensor_at(f"wL{i}", [P, KT, CW], F32R,
                                  offset=ring_base + ((PARTS_SLOT + i) * 16 + 8) * KB) for i in range(2)]
    mergedT = at("mergedT", [P, KT, SEQ], 48)
    oH = [at(f"oH{i}", [P, SEQ], kb, F32R) for i, kb in enumerate((64, 66, 72, 74))]
    oL = at("oL", [P, 4, SEQ], 40, F32R)
    o_tok = at("o_tok", [P, 4 * TT, P], 48)
    junk_a = at("junk_a", [P, P], 56)
    prob = at("prob", [P, 4, 512], 64)
    xn = at("xn", [P, 2, D], 48)
    scaledT = at("scaledT", [P, 2, KT, P], 56)
    roped = at("roped", [P, 2, CW], 64)
    raw = at("raw", [P, 2, CW], 68)
    tmp = at("tmp", [P, 512], 70)
    pT = at("pT", [P, 2, 4, P], 72)
    junk = at("junk", [P, D], 72)
    foldc = at("foldc", [P, 2, TT, 2, 32], 72)
    folds = at("folds", [P, 2, TT, 2, 32], 74)
    iota = at("iota", [P, QW], 76)
    hsT = at("hsT", [P, KT, SLOTS + CAP], 16)
    xnH = at("xnH", [P, TT, D], 52, F32R)
    xnL = at("xnL", [P, TT, D], 0, F32R)
    pick = at("pick", [P, 2, TT, QW], 68, F32R)
    gate_s = at("gate_s", [P, 2, 4, CAP], 52)
    hidH = at("hidH", [P, 2, 4, CAP], 55, F32R)
    hidL = at("hidL", [P, 2, 4, CAP], 58, F32R)
    ysb = at("ysb", [P, D], 61)
    dH = [at(f"dH{i}", [P, D], kb, F32R) for i, kb in enumerate((0, 4, 8))]
    dL = [at(f"dL{i}", [P, D], kb, F32R) for i, kb in enumerate((12, 66, 70))]
    gath = at("gath", [P, 2 * TT, D], 16)
    lg = at("lg", [P, TT, NG + NE], 16)
    em = at("em", [P, TT, NE], 17)
    cand = at("cand", [P, TT, NE], 17.5)
    sel1 = at("sel1", [P, TT, NE], 18)
    sel2 = at("sel2", [P, TT, NE], 18.5)
    gt = at("gt", [P, TT, NG], 19)
    gsel = at("gsel", [P, TT, NG], 19.25)
    first = sb("first", [P, NE])
    slotno = sb("slotno", [1, MAXOV])
    m1 = sb("m1", [P, TT])
    m2 = sb("m2", [P, TT])
    gp = sb("gp", [P, TT])
    ex = sb("ex", [P, TT])
    cnt = at("cnt", [P, NE], 51)
    incl = at("incl", [P, NE], 51.25)
    start = at("start", [P, NE], 51.5)
    ovc = at("ovc", [1, 4, NE], 68)
    ovr = at("ovr", [1, 6, MAXOV], 69)
    ovt = at("ovt", [1, 3, MAXOV, NE], 70)

    bank = [ctx.enter_context(nc.psum_tensor(f"bank{i}", [P, 512], F32)) for i in range(8)]
    ybuf = nc.dram_tensor("ybuf", [SLOTS + CAP, D], F32, kind="Internal").ap()

    consts_in = sem("consts_in")
    x_in = sem("x_in")
    mem_in = sem("mem_in")
    ident_in = sem("ident_in")
    mem_gain_in = sem("mem_gain_in")
    const_made = sem("const_made")
    mem_w_in = [sem(f"mem_w_in{i}") for i in range(2)]
    loaded = [sem(f"loaded{i}") for i in range(DRING)]
    high_done = sem("high_done")
    act_high = sem("act_high")
    split_done = sem("split_done")
    first_high = sem("first_high")
    first_split = sem("first_split")
    exp_loaded = [sem(f"exp_loaded{i}") for i in range(RING)]
    ss_done = sem("ss_done")
    std_done = sem("std_done")
    xn_ready = sem("xn_ready")
    nt_done = sem("nt_done")
    nt_out = sem("nt_out")
    dv_done = sem("dv_done")
    dv_free = sem("dv_free")
    da_done = sem("da_done")
    da_free = sem("da_free")
    rope_ready = sem("rope_ready")
    tr_done = sem("tr_done")
    tr_out = sem("tr_out")
    hss_done = sem("hss_done")
    hstd_done = sem("hstd_done")
    s_done = sem("s_done")
    bias_ready = sem("bias_ready")
    exp_done = sem("exp_done")
    p_ready = sem("p_ready")
    pt_done = sem("pt_done")
    pt_out = sem("pt_out")
    pv_done = sem("pv_done")
    o_out = sem("o_out")
    sub_scaled = sem("sub_scaled")
    sub_turned = sem("sub_turned")
    sq_root = sem("sq_root")
    sub_out = sem("sub_out")
    o_high = sem("o_high")
    o_split = sem("o_split")
    raw_ready = sem("raw_ready")
    gate_ready = sem("gate_ready")
    merged = sem("merged")
    lg_done = sem("lg_done")
    gd_ready = sem("gd_ready")
    gexp_done = sem("gexp_done")
    sel_ready = sem("sel_ready")
    rank_done = sem("rank_done")
    tab_ready = sem("tab_ready")
    starts_ready = sem("starts_ready")
    xn_high = sem("xn_high")
    split_ready = sem("split_ready")
    pick_ready = sem("pick_ready")
    perm_done = sem("perm_done")
    perm_out = sem("perm_out")
    pad_done = sem("pad_done")
    gate_done = sem("gate_done")
    silu_done = sem("silu_done")
    up_done = sem("up_done")
    hid_done = sem("hid_done")
    hid_steps = sem("hid_steps")
    down_done = sem("down_done")
    down_high = sem("down_high")
    down_split = sem("down_split")
    y_out = sem("y_out")
    y_stored = sem("y_stored")
    ov = [{n: sem(f"ov_{n}{l}") for n in ("l0", "l1", "l2", "gate", "silu", "up", "hid", "steps", "high", "split",
                            "down", "yout", "store", "over")}
          for l in range(DEPTH)]
    y_all = sem("y_all")
    gathered = [sem(f"gathered{i}") for i in range(2 * TT)]
    combined = sem("combined")
    fin = sem("fin")
    out_sem = sem("out_sem")
    vs = sem("vs")
    asm = sem("asm")
    lam_d = sem("lam_d")
    lam_e = sem("lam_e")
    fing_in = sem("fing_in")

    fing = at("fing", [P, D], 48)
    yfin = at("yfin", [P, 2, D], 52)

    block = ctx.enter_context(nc.Block())

    def wait(eng, s, n):
        if not isinstance(n, int) or n > 0:
            eng.wait_ge(s, n)

    def used(l, j, c=None):
        kind, n = used_after(l, j, c)
        return (dv_done if kind == "dv" else da_done), n

    def split_at(l, n):
        return (first_split, 2 * (l - 1) + n + 1) if l and n < 2 else (split_done, NC * l - 2 * l + n + 1)

    def chunk_of(l, n):
        j, ch = CHUNKS[n]
        s, count = dense_slot(l, j)
        if DENSE_PANELS[j][0] == "up":
            w = ring[s][:].rearrange("p (k c) -> p k c", k=4)[:, :, 2 * ch * CW:2 * (ch + 1) * CW]
        else:
            w = wide(ring[s], DENSE_PANELS[j][2])[:, :, ch * CW:(ch + 1) * CW]
        return w, (loaded[s], 16 * count)

    def parts_of(n):
        H, L = wH[n % 2][:], wL[n % 2][:]
        if DENSE_PANELS[CHUNKS[n][0]][0] == "up":
            H, L = (x.rearrange("p k c -> p (k c)").rearrange("p (k c) -> p k c", k=4) for x in (H, L))
        return H, L

    def act_high_at(l, n):
        return act_high, len(ACT_HIGH) * l + ACT_HIGH.index(n) + 1

    def panel_free(l, j):
        return split_at(l, sum(q <= j for q, _ in CHUNKS) - 1)

    def slot_free(l, s):
        if s == GATE_SLOT:
            return dv_free, PER_DV * l + UPS_DV[2]
        if s == LOW_SLOT:
            return used(l, ND - 1)
        if s >= PARTS_SLOT:
            return used(l, *CHUNKS[max(n for n in range(NC) if n % 2 == s - PARTS_SLOT)])
        return panel_free(l, max(j for j in range(ND) if j % DRING == s))

    def wide(t, c):
        return t[:, 0:KT * c].rearrange("p (k c) -> p k c", k=KT)

    @block.sync
    def _(sp):
        def col(v, n):
            return v.rearrange("(k p) -> p k", p=P)

        def dense_load(l, j):
            kind, c0, width = DENSE_PANELS[j][:3]
            s, _ = dense_slot(l, j)
            if kind == "in":
                dst, src = wide(ring[s], width), a["w_in"][l, :, c0:c0 + width].rearrange("(k p) c -> p k c", p=P)
            elif kind == "out":
                dst, src = wide(ring[s], width), a["w_out"][l, :, c0:c0 + width].rearrange("(k p) c -> p k c", p=P)
            else:
                w = (a["w_up_a"], a["w_up_b"], a["w_up_c"])[c0]
                dst, src = ring[s][:].rearrange("p (k c) -> p k c", k=4), w[l].rearrange("(k p) c -> p k c", p=P)
            sp.dma_start(dst, src).then_inc(loaded[s], 16)

        sp.dma_start(memx[:], a["mem"].rearrange("b (t p) d -> p (b t) d", p=P)).then_inc(mem_in, 16)
        sp.dma_start(ident[:], a["ident"]).then_inc(ident_in, 16)
        sp.dma_start(gcols[:, 2 * DEPTH, :], col(a["mem_norm_g"], KT), allow_slow_non_contiguous=True).then_inc(mem_gain_in, 16)
        for n in range(2):
            sp.dma_start(wide(ring[MEM_SLOTS[n]], 512), a["w_mem_kv"][:, n * 512:(n + 1) * 512].rearrange(
                "(k p) c -> p k c", p=P)).then_inc(mem_w_in[n], 16)
        dense_load(0, 0)
        sp.dma_start(xres[:], a["x"].rearrange("b (t p) d -> p (b t) d", p=P)).then_inc(x_in, 16)
        small = []

        def load(dst, src):
            small.append(sp.dma_start(dst, src, allow_slow_non_contiguous=True).then_inc(consts_in, 16))

        for l in range(DEPTH):
            load(gcols[:, 2 * l, :], col(a["norm1_g"][l], KT))
            load(gcols[:, 2 * l + 1, :], col(a["norm2_g"][l], KT))
            load(router_w[:, l, :, 0:NG], a["w_router_group"][l].rearrange("(k p) c -> p k c", p=P))
            load(router_w[:, l, :, NG:], a["w_router_expert"][l].rearrange("(k p) c -> p k c", p=P))
            load(router_b[:, l, 0:NG], a["b_router_group"][l:l + 1].broadcast_to([P, NG]))
            load(router_b[:, l, NG:], a["b_router_expert"][l:l + 1].broadcast_to([P, NE]))
            load(subg[:, l:l + 1], a["subln_g"][l:l + 1].rearrange("o p -> p o"))
            load(qg[:, l, 0], a["q_norm_g"][l:l + 1].broadcast_to([P, HD]))
            load(qg[:, l, 1], a["k_norm_g"][l:l + 1].broadcast_to([P, HD]))
            for n, name in enumerate(("lam_q1", "lam_k1", "lam_q2", "lam_k2")):
                load(lamv[:, 4 * l + n], a[name][l:l + 1].broadcast_to([P, HD]))
        load(cosA[:], a["cos_a"].rearrange("(t p) c -> p t c", p=P))
        load(sinA[:].rearrange("p t a c -> p t (a c)"), a["sin_a"].rearrange("(t p) c -> p t c", p=P))
        load(cosB[:], a["cos_b"].rearrange("(t p) c -> p t c", p=P))
        load(sinB[:].rearrange("p t a c -> p t (a c)"), a["sin_b"].rearrange("(t p) c -> p t c", p=P))
        load(laminit[:].rearrange("p l a -> p (l a)"), a["lam_init"].broadcast_to([P, 2 * DEPTH]))
        load(upper[:], a["upper"])
        load(iota[:], a["iota"].broadcast_to([P, QW]))
        load(first[:], a["first"].broadcast_to([P, NE]))
        load(slotno[:], a["iota"][:, 0:MAXOV])
        assert len(small) == NSMALL
        dense_load(0, 1)

        def dense_loads(l, js):
            for j in js:
                if j == DRING and l:
                    sp.wait_ge(gathered[2 * TT - 1], 16 * l)
                if j >= DRING:
                    sp.wait_ge(*panel_free(l, j - DRING))
                else:
                    sp.wait_ge(down_split, 4 * (NE * l - 1))
                dense_load(l, j)

        for l in range(DEPTH):
            dense_loads(l, range(DRING, ND))

            def expert_loads(i):
                for b in range(2):
                    e = 2 * i + b
                    ei = slice(e, e + 1) if isinstance(e, int) else bass.ds(e, 1)
                    for k, w in enumerate((a["w_exp_gate"], a["w_exp_up"], a["w_exp_down"])):
                        s = EXPERT_SLOTS[b][k]
                        if isinstance(i, int):
                            sp.wait_ge(*slot_free(l, s))
                        else:
                            E = NE * l + e - 2
                            sp.wait_ge(*((gate_done, E + 1), (up_done, 2 * E + 2), (down_split, 4 * E + 4))[k])
                        sp.dma_start(ring[s][:].rearrange("p (k c) -> p k c", c=w.shape[3]),
                                     w[l, ei].rearrange("e (k p) c -> p (e k) c", p=P)).then_inc(exp_loaded[s], 16)
            expert_loads(0)
            with sp.Fori(1, NE // 2) as i:
                expert_loads(i)
            sp.wait_ge(tab_ready, l + 1)
            nov = sp.value_load(ovn[0:1, 0:1], min_val=0, max_val=MAXOV)
            with sp.If(nov > 0):
                with sp.Fori(0, nov) as i:
                    e = sp.value_load(ove[0:1, bass.ds(i, 1)], min_val=0, max_val=NE - 1)
                    for k, w in enumerate((a["w_exp_gate"], a["w_exp_up"], a["w_exp_down"])):
                        s = OVER_SLOTS[k]
                        o = ov[l]
                        sp.wait_ge(*((gate_done, NE * (l + 1) - 1), (gate_done, NE * (l + 1)), (up_done, 2 * NE * (l + 1)))[k])
                        sp.wait_ge(*((o["gate"], i + 1), (o["up"], 2 * i + 2), (o["down"], 4 * i + 4))[k])
                        sp.dma_start(ring[s][:].rearrange("p (k c) -> p k c", c=w.shape[3]),
                                     w[l, bass.ds(e, 1)].rearrange("e (k p) c -> p (e k) c", p=P)
                                     ).then_inc(ov[l][f"l{k}"], 16)
            sp.nop()
            if l + 1 < DEPTH:
                dense_loads(l + 1, range(DRING))
        for t in range(TT):
            sp.wait_ge(fin, t + 1)
            sp.dma_start(out[0, t * P:(t + 1) * P, :], yfin[:, t % 2, :]).then_inc(out_sem, 16)
            sp.wait_ge(out_sem, 16 * (t + 1))

    @block.gpsimd
    def _(pool):
        own_high = 0
        for l in range(DEPTH):
            for n in range(2 if l else 0, NC):
                if n >= 2:
                    pool.wait_ge(*used(l, *CHUNKS[n - 2]))
                w, arrived = chunk_of(l, n)
                pool.wait_ge(*arrived)
                H, L = parts_of(n)
                if n in ACT_HIGH:
                    pool.wait_ge(*act_high_at(l, n))
                else:
                    own_high += 1
                    pool.tensor_scalar(H, w, 1.0, None, ALU.mult).then_inc(high_done, 1)
                    pool.wait_ge(high_done, own_high)
                pool.tensor_tensor(L, w, H.bitcast(F32), ALU.subtract).then_inc(split_done, 1)
            pool.wait_ge(y_all, l + 1)
            for t in range(TT):
                for j in range(2):
                    pool.indirect_dma_start(
                        out=gath[:, 2 * t + j, :], out_offset=None, in_=ybuf[0:SLOTS, :],
                        in_offset=bass.IndirectOffsetOnAxis(ap=desti[:, j, t:t + 1], axis=0),
                    ).then_inc(gathered[2 * t + j], 16)
        pool.dma_start(fing[:], a["final_norm_g"].rearrange("(o d) -> o d", o=1).broadcast_to([P, D])).then_inc(fing_in, 16)

    all_consts = 16 * NSMALL
    norm_tiles = {"mem": 0}
    for l in range(DEPTH):
        norm_tiles["n1", l] = 2 + 8 * l
        norm_tiles["n2", l] = 2 + 8 * l + 4
    norm_tiles["fin"] = 2 + 8 * DEPTH

    @block.tensor
    def _(pe):
        cnt_ = {"dv": 0, "da": 0, "tr": 0, "perm": 0, "chunk": 0}

        def chunk():
            n = cnt_["chunk"]
            cnt_["chunk"] += 1
            pe.wait_ge(*split_at(n // NC, n % NC))
            return wH[n % NC % 2], wL[n % NC % 2]

        def product(dst, lhs, rhs, k, n=KT):
            (lH, lL), (rH, rL) = lhs, rhs
            pe.matmul(dst, lH, rH, start=(k == 0), stop=False)
            pe.matmul(dst, lH, rL, start=False, stop=False)
            return pe.matmul(dst, lL, rH, start=False, stop=(k == n - 1))

        def dense(kind, lhs, rhs, n, cols):
            c = cnt_[kind]
            cnt_[kind] += 1
            done, free, b = (dv_done, dv_free, 0) if kind == "dv" else (da_done, da_free, 2)
            wait(pe, free, c - 1)
            for k in range(n):
                mm = pe.matmul(bank[b + c % 2][:, 0:cols], lhs(k), rhs(k), start=(k == 0), stop=(k == n - 1))
            return mm.then_inc(done, 1)

        def split_dense(kind, lhs, rhs, cols, merged_before=None):
            c = cnt_[kind]
            cnt_[kind] += 1
            done, free, b = (dv_done, dv_free, 0) if kind == "dv" else (da_done, da_free, 2)
            wait(pe, free, c - 1)
            for k in range(KT):
                if merged_before is not None:
                    pe.wait_ge(merged, merged_before + k + 1)
                mm = product(bank[b + c % 2][:, 0:cols], lhs(k), rhs(k), k)
            mm.then_inc(done, 1)

        def norm_transposes(key, tiles):
            g0 = norm_tiles[key]
            for t in tiles:
                g = g0 + t
                pe.wait_ge(xn_ready, g + 1)
                wait(pe, nt_out, g - 1)
                for k in range(KT):
                    tr = pe.transpose(bank[4 + 2 * (g % 2) + k // 4][:, (k % 4) * P:(k % 4 + 1) * P],
                                      xn[:, g % 2, k * P:(k + 1) * P], ident[:])
                tr.then_inc(nt_done, 1)

        def head_transposes():
            r = cnt_["tr"]
            cnt_["tr"] += 1
            pe.wait_ge(rope_ready, r + 1)
            wait(pe, tr_out, r - 1)
            for k in range(2):
                tr = pe.transpose(bank[4 + r % 2][:, k * P:(k + 1) * P], roped[:, r % 2, k * P:(k + 1) * P], ident[:])
            tr.then_inc(tr_done, 1)

        def by_tokens(kind, chunks, between, merged_before=None):
            for ch in range(chunks):
                H, L = chunk()
                for t in range(TT):
                    tok = slice(t * P, (t + 1) * P)
                    split_dense(kind, lambda k: (hH[:, k, tok], hL[:, k, tok]), lambda k: (H[:, k, :], L[:, k, :]), CW,
                                merged_before if ch == t == 0 else None)
                    between(TT * ch + t)

        def by_features(groups):
            for f in range(groups):
                if f % 2 == 0:
                    H, L = chunk()
                cols = slice(f % 2 * P, (f % 2 + 1) * P)
                split_dense("da", lambda k: (H[:, k, cols], L[:, k, cols]), lambda k: (hH[:, k, :], hL[:, k, :]), 512)

        def attention(l, br):
            items = [l * NI + n for n in BRANCH_ITEMS[br]]
            wait(pe, dv_free, cnt_["dv"])
            pe.wait_ge(da_free, cnt_["da"])

            def scores(n):
                _, j, t = ITEMS[n % NI]
                tok = slice(t * P, (t + 1) * P)
                for m in range(2):
                    wait(pe, exp_done, 2 * n + m - 1)
                    b = bank[m]
                    if br < 2:
                        r = slice(m * HD, (m + 1) * HD)
                        kb = j if br == 0 else j // 2
                        mm = pe.matmul(b[:], qT[r, j, tok], kT[r, kb, :], start=True, stop=True)
                    else:
                        mm = pe.matmul(b[:, 0:MEM], av[:, 2 * j + m, tok], memkT[:, 2 * j + m, :], start=True, stop=True)
                    mm.then_inc(s_done, 1)

            def gate_part(q):
                for x in range(64 // len(items) * q, 64 // len(items) * (q + 1)):
                    f, k = x // KT, x % KT
                    if x % (2 * KT) == 0:
                        gate_w[0] = chunk()
                    if k == 0:
                        wait(pe, da_free, cnt_["da"] - 1)
                    H, L = (w[:, k, f % 2 * P:(f % 2 + 1) * P] for w in gate_w[0])
                    mm = product(bank[2 + cnt_["da"] % 2][:], (H, L), (hH[:, k, :], hL[:, k, :]), k)
                    if k == KT - 1:
                        mm.then_inc(da_done, 1)
                        cnt_["da"] += 1

            def turn(n):
                pe.wait_ge(p_ready, n + 1)
                wait(pe, pt_out, n)
                maps = 1 if br == 0 else 2
                nk = 4 if br < 2 else 2
                for m in range(maps):
                    for k in range(nk):
                        tr = pe.transpose(bank[4 + m][:, k * P:(k + 1) * P], prob[:, 2 * (n % 2) + m, k * P:(k + 1) * P], ident[:])
                tr.then_inc(pt_done, 1)

            def values(n):
                _, j, t = ITEMS[n % NI]
                pe.wait_ge(pt_out, n + 1)
                wait(pe, o_out, n - 1)
                b = bank[6 + n % 2]
                if br == 0:
                    for k in range(4):
                        mm = pe.matmul(b[:, 0:P], pT[:, 0, k, :], av[:, k, j * P:(j + 1) * P], start=(k == 0), stop=(k == 3))
                elif br == 1:
                    for m in range(2):
                        for k in range(4):
                            mm = pe.matmul(b[m * HD:(m + 1) * HD, 0:P], bv[:, k, (j // 2) * HD:(j // 2 + 1) * HD],
                                           pT[:, m, k, :], start=(k == 0), stop=(k == 3))
                else:
                    for m in range(2):
                        for k in range(2):
                            mm = pe.matmul(b[:, m * P:(m + 1) * P], memv[:, k, (2 * j + m) * P:(2 * j + m + 1) * P],
                                           pT[:, m, k, :], start=(k == 0), stop=(k == 1))
                mm.then_inc(pv_done, 1)

            gate_w = [None]
            for q, n in enumerate(items):
                scores(n)
                if q:
                    values(n - 1)
                gate_part(q)
                turn(n)
            values(items[-1])

        def ups(l, br):
            at_branch = 12 * l + 4 * br
            for f in range(KT):
                if f % 4 == 0:
                    H, L = (w[:].rearrange("p k c -> p (k c)").rearrange("p (k c) -> p k c", k=4) for w in chunk())
                cols = slice(f % 4 * P, (f % 4 + 1) * P)
                c = cnt_["dv"]
                cnt_["dv"] += 1
                wait(pe, dv_free, c - 1)
                for k in range(4):
                    if f == 0:
                        pe.wait_ge(o_split, at_branch + k + 1)
                    mm = product(bank[c % 2][:], (H[:, k, cols], L[:, k, cols]), (oH[k][:], oL[:, k, :]), k, 4)
                mm.then_inc(dv_done, 1)

        pe.wait_ge(ident_in, 16)
        for l in range(DEPTH):
            pe.sem_inc(ov[l]["gate"], 1)
            pe.sem_inc(ov[l]["up"], 2)
            pe.sem_inc(ov[l]["down"], 4)
        norm_transposes("mem", range(2))
        pe.wait_ge(nt_out, 2)
        pe.wait_ge(mem_w_in[0], 16)
        w = wide(ring[MEM_SLOTS[0]], 512)
        for h in range(4):
            dense("da", lambda k: w[:, k, h * P:(h + 1) * P], lambda k: hT[:, k, 0:MEM], KT, MEM)
        pe.wait_ge(mem_w_in[1], 16)
        w = wide(ring[MEM_SLOTS[1]], 512)
        for t in range(2):
            dense("da", lambda k: hT[:, k, t * P:(t + 1) * P], lambda k: w[:, k, :], KT, 512)

        for l in range(DEPTH):
            n1 = norm_tiles["n1", l]
            norm_transposes(("n1", l), range(2))
            pe.wait_ge(nt_out, n1 + 1)

            def after_query(i):
                if i < 2:
                    norm_transposes(("n1", l), [i + 2])
                if i < 3:
                    pe.wait_ge(nt_out, n1 + i + 2)
                for _ in range((0, 0, 1, 2)[i] if i < 4 else 1):
                    head_transposes()
            by_tokens("dv", 2, after_query)
            by_tokens("dv", 2, lambda i: head_transposes())
            by_tokens("da", 2, lambda i: i or head_transposes())
            pe.wait_ge(tr_out, cnt_["tr"])
            attention(l, 0)
            for h in range(4):
                pe.wait_ge(sub_scaled, 4 * l + h + 1)
                for t in range(TT):
                    tr = pe.transpose(bank[4 + h][:, t * P:(t + 1) * P], o_tok[:, TT * h + t, :], ident[:])
                tr.then_inc(sub_turned, 1)
            ups(l, 0)
            by_tokens("da", 2, lambda i: i >= 2 and head_transposes())
            by_tokens("da", 1, lambda i: head_transposes())
            for _ in range(2):
                head_transposes()
            pe.wait_ge(tr_out, cnt_["tr"])
            attention(l, 1)
            ups(l, 1)
            by_features(4)
            attention(l, 2)
            ups(l, 2)
            by_tokens("dv", 4, merged_before=KT * l, between=lambda i: i >= 3 * TT + 2 and norm_transposes(("n2", l), [i - 3 * TT - 2]))
            wait(pe, dv_free, cnt_["dv"])
            for t in range(TT):
                if t < 2:
                    norm_transposes(("n2", l), [t + 2])
                pe.wait_ge(nt_out, norm_tiles["n2", l] + t + 1)
                for k in range(KT):
                    mm = pe.matmul(bank[0][:, t * 36:(t + 1) * 36], hT[:, k, t * P:(t + 1) * P],
                                   router_w[:, l, k, :], start=(k == 0), stop=(k == KT - 1))
            mm.then_inc(lg_done, 1)
            pe.wait_ge(sel_ready, l + 1)
            for t in range(TT):
                for u in range(t + 1):
                    mm = pe.matmul(bank[1][:, t * NE:(t + 1) * NE], upper[:] if u == t else ones[:], cand[:, u, :],
                                   start=(u == 0), stop=(u == t))
            for u in range(TT):
                mm = pe.matmul(bank[1][:, TT * NE:(TT + 1) * NE], ones[:], cand[:, u, :], start=(u == 0), stop=(u == TT - 1))
            mm.then_inc(rank_done, 1)
            pe.wait_ge(split_ready, l + 1)
            for q in range(NQ):
                pe.wait_ge(pick_ready, NQ * l + q + 1)
                for k in range(KT):
                    g = cnt_["perm"]
                    cnt_["perm"] += 1
                    wait(pe, perm_out, g - 3)
                    for t in range(TT):
                        for part in (xnH, xnL):
                            mm = pe.matmul(bank[4 + g % 4][:, 0:QW], part[:, t, k * P:(k + 1) * P], pick[:, q % 2, t, :],
                                           start=(t == 0 and part is xnH), stop=(t == TT - 1 and part is xnL))
                    mm.then_inc(perm_done, 1)
            pe.wait_ge(perm_out, cnt_["perm"])
            pe.wait_ge(pad_done, l + 1)
            pe.wait_ge(starts_ready, l + 1)

            def expert(i, b):
                E = NE * l + b + 2 * i
                panels = EXPERT_SLOTS[b]
                s0 = pe.value_load(sidx[0:1, bass.ds(2 * i + b, 1)] if not isinstance(i, int) else sidx[0:1, b:b + 1],
                                   min_val=0, max_val=SLOTS)
                wg, wu = (ring[s] for s in panels[:2])
                one_expert(s0, wg, wu, b, [(exp_loaded[s], 16 * (NE // 2 * l + i + 1)) for s in panels[:2]],
                           silu_free=(silu_done, E - 1), hid_free=(hid_done, 2 * (E - 1)), hid_at=(hid_done, 2 * E),
                           y_free=(y_out, 2 * E), split_at=(down_split, 4 * E), done=(gate_done, up_done, down_done))

            def one_expert(s0, wg, wu, b, arrive, silu_free, hid_free, hid_at, y_free, split_at, done):
                wgv, wuv = wide(wg, 512), wide(wu, 512)
                pe.wait_ge(*arrive[0])
                wait(pe, *silu_free)
                for f in range(4):
                    for k in range(KT):
                        mm = pe.matmul(bank[b][:, f * CAP:(f + 1) * CAP], wgv[:, k, f * P:(f + 1) * P],
                                       hsT[:, k, bass.ds(s0, CAP)], start=(k == 0), stop=(k == KT - 1))
                mm.then_inc(done[0], 1)
                pe.wait_ge(*arrive[1])
                wait(pe, *hid_free)
                for f in range(4):
                    for k in range(KT):
                        mm = pe.matmul(bank[2 + 4 * b + f // 2][:, f % 2 * CAP:(f % 2 + 1) * CAP], wuv[:, k, f * P:(f + 1) * P],
                                       hsT[:, k, bass.ds(s0, CAP)], start=(k == 0), stop=(k == KT - 1))
                    if f % 2:
                        mm.then_inc(done[1], 1)
                wait(pe, *y_free)
                for f in range(4):
                    if f % 2 == 0:
                        pe.wait_ge(hid_at[0], hid_at[1] + f // 2 + 1)
                    pe.wait_ge(split_at[0], split_at[1] + f + 1)
                    H, L = dH[f % 3], dL[f % 3]
                    for h in range(2):
                        y, cols = bank[4 + h][0:CAP, :], slice(h * 512, (h + 1) * 512)
                        pe.matmul(y, hidH[:, b, f, :], H[:, cols], start=(f == 0), stop=False)
                        pe.matmul(y, hidH[:, b, f, :], L[:, cols], start=False, stop=False)
                        mm = pe.matmul(y, hidL[:, b, f, :], H[:, cols], start=False, stop=(f == 3))
                    mm.then_inc(done[2], 1)

            for b in range(2):
                expert(0, b)
            with pe.Fori(1, NE // 2) as i:
                for b in range(2):
                    expert(i, b)
            o = ov[l]
            pe.wait_ge(tab_ready, l + 1)
            nov = pe.value_load(ovn[0:1, 0:1], min_val=0, max_val=MAXOV)
            with pe.If(nov > 0):
                with pe.Fori(0, nov) as i:
                    s0 = pe.value_load(ovs[0:1, bass.ds(i, 1)], min_val=0, max_val=SLOTS)
                    one_expert(s0, *(ring[slot] for slot in OVER_SLOTS[:2]), 0, [(o[f"l{k}"], 16 * i + 16) for k in range(2)],
                               silu_free=(silu_done, NE * (l + 1)), hid_free=(o["hid"], 2 * i + 2), hid_at=(o["hid"], 2 * i + 2),
                               y_free=(o["yout"], 2 * i + 2), split_at=(o["split"], 4 * i), done=(o["gate"], o["up"], o["down"]))
                    pe.wait_ge(o["down"], 4 * i + 8)
            pe.wait_ge(down_done, 4 * NE * (l + 1))
            pe.sem_inc(o["over"], 1)

    @block.scalar
    def _(act):
        c = {"da": 0, "tr": 0}
        made = {}

        def own(s):
            made[s.name] = made.get(s.name, 0) + 1
            act.wait_ge(s, made[s.name])

        def squares(key, nt, src, ready):
            g0 = norm_tiles[key]
            for t in range(nt):
                ready(t)
                act.activation(junk[:], src(t), ACT.Square, accum_out=ss[:, t:t + 1]).then_inc(ss_done, 1)
                own(ss_done)
                act.activation(std[:, t:t + 1], ss[:, t:t + 1], ACT.Sqrt, scale=1.0 / D, bias=eps[:, 0:1]).then_inc(std_done, 1)
                own(std_done)

        def dense_out(dst, cols):
            n = c["da"]
            c["da"] += 1
            act.wait_ge(da_done, n + 1)
            act.activation(dst, bank[2 + n % 2][:, 0:cols], ACT.Copy).then_inc(da_free, 1)
            own(da_free)

        def heads_out(dst, tok):
            n = c["tr"]
            c["tr"] += 1
            act.wait_ge(tr_done, n + 1)
            act.activation(dst[:, :, tok], bank[4 + n % 2][:, 0:2 * P].rearrange("p (b t) -> p b t", b=2),
                           ACT.Copy).then_inc(tr_out, 1)
            own(tr_out)

        act.wait_ge(const_made, 2)
        act.wait_ge(mem_in, 16)
        squares("mem", 2, lambda t: memx[:, t, :], lambda t: None)
        for h in range(4):
            dense_out(memkT[:, h, :], MEM)
        squares(("n1", 0), TT, lambda t: xres[:, t, :], lambda t: act.wait_ge(x_in, 16))
        for t in range(2):
            dense_out(memv[:, t, :], 512)
        act.wait_ge(lam_d, DEPTH)
        act.activation(lamd[:], lamd[:], ACT.Exp).then_inc(lam_e, 1)
        own(lam_e)

        def attention(l, br):
            maps_t = 1 if br == 0 else 2
            nk = 4 if br < 2 else 2
            cols = 512 if br < 2 else MEM
            scale = HD ** -0.5 if br < 2 else P ** -0.5
            items = [l * NI + n for n in BRANCH_ITEMS[br]]

            def exps(n):
                for m in range(2):
                    act.wait_ge(bias_ready, 2 * n + m + 1)
                    wait(act, pt_done, n - 1)
                    act.activation(prob[:, 2 * (n % 2) + m, 0:cols], bank[m][:, 0:cols], ACT.Exp,
                                   bias=nbias[:, 2 * (n % 2) + m:2 * (n % 2) + m + 1], scale=scale,
                                   accum_out=rowsum[:, 2 * (n % 2) + m:2 * (n % 2) + m + 1]).then_inc(exp_done, 1)
                    own(exp_done)

            def turned(n):
                act.wait_ge(pt_done, n + 1)
                wait(act, pv_done, n)
                for m in range(maps_t):
                    ins = act.activation(pT[:, m, 0:nk, :], bank[4 + m][:, 0:nk * P].rearrange("p (k t) -> p k t", k=nk), ACT.Copy)
                ins.then_inc(pt_out, 1)
                own(pt_out)

            def outputs(n):
                _, j, t = ITEMS[n % NI]
                tok = slice(t * P, (t + 1) * P)
                act.wait_ge(pv_done, n + 1)
                b = bank[6 + n % 2]
                if br == 0:
                    i = n % NI
                    act.activation(junk_a[:], b[:, 0:P], ACT.Square, accum_out=hsq[:, i:i + 1])
                    ins = act.activation(o_tok[:, i, :], b[:, 0:P], ACT.Copy)
                elif br == 1:
                    ins = act.activation(oT[:, j, tok], b[:, 0:P], ACT.Copy)
                else:
                    ins = act.activation(oT[:, 2 * j:2 * j + 2, tok], b[:, 0:2 * P].rearrange("p (m t) -> p m t", m=2), ACT.Copy)
                ins.then_inc(o_out, 1)
                own(o_out)

            def gate_out(f):
                g = c["da"]
                c["da"] += 1
                act.wait_ge(da_done, g + 1)
                if f == 0:
                    wait(act, dv_free, PER_DV * l + UPS_DV[br - 1] if br else 0)
                act.activation(gates_s[:, f, :], bank[2 + g % 2][:], ACT.Copy).then_inc(da_free, 1)
                own(da_free)

            per = len(items) // KT
            for q, n in enumerate(items):
                exps(n)
                if q:
                    outputs(n - 1)
                turned(n)
                if q % per == per - 1:
                    gate_out(q // per)
            outputs(items[-1])

        def high_chunks(l, ns):
            for n in ns:
                act.wait_ge(*used(l, *CHUNKS[n - 2]))
                w, arrived = chunk_of(l, n)
                act.wait_ge(*arrived)
                act.activation(parts_of(n)[0], w, ACT.Copy).then_inc(act_high, 1)
                own(act_high)

        def high_heads():
            for k in range(4):
                act.activation(oH[k][:], oT[:, k, :], ACT.Copy).then_inc(o_high, 1)
                own(o_high)

        def sigmoids():
            for f in range(KT):
                act.activation(gates_s[:, f, :], gates_s[:, f, :], ACT.Sigmoid).then_inc(gate_ready, 1)
                own(gate_ready)

        for l in range(DEPTH):
            if l:
                squares(("n1", l), TT, lambda t: xres[:, t, :], lambda t: act.wait_ge(combined, (l - 1) * TT + t + 1))
            def turned_tile(i):
                h = i // TT % 2 * 2
                heads_out((qT if i < 2 * TT else kT)[:, h:h + 2], slice(i % TT * P, (i % TT + 1) * P))

            ahead = chunks_of("ak") + chunks_of("av")
            for i in range(4 * TT - 1):
                turned_tile(i)
                if i % TT == TT - 1:
                    high_chunks(l, [ahead[i // TT]])
            for i in range(2 * TT):
                dense_out(av[:, i % TT, i // TT * CW:(i // TT + 1) * CW], CW)
                if i == 0:
                    turned_tile(4 * TT - 1)
                    high_chunks(l, [ahead[3]])
            attention(l, 0)
            act.activation(hsq[:], hsq[:], ACT.Sqrt, scale=1.0 / P, bias=eps[:, 0:1]).then_inc(sq_root, 1)
            own(sq_root)
            for h in range(4):
                act.wait_ge(sub_turned, 4 * l + h + 1)
                act.activation(oT[:, h, :], bank[4 + h][:], ACT.Copy, scale=subg[:, l:l + 1]).then_inc(sub_out, 1)
                own(sub_out)
                act.activation(oH[h][:], oT[:, h, :], ACT.Copy).then_inc(o_high, 1)
                own(o_high)
            sigmoids()
            high_chunks(l, chunks_of("bq"))
            for i in range(3 * TT):
                nh = 4 if i < 2 * TT else 2
                w = nh * HD
                n = c["da"]
                c["da"] += 1
                act.wait_ge(da_done, n + 1)
                b = bank[2 + n % 2]
                act.wait_ge(rope_ready, 7 * TT * l + 4 * TT + i - 1)
                if nh == 2:
                    act.activation(bv[:, i % TT, :], b[:, w:2 * w], ACT.Copy)
                act.activation(raw[:, i % 2, 0:w], b[:, 0:w], ACT.Copy).then_inc(da_free, 1)
                own(da_free)
                wait(act, hss_done, 3 * TT * l + i)
                act.activation(tmp[:, CW:CW + w], raw[:, i % 2, 0:w], ACT.Square).then_inc(raw_ready, 1)
                own(raw_ready)
                act.wait_ge(hss_done, 3 * TT * l + i + 1)
                act.activation(hstd[:, i % 2, 0:nh], hss[:, i % 2, 0:nh], ACT.Sqrt, scale=1.0 / HD, bias=eps[:, 0:1]).then_inc(hstd_done, 1)
                own(hstd_done)
                if i >= 2:
                    turned_tile(i - 2)
            for i in range(2):
                turned_tile(3 * TT - 2 + i)
            attention(l, 1)
            high_heads()
            sigmoids()
            high_chunks(l, chunks_of("cq"))
            for h in range(4):
                dense_out(av[:, h, :], 512)
            attention(l, 2)
            high_heads()
            sigmoids()
            high_chunks(l, chunks_of("out0") + chunks_of("out1"))
            squares(("n2", l), TT, lambda t: xres[:, t, :], lambda t: act.wait_ge(dv_free, PER_DV * (l + 1) - TT + t + 1))
            act.wait_ge(nt_out, norm_tiles["n2", l] + TT)
            for t in range(TT):
                act.activation(xnH[:, t, :], xres[:, t, :], ACT.Copy, scale=rstd[:, t:t + 1]).then_inc(xn_high, 1)
                own(xn_high)
            act.wait_ge(gd_ready, 2 * l + 1)
            act.activation(gt[:], gt[:], ACT.Exp).then_inc(gexp_done, 1)
            own(gexp_done)
            act.wait_ge(gd_ready, 2 * l + 2)
            act.activation(ex[:], m2[:], ACT.Exp).then_inc(gexp_done, 1)
            own(gexp_done)
            for q in range(NQ):
                for k in range(KT):
                    g = (NQ * l + q) * KT + k
                    act.wait_ge(perm_done, g + 1)
                    act.activation(hsT[:, k, q * QW:(q + 1) * QW], bank[4 + g % 4][:, 0:QW], ACT.Copy,
                                   scale=gcols[:, 2 * l + 1, k:k + 1]).then_inc(perm_out, 1)
                    own(perm_out)
            act.wait_ge(starts_ready, l + 1)

            def window(b, s0, down_w, arrive, gate_at, hid_at, down_at, high, silu, y, stored, store):
                wd = down_w[:].rearrange("p (k c) -> p k c", k=4)

                def high_part(f):
                    wait(act, down_at[0], down_at[1] + (0, -2, -1, 1)[f])
                    act.activation(dH[f % 3][:], wd[:, f, :], ACT.Copy).then_inc(high, 1)

                act.wait_ge(*arrive)
                for f in range(3):
                    high_part(f)
                act.wait_ge(*gate_at)
                wait(act, *hid_at)
                act.activation(gate_s[:, b], bank[b][:, 0:4 * CAP].rearrange("p (f c) -> p f c", f=4), ACT.Silu).then_inc(silu, 1)
                high_part(3)
                act.wait_ge(down_at[0], down_at[1] + 4)
                for s in stored:
                    wait(act, *s)
                for h in range(2):
                    act.activation(ysb[0:CAP, h * 512:(h + 1) * 512], bank[4 + h][0:CAP, :], ACT.Copy).then_inc(y[0], 1)
                act.wait_ge(y[0], y[1] + 2)
                act.dma_start(ybuf[bass.ds(s0, CAP), :], ysb[0:CAP, :]).then_inc(store, 16)

            def expert(i, b):
                E = NE * l + 2 * i + b
                s0 = act.value_load(sidx[0:1, bass.ds(2 * i + b, 1)] if not isinstance(i, int) else sidx[0:1, b:b + 1],
                                    min_val=0, max_val=SLOTS)
                slot = EXPERT_SLOTS[b][2]
                window(b, s0, ring[slot], (exp_loaded[slot], 16 * (NE // 2 * l + i + 1)), (gate_done, E + 1),
                       (hid_done, 2 * (E - 1)), (down_done, 4 * E), down_high, silu_done, (y_out, 2 * E),
                       [(y_stored, 16 * E)], y_stored)

            for b in range(2):
                expert(0, b)
            with act.Fori(1, NE // 2) as i:
                for b in range(2):
                    expert(i, b)
            act.wait_ge(tab_ready, l + 1)
            o = ov[l]
            act.sem_inc(o["yout"], 2)
            act.sem_inc(o["store"], 16)
            nov = act.value_load(ovn[0:1, 0:1], min_val=0, max_val=MAXOV)
            with act.If(nov > 0):
                with act.Fori(0, nov) as i:
                    s0 = act.value_load(ovs[0:1, bass.ds(i, 1)], min_val=0, max_val=SLOTS)
                    window(0, s0, ring[OVER_SLOTS[2]], (o["l2"], 16 * i + 16), (o["gate"], i + 2), (o["hid"], 2 * i + 2),
                           (o["down"], 4 * i + 4), o["high"], o["silu"], (o["yout"], 2 * i + 2),
                           [(y_stored, 16 * NE * (l + 1)), (o["store"], 16 * i + 16)], o["store"])
            if l + 1 < DEPTH:
                act.wait_ge(o["over"], 1)
                for n in range(2):
                    w, arrived = chunk_of(l + 1, n)
                    act.wait_ge(*arrived)
                    act.activation(wH[n][:], w, ACT.Copy).then_inc(first_high, 1)
            act.wait_ge(y_stored, 16 * NE * (l + 1))
            act.wait_ge(o["store"], 16 * nov + 16)
            act.sem_inc(y_all, 1)
        squares("fin", TT, lambda t: xres[:, t, :], lambda t: act.wait_ge(combined, (DEPTH - 1) * TT + t + 1))

    @block.vector
    def _(dve):
        c = {"dv": 0, "vs": 0, "rope": 0}
        made = {}

        def own(s):
            made[s.name] = made.get(s.name, 0) + 1
            dve.wait_ge(s, made[s.name])

        def v(ins):
            c["vs"] += 1
            ins.then_inc(vs, 1)
            dve.wait_ge(vs, c["vs"])

        def norm(key, nt, src, gcol, dst, ready=lambda t: None, between=lambda t: None):
            g0 = norm_tiles[key]

            def normalise(t):
                g = g0 + t
                ready(t)
                dve.wait_ge(std_done, g + 1)
                v(dve.reciprocal(rstd[:, t:t + 1], std[:, t:t + 1]))
                wait(dve, nt_done, g - 1)
                dve.tensor_scalar(xn[:, g % 2, :], src(t), rstd[:, t:t + 1], None, ALU.mult).then_inc(xn_ready, 1)
                own(xn_ready)

            def columns(t):
                g = g0 + t
                dve.wait_ge(nt_done, g + 1)
                for h in range(2):
                    ins = dve.tensor_tensor(dst[:, 4 * h:4 * h + 4, t * P:(t + 1) * P],
                                            bank[4 + 2 * (g % 2) + h][:].rearrange("p (k t) -> p k t", k=4),
                                            gcol[:, 4 * h:4 * h + 4].unsqueeze(2).broadcast_to([P, 4, P]), ALU.mult)
                ins.then_inc(nt_out, 1)
                own(nt_out)

            def split_columns(t):
                g = g0 + t
                tok = slice(t * P, (t + 1) * P)
                dve.wait_ge(nt_done, g + 1)
                for h in range(2):
                    ins = dve.tensor_tensor(scaledT[:, g % 2, 4 * h:4 * h + 4, :],
                                            bank[4 + 2 * (g % 2) + h][:].rearrange("p (k t) -> p k t", k=4),
                                            gcol[:, 4 * h:4 * h + 4].unsqueeze(2).broadcast_to([P, 4, P]), ALU.mult)
                v(ins)
                v(dve.tensor_copy(hH[:, :, tok], scaledT[:, g % 2]))
                dve.tensor_tensor(hL[:, :, tok], scaledT[:, g % 2], hH[:, :, tok].bitcast(F32),
                                  ALU.subtract).then_inc(nt_out, 1)
                own(nt_out)
            normalise(0)
            for t in range(nt):
                if t + 1 < nt:
                    normalise(t + 1)
                if dst is None:
                    split_columns(t)
                else:
                    columns(t)
                if t >= 2:
                    between(t - 2)

        def take_dense():
            n = c["dv"]
            c["dv"] += 1
            dve.wait_ge(dv_done, n + 1)
            return bank[n % 2]

        def rotate(x, cos, sin, nh, dst, free):
            xv = x.rearrange("p (h a c) -> p h a c", a=2, c=32)
            dv = dst.rearrange("p (h a c) -> p h a c", a=2, c=32)
            tv = tmp[:, 0:nh * HD].rearrange("p (h a c) -> p h a c", a=2, c=32)
            dve.tensor_tensor(dv, xv, cos, ALU.mult)
            dve.tensor_tensor(tv[:, :, 0], xv[:, :, 1], sin[:, 0].unsqueeze(1).broadcast_to([P, nh, 32]), ALU.mult)
            ins = dve.tensor_tensor(tv[:, :, 1], xv[:, :, 0], sin[:, 1].unsqueeze(1).broadcast_to([P, nh, 32]), ALU.mult)
            if free:
                ins.then_inc(dv_free, 1)
                own(dv_free)
            else:
                v(ins)
            return dve.tensor_tensor(dst, dst, tmp[:, 0:nh * HD], ALU.add)

        dve.memset(ones[:], 1.0).then_inc(const_made, 1)
        own(const_made)
        dve.memset(eps[:], EPS).then_inc(const_made, 1)
        own(const_made)
        dve.wait_ge(mem_in, 16)
        dve.wait_ge(mem_gain_in, 16)
        norm("mem", 2, lambda t: memx[:, t, :], gcols[:, 2 * DEPTH, :], hT)
        dve.wait_ge(consts_in, all_consts)
        for l in range(DEPTH):
            lv = lamv[:, 4 * l:4 * l + 4, :].rearrange("p (a b) c -> p a b c", b=2)
            v(dve.tensor_tensor(lv[:, :, 0], lv[:, :, 0], lv[:, :, 1], ALU.mult))
            dve.tensor_reduce(lamd[:, 2 * l:2 * l + 2], lv[:, :, 0], AX.X, ALU.add).then_inc(lam_d, 1)
            own(lam_d)

        def lambdas():
            dve.wait_ge(lam_e, 1)
            for l in range(DEPTH):
                v(dve.tensor_tensor(lam[:, l:l + 1], lamd[:, 2 * l:2 * l + 1], lamd[:, 2 * l + 1:2 * l + 2], ALU.subtract))
                v(dve.tensor_tensor(lam[:, l:l + 1], lam[:, l:l + 1], laminit[:, l, 0:1], ALU.add))
                v(dve.tensor_tensor(subg[:, l:l + 1], subg[:, l:l + 1], laminit[:, l, 1:2], ALU.mult))

        def attention(l, br):
            cols = 512 if br < 2 else MEM
            scale = HD ** -0.5 if br < 2 else P ** -0.5
            items = [l * NI + n for n in BRANCH_ITEMS[br]]

            def maxima(n):
                for m in range(2):
                    q = 2 * (n % 2) + m
                    dve.wait_ge(s_done, 2 * n + m + 1)
                    wait(dve, exp_done, 2 * n + m - 3)
                    v(dve.tensor_reduce(mx[:, q:q + 1], bank[m][:, 0:cols], AX.X, ALU.max))
                    dve.tensor_scalar(nbias[:, q:q + 1], mx[:, q:q + 1], -scale, None, ALU.mult).then_inc(bias_ready, 1)
                    own(bias_ready)

            def normalise(n):
                q = 2 * (n % 2)
                dve.wait_ge(exp_done, 2 * n + 2)
                v(dve.reciprocal(rsum[:, q:q + 2], rowsum[:, q:q + 2]))
                p0, p1 = prob[:, q, 0:cols], prob[:, q + 1, 0:cols]
                if br == 0:
                    v(dve.tensor_scalar(p1, p1, rsum[:, q + 1:q + 2], lam[:, l:l + 1], ALU.mult, ALU.mult))
                    ins = dve.scalar_tensor_tensor(out=p0, in0=p0, scalar=rsum[:, q:q + 1], in1=p1, op0=ALU.mult, op1=ALU.subtract)
                else:
                    dve.tensor_scalar(p0, p0, rsum[:, q:q + 1], None, ALU.mult)
                    ins = dve.tensor_scalar(p1, p1, rsum[:, q + 1:q + 2], None, ALU.mult)
                ins.then_inc(p_ready, 1)
                own(p_ready)

            for n in items:
                maxima(n)
                normalise(n)

        def combine(l, t):
            for j in range(2):
                dve.wait_ge(gathered[2 * t + j], 16 * (l + 1))
                ins = dve.scalar_tensor_tensor(out=xres[:, t, :], in0=gath[:, 2 * t + j, :], scalar=wts[:, j, t:t + 1],
                                               in1=xres[:, t, :], op0=ALU.mult, op1=ALU.add)
                if j == 0:
                    v(ins)
            ins.then_inc(combined, 1)
            own(combined)

        def combine_ahead(l, t):
            for u in ([0, 1], [2], [3], [])[t]:
                combine(l, u)

        def low_heads(l, br):
            for k in range(4):
                dve.wait_ge(o_high, 12 * l + 4 * br + k + 1)
                dve.tensor_tensor(oL[:, k, :], oT[:, k, :], oH[k][:].bitcast(F32), ALU.subtract).then_inc(o_split, 1)
                own(o_split)

        def gates(l, br):
            for f in range(KT):
                b = take_dense()
                dve.wait_ge(gate_ready, 24 * l + 8 * br + f + 1)
                to = mergedT[:, f, :] if br == 0 else tmp[:]
                mf = mergedT[:, f, :]
                dve.tensor_tensor(to, gates_s[:, f, :], b[:], ALU.mult).then_inc(dv_free, 1)
                own(dv_free)
                if br:
                    v(dve.tensor_tensor(mf, mf, tmp[:], ALU.add))
                if br == 2:
                    v(dve.tensor_copy(hH[:, f, :], mf))
                    dve.tensor_tensor(hL[:, f, :], mf, hH[:, f, :].bitcast(F32), ALU.subtract).then_inc(merged, 1)
                    own(merged)

        for l in range(DEPTH):
            def rope_a(i):
                t = i % TT
                b = take_dense()
                r = c["rope"]
                c["rope"] += 1
                wait(dve, tr_done, r - 1)
                rotate(b[:, 0:CW], cosA[:, t].unsqueeze(1).unsqueeze(1).broadcast_to([P, 4, 2, 32]), sinA[:, t], 4,
                       roped[:, r % 2, :], True).then_inc(rope_ready, 1)
                own(rope_ready)
            norm(("n1", l), TT, lambda t: xres[:, t, :], gcols[:, 2 * l, :], None,
                 ready=(lambda t: combine_ahead(l - 1, t)) if l else lambda t: None, between=rope_a)
            for i in range(2, 4 * TT):
                rope_a(i)
            if l == 0:
                lambdas()
            attention(l, 0)
            dve.wait_ge(sq_root, l + 1)
            v(dve.reciprocal(hsq[:], hsq[:]))
            for h in range(4):
                oh = o_tok[:, TT * h:TT * h + TT, :]
                dve.tensor_tensor(oh, oh, hsq[:, TT * h:TT * h + TT].unsqueeze(2).broadcast_to([P, TT, P]),
                                  ALU.mult).then_inc(sub_scaled, 1)
                own(sub_scaled)
            low_heads(l, 0)
            gates(l, 0)
            for m in range(2):
                for t in range(TT):
                    g2 = qg[:, l, m].rearrange("p (a c) -> p a c", a=2)
                    dve.tensor_tensor(foldc[:, m, t], g2, cosB[:, t].unsqueeze(1).broadcast_to([P, 2, 32]), ALU.mult)
                    dve.tensor_tensor(folds[:, m, t, 0], g2[:, 1], sinB[:, t, 0], ALU.mult)
                    last = dve.tensor_tensor(folds[:, m, t, 1], g2[:, 0], sinB[:, t, 1], ALU.mult)
            v(last)

            def head_sums(i):
                nh = 4 if i < 2 * TT else 2
                dve.wait_ge(raw_ready, 3 * TT * l + i + 1)
                dve.tensor_reduce(hss[:, i % 2, 0:nh], tmp[:, CW:CW + nh * HD].rearrange("p (h c) -> p h c", c=HD),
                                  AX.X, ALU.add).then_inc(hss_done, 1)
                own(hss_done)

            head_sums(0)
            for i in range(3 * TT):
                if i + 1 < 3 * TT:
                    head_sums(i + 1)
                t, m = i % TT, i // (2 * TT)
                nh = 4 if m == 0 else 2
                w = nh * HD
                r = c["rope"]
                c["rope"] += 1
                dve.wait_ge(hstd_done, 3 * TT * l + i + 1)
                v(dve.reciprocal(hr[:, 0:nh], hstd[:, i % 2, 0:nh]))
                x = raw[:, i % 2, 0:w]
                rv = x.rearrange("p (h c) -> p h c", c=HD)
                v(dve.tensor_tensor(rv, rv, hr[:, 0:nh].unsqueeze(2).broadcast_to([P, nh, HD]), ALU.mult))
                wait(dve, tr_done, r - 1)
                fc = foldc[:, m, t].unsqueeze(1).broadcast_to([P, nh, 2, 32])
                if m == 0:
                    rotate(x, fc, folds[:, m, t], nh, roped[:, r % 2, :], False).then_inc(rope_ready, 1)
                    own(rope_ready)
                else:
                    y = raw[:, i % 2, w:2 * w]
                    v(rotate(x, fc, folds[:, m, t], nh, y, False))
                    dve.tensor_copy(roped[:, r % 2, :].rearrange("p (h a c) -> p h a c", a=2, c=HD),
                                    y.rearrange("p (h c) -> p h c", c=HD).unsqueeze(2).broadcast_to(
                                        [P, 2, 2, HD])).then_inc(rope_ready, 1)
                    own(rope_ready)
            attention(l, 1)
            low_heads(l, 1)
            gates(l, 1)
            attention(l, 2)
            low_heads(l, 2)
            gates(l, 2)
            def add_out(n, t):
                b = take_dense()
                xs = xres[:, t, n * CW:(n + 1) * CW]
                dve.tensor_tensor(xs, xs, b[:, 0:CW], ALU.add).then_inc(dv_free, 1)
                own(dv_free)
            for n in range(3):
                for t in range(TT):
                    add_out(n, t)
            for t in range(2):
                add_out(3, t)
            norm(("n2", l), TT, lambda t: xres[:, t, :], gcols[:, 2 * l + 1, :], hT,
                 ready=lambda t: t in (1, 2) and add_out(3, t + 1))
            dve.memset(hsT[:, :, SLOTS:], 0.0).then_inc(pad_done, 1)
            own(pad_done)

            dve.wait_ge(lg_done, l + 1)
            v(dve.tensor_tensor(lg[:], bank[0][:, 0:TT * 36].rearrange("p (t c) -> p t c", t=TT),
                                router_b[:, l, :].unsqueeze(1).broadcast_to([P, TT, 36]), ALU.add))

            def argmax(vals, width, m, sel, cnd):
                v(dve.tensor_reduce(m, vals, AX.X, ALU.max))
                v(dve.tensor_tensor(cnd, vals, m.unsqueeze(2).broadcast_to([P, TT, width]), ALU.is_equal))
                v(dve.tensor_tensor(cnd, cnd, first[:, 0:width].unsqueeze(1).broadcast_to([P, TT, width]), ALU.mult))
                v(dve.tensor_reduce(ex[:], cnd, AX.X, ALU.max))
                v(dve.tensor_tensor(sel, cnd, ex[:].unsqueeze(2).broadcast_to([P, TT, width]), ALU.is_equal))

            lgg = lg[:, :, 0:NG]
            argmax(lgg, NG, m1[:], gsel[:], gt[:])
            dve.tensor_tensor(gt[:], lgg, m1[:].unsqueeze(2).broadcast_to([P, TT, NG]), ALU.subtract).then_inc(gd_ready, 1)
            own(gd_ready)
            v(dve.tensor_scalar(gsel[:], gsel[:], 1.0, 1e30, ALU.subtract, ALU.mult))
            v(dve.tensor_tensor(em[:].rearrange("p t (g e) -> p t g e", g=NG),
                                lg[:, :, NG:].rearrange("p t (g e) -> p t g e", g=NG),
                                gsel[:].unsqueeze(3).broadcast_to([P, TT, NG, EPG]), ALU.add))
            argmax(em[:], NE, m1[:], sel1[:], cand[:])
            v(dve.tensor_scalar(cand[:], sel1[:], -3e38, None, ALU.mult))
            v(dve.tensor_tensor(em[:], em[:], cand[:], ALU.add))
            argmax(em[:], NE, m2[:], sel2[:], cand[:])
            dve.tensor_tensor(cand[:], sel1[:], sel2[:], ALU.add).then_inc(sel_ready, 1)
            own(sel_ready)
            dve.wait_ge(gexp_done, 2 * l + 1)
            dve.tensor_tensor(m2[:], m2[:], m1[:], ALU.subtract).then_inc(gd_ready, 1)
            own(gd_ready)
            v(dve.tensor_reduce(gp[:], gt[:], AX.X, ALU.add))
            v(dve.reciprocal(gp[:], gp[:]))
            for t in range(TT):
                dve.wait_ge(xn_high, TT * l + t + 1)
                ins = dve.scalar_tensor_tensor(out=xnL[:, t, :], in0=xres[:, t, :], scalar=rstd[:, t:t + 1],
                                               in1=xnH[:, t, :].bitcast(F32), op0=ALU.mult, op1=ALU.subtract)
            ins.then_inc(split_ready, 1)
            own(split_ready)
            dve.wait_ge(gexp_done, 2 * l + 2)
            dve.wait_ge(rank_done, l + 1)
            v(dve.tensor_copy(cnt[:], bank[1][:, TT * NE:(TT + 1) * NE]))
            v(dve.tensor_tensor_scan(incl[:], ones[:, 0:NE], cnt[:], 0.0, ALU.mult, ALU.add))
            v(dve.tensor_tensor(start[:], incl[:], cnt[:], ALU.subtract))
            v(dve.tensor_tensor(em[:], bank[1][:, 0:TT * NE].rearrange("p (t e) -> p t e", t=TT),
                                start[:].unsqueeze(1).broadcast_to([P, TT, NE]), ALU.add))
            for j, s in enumerate((sel1, sel2)):
                v(dve.tensor_tensor(s[:], s[:], em[:], ALU.mult))
                v(dve.tensor_reduce(destf[:, j], s[:], AX.X, ALU.add))
            dve.tensor_copy(desti[:], destf[:])
            v(dve.tensor_copy(sidx[:], start[0:1]))
            dve.sem_inc(starts_ready, 1)
            for q in range(NQ):
                v(dve.tensor_scalar(desth[:], destf[:], float(-q * QW), None, ALU.add))
                if q >= 2:
                    dve.wait_ge(perm_done, (NQ * l + q - 1) * KT)
                for t in range(TT):
                    ins = dve.tensor_scalar(pick[:, q % 2, t, :], iota[:], desth[:, 0, t:t + 1], None, ALU.is_equal)
                v(ins)
                for t in range(TT):
                    ins = dve.scalar_tensor_tensor(out=pick[:, q % 2, t, :], in0=iota[:], scalar=desth[:, 1, t:t + 1],
                                                   in1=pick[:, q % 2, t, :].bitcast(F32),
                                                   op0=ALU.is_equal, op1=ALU.add)
                ins.then_inc(pick_ready, 1)
                own(pick_ready)
                if q == 1:
                    v(dve.tensor_scalar(m1[:], ex[:], 1.0, None, ALU.add))
                    v(dve.reciprocal(m1[:], m1[:]))
                    v(dve.tensor_tensor(wts[:, 0], gp[:], m1[:], ALU.mult))
                    v(dve.tensor_tensor(wts[:, 1], wts[:, 0], ex[:], ALU.mult))
            dve.wait_ge(perm_done, NQ * KT * (l + 1))
            c0, s0, e0 = cnt[0:1], start[0:1], incl[0:1]
            n_ov, cum, exc, t_ = (ovc[:, q] for q in range(4))
            v(dve.tensor_scalar(n_ov, c0, float(CAP), None, ALU.is_gt))
            for q in range(2, SEQ // CAP + 1):
                v(dve.tensor_scalar(t_, c0, float(CAP * q), None, ALU.is_gt))
                v(dve.tensor_tensor(n_ov, n_ov, t_, ALU.add))
            v(dve.tensor_tensor_scan(cum, ones[0:1, 0:NE], n_ov, 0.0, ALU.mult, ALU.add))
            v(dve.tensor_tensor(exc, cum, n_ov, ALU.subtract))
            full = [1, MAXOV, NE]
            T0, T1, T2 = (ovt[:, q] for q in range(3))
            sl = slotno[:].unsqueeze(2).broadcast_to(full)

            def per_e(x):
                return x.unsqueeze(1).broadcast_to(full)
            v(dve.tensor_tensor(T0, per_e(cum), sl, ALU.is_le))
            v(dve.tensor_reduce(ovr[:, 0], T0, AX.X, ALU.add))
            v(dve.tensor_tensor(T1, per_e(exc), sl, ALU.is_le))
            v(dve.tensor_tensor(T1, T1, T0, ALU.subtract))
            for q, x in ((1, s0), (2, e0), (3, exc)):
                v(dve.tensor_tensor(T2, T1, per_e(x), ALU.mult))
                v(dve.tensor_reduce(ovr[:, q], T2, AX.X, ALU.add))
            v(dve.tensor_tensor(ovr[:, 4], slotno[:], ovr[:, 3], ALU.subtract))
            v(dve.tensor_scalar(ovr[:, 4], ovr[:, 4], 1.0, float(CAP), ALU.add, ALU.mult))
            v(dve.tensor_tensor(ovr[:, 4], ovr[:, 4], ovr[:, 1], ALU.add))
            v(dve.tensor_scalar(ovr[:, 2], ovr[:, 2], float(-CAP), None, ALU.add))
            v(dve.tensor_tensor(ovr[:, 4], ovr[:, 4], ovr[:, 2], ALU.min))
            v(dve.tensor_scalar(ovr[:, 4], ovr[:, 4], 0.0, None, ALU.max))
            v(dve.tensor_scalar(ovr[:, 0], ovr[:, 0], float(NE - 1), None, ALU.min))
            dve.tensor_copy(ovs[:], ovr[:, 4])
            dve.tensor_copy(ove[:], ovr[:, 0])
            v(dve.tensor_copy(ovn[:], cum[:, NE - 1:NE]))
            dve.sem_inc(tab_ready, 1)

            def window(b, down_w, high_at, split, down_at, silu_at, up_at, hid_sem, steps, steps_at):
                wd = down_w[:].rearrange("p (k c) -> p k c", k=4)

                def low_part(f):
                    dve.wait_ge(high_at[0], high_at[1] + f + 1)
                    wait(dve, down_at[0], down_at[1] + (0, -2, -1, 1)[f])
                    dve.tensor_tensor(dL[f % 3][:], wd[:, f, :], dH[f % 3][:].bitcast(F32), ALU.subtract).then_inc(split, 1)

                for f in range(3):
                    low_part(f)
                dve.wait_ge(*silu_at)
                for h in range(2):
                    fs = slice(2 * h, 2 * h + 2)
                    dve.wait_ge(up_at[0], up_at[1] + h + 1)
                    dve.tensor_tensor(gate_s[:, b, fs, :], gate_s[:, b, fs, :],
                                      bank[2 + 4 * b + h][:, 0:2 * CAP].rearrange("p (f c) -> p f c", f=2),
                                      ALU.mult).then_inc(steps, 1)
                    dve.wait_ge(steps, steps_at + 2 * h + 1)
                    dve.tensor_copy(hidH[:, b, fs, :], gate_s[:, b, fs, :]).then_inc(steps, 1)
                    dve.wait_ge(steps, steps_at + 2 * h + 2)
                    dve.tensor_tensor(hidL[:, b, fs, :], gate_s[:, b, fs, :], hidH[:, b, fs, :].bitcast(F32),
                                      ALU.subtract).then_inc(hid_sem, 1)
                low_part(3)

            def expert(i, b):
                E = NE * l + 2 * i + b
                window(b, ring[EXPERT_SLOTS[b][2]], (down_high, 4 * E), down_split, (down_done, 4 * E),
                       (silu_done, E + 1), (up_done, 2 * E), hid_done, hid_steps, 4 * E)
            for b in range(2):
                expert(0, b)
            with dve.Fori(1, NE // 2) as i:
                for b in range(2):
                    expert(i, b)
            o = ov[l]
            dve.sem_inc(o["hid"], 2)
            nov = dve.value_load(ovn[0:1, 0:1], min_val=0, max_val=MAXOV)
            with dve.If(nov > 0):
                with dve.Fori(0, nov) as i:
                    window(0, ring[OVER_SLOTS[2]], (o["high"], 4 * i), o["split"], (o["down"], 4 * i + 4),
                           (o["silu"], i + 1), (o["up"], 2 * i + 2), o["hid"], o["steps"], 4 * i)
            dve.nop()
            if l + 1 < DEPTH:
                for n in range(2):
                    w, _ = chunk_of(l + 1, n)
                    dve.wait_ge(first_high, 2 * l + n + 1)
                    dve.tensor_tensor(wL[n][:], w, wH[n][:].bitcast(F32), ALU.subtract).then_inc(first_split, 1)

        for t in range(TT):
            combine_ahead(DEPTH - 1, t)
            if t == 0:
                dve.wait_ge(fing_in, 16)
            dve.wait_ge(std_done, norm_tiles["fin"] + t + 1)
            v(dve.reciprocal(rstd[:, t:t + 1], std[:, t:t + 1]))
            wait(dve, out_sem, 16 * (t - 1))
            dve.scalar_tensor_tensor(out=yfin[:, t % 2, :], in0=xres[:, t, :], scalar=rstd[:, t:t + 1], in1=fing[:],
                                     op0=ALU.mult, op1=ALU.mult).then_inc(fin, 1)
            own(fin)


_INS = ("x", "mem", "mem_norm_g", "w_mem_kv", "norm1_g", "w_in", "lam_q1", "lam_k1", "lam_q2", "lam_k2",
        "subln_g", "q_norm_g", "k_norm_g", "w_up_a", "w_up_b", "w_up_c", "w_out", "norm2_g",
        "w_router_group", "b_router_group", "w_router_expert", "b_router_expert",
        "w_exp_gate", "w_exp_up", "w_exp_down", "final_norm_g")


def _constants():
    pos = np.arange(SEQ, dtype=np.float32)
    inv = (10000.0 ** (-np.arange(0, HD, 2, dtype=np.float32) / HD)).astype(np.float32)
    ang_a = pos[:, None] * inv
    inv = (10000.0 ** (-np.arange(0, HD // 2, 2, dtype=np.float32) / (HD // 2))).astype(np.float32)
    ang_b = np.concatenate([(pos // GRID_W)[:, None] * inv, (pos % GRID_W)[:, None] * inv], 1)
    made = {}
    for n, ang in (("a", ang_a), ("b", ang_b)):
        ang = ang.astype(np.float32).astype(np.float64)
        made["cos_" + n] = np.cos(ang)
        made["sin_" + n] = np.concatenate([-np.sin(ang), np.sin(ang)], 1)
    li = [0.8 - 0.6 * math.exp(-0.3 * l) for l in range(DEPTH)]
    made["lam_init"] = np.array([[x for l in li for x in (l, 1.0 - l)]])
    made["ident"] = np.eye(P)
    made["upper"] = np.triu(np.ones((P, P)), 1)
    made["iota"] = np.arange(QW)[None]
    made["first"] = (NE - np.arange(NE))[None]
    return {k: np.ascontiguousarray(v, np.float32) for k, v in made.items()}


def kernel(**inputs):
    import concourse.bacc as bacc
    from concourse.bass_utils import run_bass_kernel_spmd

    nc = bacc.Bacc("TRN2", target_bir_lowering=False, num_devices=1)
    given = {n: np.ascontiguousarray(inputs[n]) for n in _INS} | _constants()
    arrays, aps = {}, {}
    for name, arr in given.items():
        arrays[f"in_{name}"] = arr
        aps[name] = nc.dram_tensor(f"in_{name}", arr.shape, mybir.dt.from_np(arr.dtype), kind="ExternalInput").ap()
    result = nc.dram_tensor("result", (1, SEQ, D), F32, kind="ExternalOutput").ap()
    build(nc, aps, result)
    r = run_bass_kernel_spmd(nc, [arrays], core_ids=[0])
    return r.results[0]["result"]
```
